# Optimizing a Trainium2 kernel written in Bass

```python
import jax
import jax.numpy as jnp
from jax import lax
import numpy as np

D_MODEL = 1024
BATCH = 1
SEQ = 256
DEPTH = 2

CTX_LEN = 256
GRID_W = 64
EPS = 1e-6

MLA_HEADS = 4
MLA_Q_RANK = 256
MLA_KV_RANK = 128
MLA_NOPE = 64
MLA_ROPE = 32
MLA_V = 64
ROPE_BASE = 10000.0
Q_BLOCK = 128

NA_HEADS = 4
NA_DIM = 64
NA_KR = 8
NA_KC = 16

ML_HEADS = 4
ML_QK = 64
ML_V = 128
ML_CHUNK = 128

N_EXPERTS = 16
D_EXPERT = 1024
EC_FACTOR = 2

MLA_W = MLA_HEADS * MLA_V
NA_W = NA_HEADS * NA_DIM
ML_W = ML_HEADS * ML_V

IN_SIZES = (MLA_Q_RANK, MLA_KV_RANK, MLA_ROPE,
            NA_W, NA_W, NA_W,
            ML_HEADS * ML_QK, ML_HEADS * ML_QK, ML_W, ML_W, 4 * ML_HEADS,
            3 * D_MODEL)
D_IN = sum(IN_SIZES)

kernel_name = 'hybrid_mla_natten_mlstm_ecmoe_diffusion'

def rmsnorm(x, g):
    xf = x.astype(jnp.float32)
    xf = xf * lax.rsqrt(jnp.mean(jnp.square(xf), axis=-1, keepdims=True) + EPS)
    return (xf * g.astype(jnp.float32)).astype(x.dtype)

def split_in(z):
    offs = np.cumsum(IN_SIZES)[:-1].tolist()
    return jnp.split(z, offs, axis=-1)

def rope_2d(n):
    t = jnp.arange(n)
    pos = jnp.stack([t // GRID_W, t % GRID_W], axis=-1).astype(jnp.float32)
    nf = MLA_ROPE // 4
    inv = ROPE_BASE ** (-jnp.arange(nf, dtype=jnp.float32) / nf)
    ang = pos[..., None] * inv
    return jnp.cos(ang), jnp.sin(ang)

def apply_rope_2d(x, cos, sin):
    xs = x.reshape(x.shape[:-1] + (2, 2, MLA_ROPE // 4))
    x1, x2 = xs[..., 0, :], xs[..., 1, :]
    cos, sin = cos.astype(x.dtype), sin.astype(x.dtype)
    out = jnp.stack([x1 * cos - x2 * sin, x1 * sin + x2 * cos], axis=-2)
    return out.reshape(x.shape)

def mla_queries(cq, g_q, w_uq, cos, sin):
    q = jnp.einsum('bnr,rhe->bnhe', rmsnorm(cq, g_q), w_uq)
    q_nope, q_rope = q[..., :MLA_NOPE], q[..., MLA_NOPE:]
    if cos is not None:
        q_rope = apply_rope_2d(q_rope, cos[:, None], sin[:, None])
    return jnp.concatenate([q_nope, q_rope], axis=-1)

def mla_keys_values(ckv, kr, g_kv, w_ukv, cos, sin):
    kv = jnp.einsum('bnr,rhe->bnhe', rmsnorm(ckv, g_kv), w_ukv)
    k_nope, v = kv[..., :MLA_NOPE], kv[..., MLA_NOPE:]
    if cos is not None:
        kr = apply_rope_2d(kr, cos, sin)
    k_rope = jnp.broadcast_to(kr[:, :, None, :], k_nope.shape[:3] + (MLA_ROPE,))
    return jnp.concatenate([k_nope, k_rope], axis=-1), v

def block_attention(q, k, v):
    B, n, H, E = q.shape
    scale = E ** -0.5
    qb = jnp.moveaxis(q.reshape(B, n // Q_BLOCK, Q_BLOCK, H, E), 1, 0)

    def one_block(q_blk):
        s = jnp.einsum('bqhe,bkhe->bhqk', q_blk, k).astype(jnp.float32) * scale
        p = jax.nn.softmax(s, axis=-1).astype(v.dtype)
        return jnp.einsum('bhqk,bkhv->bqhv', p, v)

    o = lax.map(one_block, qb)
    return jnp.moveaxis(o, 0, 1).reshape(B, n, H, v.shape[-1])

def neighbourhood_attention(q, k, v, k_ctx, v_ctx, rpb):
    B, n, H, d = q.shape
    rows = n // GRID_W
    kr = min(NA_KR, rows)
    scale = d ** -0.5
    grid = lambda t: t.reshape(B, rows, GRID_W, H, d)
    qg, kg, vg = grid(q), grid(k), grid(v)
    cols = jnp.arange(GRID_W)
    col_idx = jnp.clip(cols - NA_KC // 2, 0, GRID_W - NA_KC)[:, None] + jnp.arange(NA_KC)[None, :]
    dc = col_idx - cols[:, None]
    n_loc = kr * NA_KC

    def one_row(r):
        rs = jnp.clip(r - kr // 2, 0, rows - kr)
        q_r = lax.dynamic_index_in_dim(qg, r, axis=1, keepdims=False)
        k_win = lax.dynamic_slice_in_dim(kg, rs, kr, axis=1)[:, :, col_idx]
        v_win = lax.dynamic_slice_in_dim(vg, rs, kr, axis=1)[:, :, col_idx]
        dr = rs + jnp.arange(kr) - r
        bias = rpb[:, dr[:, None, None] + NA_KR - 1, dc[None] + NA_KC - 1]
        bias = jnp.transpose(bias, (0, 2, 1, 3)).reshape(H, GRID_W, n_loc).astype(jnp.float32)
        s_loc = jnp.einsum('bwhd,biwjhd->bhwij', q_r, k_win).reshape(B, H, GRID_W, n_loc)
        s_ctx = jnp.einsum('bwhd,bchd->bhwc', q_r, k_ctx)
        s = jnp.concatenate([s_loc.astype(jnp.float32) * scale + bias,
                             s_ctx.astype(jnp.float32) * scale], axis=-1)
        p = jax.nn.softmax(s, axis=-1).astype(v.dtype)
        p_loc = p[..., :n_loc].reshape(B, H, GRID_W, kr, NA_KC)
        return (jnp.einsum('bhwij,biwjhd->bwhd', p_loc, v_win)
                + jnp.einsum('bhwc,bchd->bwhd', p[..., n_loc:], v_ctx))

    o = lax.map(one_row, jnp.arange(rows))
    return jnp.moveaxis(o, 0, 1).reshape(B, n, H, d)

def mlstm_scan(q, k, v, i_pre, f_pre, state, with_out):
    B, H, n, _ = q.shape
    nc = n // ML_CHUNK
    chunks = lambda t: jnp.moveaxis(t.reshape((B, H, nc, ML_CHUNK) + t.shape[3:]), 2, 0)
    tri = jnp.tril(jnp.ones((ML_CHUNK, ML_CHUNK), dtype=bool))

    def step(carry, inp):
        C, nv, m = carry
        qc, kc, vc, ic, fc = inp
        b = jnp.cumsum(jax.nn.log_sigmoid(fc), axis=-1)
        bL = b[..., -1]
        w_log = bL[..., None] - b + ic
        m_new = jnp.maximum(bL + m, jnp.max(w_log, axis=-1))
        decay = jnp.exp(bL + m - m_new)
        w = jnp.exp(w_log - m_new[..., None])
        C_new = decay[..., None, None] * C + jnp.einsum('bhs,bhsv,bhsk->bhvk', w, vc, kc)
        n_new = decay[..., None] * nv + jnp.einsum('bhs,bhsk->bhk', w, kc)
        new = (C_new, n_new, m_new)
        if not with_out:
            return new, None
        d_log = jnp.where(tri, b[..., :, None] - b[..., None, :] + ic[..., None, :], -jnp.inf)
        inter = b + m[..., None]
        m_t = jnp.maximum(inter, jnp.max(d_log, axis=-1))
        a = jnp.exp(inter - m_t)
        s = jnp.einsum('bhtk,bhsk->bhts', qc, kc) * jnp.exp(d_log - m_t[..., None])
        num = a[..., None] * jnp.einsum('bhvk,bhtk->bhtv', C, qc) + jnp.einsum('bhts,bhsv->bhtv', s, vc)
        den = a * jnp.einsum('bhk,bhtk->bht', nv, qc) + jnp.sum(s, axis=-1)
        h = num / jnp.maximum(jnp.abs(den), jnp.exp(-m_t))[..., None]
        return new, h

    state, hs = lax.scan(step, state, (chunks(q), chunks(k), chunks(v), chunks(i_pre), chunks(f_pre)))
    if not with_out:
        return state, None
    return state, jnp.moveaxis(hs, 0, 2).reshape(B, H, n, ML_V)

def mlstm_bidir(mq, mk, mv, mg, mq_c, mk_c, mv_c, mg_c, b_ml, ctx_out):
    def prep(q, k, v, g):
        B, n, _ = q.shape
        th = lambda t, dd: jnp.transpose(t.reshape(B, n, ML_HEADS, dd), (0, 2, 1, 3)).astype(jnp.float32)
        gates = jnp.transpose((g + b_ml).astype(jnp.float32).reshape(B, n, 4, ML_HEADS), (2, 0, 3, 1))
        return th(q, ML_QK), th(k, ML_QK) * (ML_QK ** -0.5), th(v, ML_V), gates

    q, k, v, g = prep(mq, mk, mv, mg)
    qc, kc, vc, gc = prep(mq_c, mk_c, mv_c, mg_c)
    B = q.shape[0]
    zero = (jnp.zeros((B, ML_HEADS, ML_V, ML_QK), jnp.float32),
            jnp.zeros((B, ML_HEADS, ML_QK), jnp.float32),
            jnp.zeros((B, ML_HEADS), jnp.float32))
    fl = lambda t: jnp.flip(t, axis=2)
    s_f, hc_f = mlstm_scan(qc, kc, vc, gc[0], gc[1], zero, ctx_out)
    _, h_f = mlstm_scan(q, k, v, g[0], g[1], s_f, True)
    s_b, hc_b = mlstm_scan(fl(qc), fl(kc), fl(vc), fl(gc[2]), fl(gc[3]), zero, ctx_out)
    _, h_b = mlstm_scan(fl(q), fl(k), fl(v), fl(g[2]), fl(g[3]), s_b, True)
    h = jnp.transpose(h_f + fl(h_b), (0, 2, 1, 3))
    if not ctx_out:
        return h, None
    return h, jnp.transpose(hc_f + fl(hc_b), (0, 2, 1, 3))

def mlstm_output(h, o, g_ml):
    hn = rmsnorm(h, g_ml.reshape(ML_HEADS, ML_V)).reshape(o.shape[:2] + (ML_W,))
    return hn.astype(o.dtype) * jax.nn.sigmoid(o)

def merge(a, b, m, gates, w_br_mla, w_br_na, w_br_ml, w_out):
    g_a, g_b, g_m = jnp.split(jax.nn.sigmoid(gates), 3, axis=-1)
    flat = lambda t: t.reshape(t.shape[:2] + (-1,))
    y = g_a * (flat(a) @ w_br_mla) + g_b * (flat(b) @ w_br_na) + g_m * (m @ w_br_ml)
    return y @ w_out

def token_mixers(h, hc, w_in, g_q, g_kv, w_uq, w_ukv, rpb, b_ml, g_ml,
                 w_br_mla, w_br_na, w_br_ml, w_out, ctx_out):
    n = h.shape[1]
    (cq, ckv, kr, nq, nk, nv, mq, mk, mv, mo, mg, bg) = split_in(h @ w_in)
    (cq_c, ckv_c, kr_c, nq_c, nk_c, nv_c, mq_c, mk_c, mv_c, mo_c, mg_c, bg_c) = split_in(hc @ w_in)
    cos, sin = rope_2d(n)
    k_c, v_c = mla_keys_values(ckv_c, kr_c, g_kv, w_ukv, None, None)
    k_l, v_l = mla_keys_values(ckv, kr, g_kv, w_ukv, cos, sin)
    a = block_attention(mla_queries(cq, g_q, w_uq, cos, sin),
                        jnp.concatenate([k_c, k_l], axis=1), jnp.concatenate([v_c, v_l], axis=1))
    nh = lambda t: t.reshape(t.shape[:2] + (NA_HEADS, NA_DIM))
    b = neighbourhood_attention(nh(nq), nh(nk), nh(nv), nh(nk_c), nh(nv_c), rpb)
    m, m_c = mlstm_bidir(mq, mk, mv, mg, mq_c, mk_c, mv_c, mg_c, b_ml, ctx_out)
    y = merge(a, b, mlstm_output(m, mo, g_ml), bg, w_br_mla, w_br_na, w_br_ml, w_out)
    if not ctx_out:
        return y, None
    a_c = block_attention(mla_queries(cq_c, g_q, w_uq, None, None), k_c, v_c)
    b_c = block_attention(nh(nq_c), nh(nk_c), nh(nv_c))
    y_c = merge(a_c, b_c, mlstm_output(m_c, mo_c, g_ml), bg_c, w_br_mla, w_br_na, w_br_ml, w_out)
    return y, y_c

def expert_choice_ffn(h, w_router, w1, w3, w2):
    B, n, _ = h.shape
    cap = EC_FACTOR * n // N_EXPERTS
    aff = jax.nn.softmax((h @ w_router).astype(jnp.float32), axis=-1)
    g, idx = lax.top_k(jnp.swapaxes(aff, 1, 2), cap)
    bidx = jnp.arange(B)[:, None, None]
    xs = h[bidx, idx]
    hid = jax.nn.silu(jnp.einsum('becd,edf->becf', xs, w1)) * jnp.einsum('becd,edf->becf', xs, w3)
    y = jnp.einsum('becf,efd->becd', hid, w2) * g[..., None].astype(h.dtype)
    return jnp.zeros_like(h).at[bidx, idx].add(y)

def setup_inputs(seed: int = 0) -> dict:
    key = jax.random.key(seed)
    ks = iter(jax.random.split(key, 32))
    nrm = lambda shape, scale: jax.random.normal(next(ks), shape, jnp.float32) * scale
    L, D = DEPTH, D_MODEL
    f_bias = jnp.linspace(3.0, 6.0, ML_HEADS)
    gate_base = jnp.concatenate([jnp.zeros(ML_HEADS), f_bias, jnp.zeros(ML_HEADS), f_bias])
    return {
        'x': nrm((BATCH, SEQ, D), 1.0),
        'c': nrm((BATCH, D), 1.0),
        'ctx': nrm((BATCH, CTX_LEN, D), 1.0),
        'c_ctx': nrm((D,), 1.0),
        'w_mod': nrm((L, D, 6 * D), 0.5 * D ** -0.5),
        'b_mod': nrm((L, 6 * D), 0.02),
        'g_pre1': 1.0 + nrm((L, D), 0.02),
        'g_post1': 1.0 + nrm((L, D), 0.02),
        'g_pre2': 1.0 + nrm((L, D), 0.02),
        'g_post2': 1.0 + nrm((L, D), 0.02),
        'w_in': nrm((L, D, D_IN), D ** -0.5),
        'g_q': 1.0 + nrm((L, MLA_Q_RANK), 0.02),
        'g_kv': 1.0 + nrm((L, MLA_KV_RANK), 0.02),
        'w_uq': nrm((L, MLA_Q_RANK, MLA_HEADS, MLA_NOPE + MLA_ROPE), MLA_Q_RANK ** -0.5),
        'w_ukv': nrm((L, MLA_KV_RANK, MLA_HEADS, MLA_NOPE + MLA_V), MLA_KV_RANK ** -0.5),
        'rpb': nrm((L, NA_HEADS, 2 * NA_KR - 1, 2 * NA_KC - 1), 0.1),
        'b_ml_gates': gate_base + nrm((L, 4 * ML_HEADS), 0.1),
        'g_ml': 1.0 + nrm((L, ML_W), 0.02),
        'w_br_mla': nrm((L, MLA_W, D), MLA_W ** -0.5),
        'w_br_na': nrm((L, NA_W, D), NA_W ** -0.5),
        'w_br_ml': nrm((L, ML_W, D), ML_W ** -0.5),
        'w_out': nrm((L, D, D), D ** -0.5),
        'w_router': nrm((L, D, N_EXPERTS), D ** -0.5),
        'w_e1': nrm((L, N_EXPERTS, D, D_EXPERT), D ** -0.5),
        'w_e3': nrm((L, N_EXPERTS, D, D_EXPERT), D ** -0.5),
        'w_e2': nrm((L, N_EXPERTS, D_EXPERT, D), D_EXPERT ** -0.5),
    }

def reference(x, c, ctx, c_ctx, w_mod, b_mod, g_pre1, g_post1, g_pre2, g_post2, w_in, g_q, g_kv,
              w_uq, w_ukv, rpb, b_ml_gates, g_ml, w_br_mla, w_br_na, w_br_ml, w_out,
              w_router, w_e1, w_e3, w_e2):
    xc = ctx
    for l in range(DEPTH):
        ctx_out = l < DEPTH - 1
        mod = jax.nn.silu(c) @ w_mod[l] + b_mod[l]
        mod_c = jax.nn.silu(c_ctx) @ w_mod[l] + b_mod[l]
        sh1, sc1, gt1, sh2, sc2, gt2 = jnp.split(mod[:, None, :], 6, axis=-1)
        shc1, scc1, gtc1, shc2, scc2, gtc2 = jnp.split(mod_c, 6, axis=-1)
        h = rmsnorm(x, g_pre1[l]) * (1.0 + sc1) + sh1
        hc = rmsnorm(xc, g_pre1[l]) * (1.0 + scc1) + shc1
        y, y_c = token_mixers(h, hc, w_in[l], g_q[l], g_kv[l], w_uq[l], w_ukv[l], rpb[l],
                              b_ml_gates[l], g_ml[l], w_br_mla[l], w_br_na[l], w_br_ml[l],
                              w_out[l], ctx_out)
        x = x + gt1 * rmsnorm(y, g_post1[l])
        h2 = rmsnorm(x, g_pre2[l]) * (1.0 + sc2) + sh2
        x = x + gt2 * rmsnorm(expert_choice_ffn(h2, w_router[l], w_e1[l], w_e3[l], w_e2[l]), g_post2[l])
        if ctx_out:
            xc = xc + gtc1 * rmsnorm(y_c, g_post1[l])
            hc2 = rmsnorm(xc, g_pre2[l]) * (1.0 + scc2) + shc2
            xc = xc + gtc2 * rmsnorm(expert_choice_ffn(hc2, w_router[l], w_e1[l], w_e3[l], w_e2[l]), g_post2[l])
    return x


_drawn_inputs = setup_inputs


def setup_inputs(seed=0):
    import zlib

    import numpy as np

    out = dict(_drawn_inputs(seed))
    spreads = {}
    factors = {'g_post2': 3.091, 'g_q': 7.716, 'g_kv': 2.715, 'rpb': 5.281}
    for name, (base, spread) in spreads.items():
        noise = np.random.default_rng([zlib.crc32(name.encode()), seed]).standard_normal(out[name].shape)
        drawn = base * np.exp(spread * noise) if base else spread * noise
        out[name] = jnp.asarray(drawn.astype(out[name].dtype))
    for name, factor in factors.items():
        out[name] = (out[name] * factor).astype(out[name].dtype)
    return out
```

```python
from contextlib import ExitStack

import numpy as np

import concourse.bass as bass
from concourse import mybir

F32 = mybir.dt.float32
ALU = mybir.AluOpType
ACT = mybir.ActivationFunctionType
AX = mybir.AxisListType

P = 128
D = 1024
KD = D // P
CTX = 256
SEQ = 256
T = CTX + SEQ
EPS = 1e-6
NEG = -1e30
GRID_W = 64
HEADS = 4
Q_RANK = 256
NOPE = 64
ROPE = 32
QK = NOPE + ROPE
NA_KR, NA_KC = 8, 16
RPB_R, RPB_C = 2 * NA_KR - 1, 2 * NA_KC - 1
ML_V = 128
N_EXP = 16
CAP = 32
GROUP = P // CAP
SLOTS = 8
SLOT = 2048
BLK = SLOT // KD

C_CQ, C_CKV, C_NQ, C_NK, C_NV = 0, 256, 416, 672, 928
C_MQ, C_MK, C_MV, C_MO, C_MG, C_BG = 1184, 1440, 1696, 2208, 2720, 2736


def rope_table():
    t = np.arange(SEQ)
    pos = np.stack([t // GRID_W, t % GRID_W], 0).astype(np.float32)
    nf = ROPE // 4
    inv = (np.float32(10000.0) ** (-np.arange(nf, dtype=np.float32) / np.float32(nf))).astype(np.float32)
    ang = (pos[:, None, :] * inv[None, :, None]).astype(np.float32)
    cos = np.repeat(np.cos(ang)[:, None], 2, 1).reshape(ROPE, SEQ)
    sin = np.stack([-np.sin(ang), np.sin(ang)], 1).reshape(ROPE, SEQ)
    return np.stack([cos, sin], 1).astype(np.float32)


class Layer:

    def __init__(self, n):
        self.n = n
        self.streams = [0, 1] if n == 0 else [1]
        self.chunks = [2 * s + c for s in self.streams for c in range(2)]
        self.t0 = self.chunks[0] * P
        self.tq = slice(self.t0, T)
        self.nt = len(self.chunks)
        self.ns = len(self.streams)
        self.units = [(kind, h, t) for kind in ("mla", "na") for h in range(HEADS) for t in self.chunks]
        self.pairs = [(h, d) for h in range(HEADS) for d in range(2)]
        self.M = CAP * self.ns
        self.NT = P // self.M
        self.NW = D // self.NT


UNITS0, PAIRS0 = 32, 8
LAYER0 = dict(
    params_mg=16, params=32, wgp_ready=1, wuqr_ready=1, v_ones=1, rel_loaded=16 * 2 * HEADS, rel_mm=1, rel_turned=1, rel_ready=1,
    n1_rstd=4, n1_xn=4, n1_tr=KD, n1_lat=KD, n1_ctx=KD, n2_rstd=4, n2_xn=4, n2_tr=KD, n2_lat=KD, n2_ctx=KD,
    abs_f=1, log1p=1, rows_ready=1, rows_tr=1, cols_ready=1, sc_ready=HEADS, nm_ready=PAIRS0, e1_ready=4 * PAIRS0,
    exp_done=4 * PAIRS0, p_ready=PAIRS0, num_ready=2 * PAIRS0, num_used=2 * PAIRS0, head_rstd=1, hn_ready=1,
    hm_tr=HEADS, mlstm_out=HEADS, krw_ready=1, sq_ready=1, lowrank_ready=1, roped=1,
    attn_score=UNITS0, attn_max=UNITS0, attn_exp=UNITS0, attn_p=UNITS0, attn_tr=UNITS0, attn_pt=UNITS0,
    attn_v=UNITS0, attn_o=UNITS0, mg_gate=24, mg_sig=24, mg_branch=24, mg_used=24, merged=KD,
    wo_ready=16, wo_taken=16, g1_ready=4, g1_taken=4, g2_ready=4, g2_taken=4, post1_rstd=4, post2_rstd=4,
    x_post1=4, x_post2=4, logits=1, lg_shift=1, lg_exp=1, aff_ready=1, affT_tr=1, rank_ready=1, rank_tr=1,
    routed=1, gathered=16, staged=4, gt_tr=4, gt_ready=4, xs_lat=4, xs_ctx=4, silu=N_EXP,
    hid_ready=N_EXP, hid_tr=N_EXP, hidT_ready=N_EXP, y_taken=N_EXP,
    scattered=32, ya_added=33,
)


def before(name, l):
    return LAYER0[name] * l


def weight_loads(layer):
    first = [("mod", 0, 0, k) for k in range(KD)] if layer == 0 else []
    first += [("in", layer, C_MQ, BLK), ("in", layer, C_MK, BLK), ("in", layer, C_MV, BLK), ("in", layer, C_MV + BLK, BLK)]
    if layer == 0:
        first += [("mod", 0, g, k) for g in (1, 2) for k in range(KD)]
    first += [("in", layer, C_MO, BLK), ("in", layer, C_MO + BLK, BLK)]
    first += [("in", layer, C_CQ, BLK), ("in", layer, C_CKV, C_NQ - C_CKV)]
    first += [("in", layer, c, BLK) for c in (C_NQ, C_NK, C_NV)]
    if layer == 0:
        first += [("mod", 1, g, k) for g in range(3) for k in range(KD)]
    for jp in range(KD // 2):
        first += [("br", layer, jp)] + [("in", layer, C_BG + m * D + jp * BLK, BLK) for m in range(3)]
    first += [("out", layer, nb) for nb in range(D // BLK)]
    return first


MOD_GROUPS = [(l, g) for l in range(2) for g in range(3)]
EXP_LOADS = 12
LOOP_LOADS = GROUP * EXP_LOADS
LOOPS = N_EXP // GROUP
BASE = []
_n = 0
for _l in range(2):
    BASE.append(_n)
    _n += len(weight_loads(_l)) + LOOPS * LOOP_LOADS
LOOP_BASE = [BASE[l] + len(weight_loads(l)) for l in range(2)]


def backbone(nc, x, c, ctx, c_ctx, w_mod, b_mod, g_pre1, g_post1, g_pre2, g_post2, w_in, g_q, g_kv, w_uq, w_ukv,
             rpb, b_ml_gates, g_ml, w_br_mla, w_br_na, w_br_ml, w_out, w_router, w_e1, w_e3, w_e2, rope, out):
    with ExitStack() as stack:
        def sb(name, *shape):
            return stack.enter_context(nc.sbuf_tensor(name, [P, *shape], F32))

        sems = {}

        def sem(name):
            if name not in sems:
                sems[name] = stack.enter_context(nc.semaphore(name))
            return sems[name]

        layers = [Layer(0), Layer(1)]

        X = sb("X", 4, D)
        ring = sb("ring", SLOTS, SLOT)
        gate_rows = sb("gate_rows", 4, 512)
        mod_tmp = sb("mod_tmp", 512)
        b_row = sb("b_row", 512)
        g_row = sb("g_row", 512)
        ident = sb("ident", P)
        ones = sb("ones", P)
        flip = sb("flip", P)
        mask_f = sb("mask_f", 512)
        mask_b = sb("mask_b", 640)
        rope_t = sb("rope_t", 2, SEQ)
        iota = sb("iota", CAP)
        wuq = sb("wuq", 2, HEADS * QK)
        wuqr = sb("wuqr", 2, HEADS, ROPE)
        wukv = sb("wukv", HEADS * P)
        wrt = sb("wrt", KD, N_EXP)
        mgw = sb("mgw", KD, 16)
        krw = sb("krw", KD, ROPE)
        vrow = sb("vrow", P)
        vcol = sb("vcol", 32)
        cT = sb("cT", KD, 32)
        modT = sb("modT", 2, 3, 4, 4, 2)
        bml = sb("bml", 2, 2)
        one_add = sb("one_add", 3)
        eps_t = sb("eps_t", 1)
        stat = sb("stat", 64)
        top8 = sb("top8", 8)
        ARENA = 23568
        arena = sb("arena", ARENA)

        def view(at, *dims):
            n = int(np.prod(dims))
            assert at + n <= ARENA, (at, dims)
            v = arena[:, at:at + n]
            if len(dims) == 1:
                return v
            names = "abcde"[:len(dims)]
            return v.rearrange(f"p ({' '.join(names)}) -> p {' '.join(names)}",
                               **{k: d for k, d in zip(names, dims)})

        hT = view(0, KD, T)
        mT = view(4096, HEADS, T)
        wgp = view(6144, KD, 2, 2, 32)
        aT = {"mla": view(6144, 2, T), "na": view(7168, 2, T)}
        mq = view(8192, 2, T)
        mk = view(9216, 2, T)
        sgo = view(8192, HEADS, T)
        mv1 = view(10240, 4, HEADS, ML_V + 1)
        hml = view(12304, 4, HEADS, ML_V)
        E = [view(14352 + 2048 * b, 4, T) for b in range(2)]
        rI, rF, rA, rS, rG = (view(18448 + 512 * b, T) for b in range(5))
        rM = rA
        R3 = view(21008, 3, T)
        gcol = view(22544, 4, 64)
        enm = view(22800, 4, 64)
        xn1 = view(12304, 4, D)
        junk1 = view(20000, D)
        cq = view(10240, 2, T)
        ckv = view(11264, T)
        sq = view(11776, 3, T)
        rs2 = view(13312, 2, T)
        qT = view(14336, HEADS, T)
        kT = view(16384, HEADS, T)
        vM = view(18432, 4, HEADS * 64)
        krt = view(9728, 2, SEQ)
        kr_a, kr_b = (krt[64:96, b, :] for b in range(2))
        qrt = view(12800, HEADS, SEQ)
        nq = view(19456, 2, T)
        nk = view(20480, 2, T)
        nv = view(21504, 4, HEADS * 64)
        BT = view(8192, HEADS, 6, GRID_W)
        Pa = [view(11776 + 512 * b, T) for b in range(2)]
        PT = [view(12800 + 512 * b, T) for b in range(2)]
        merged = view(8192, KD, T)
        sg_m = [view(12288 + 512 * b, T) for b in range(3)]
        tmp_m = view(13824, T)
        Ym = view(14336, 4, D)
        G1 = view(18432, 2, D)
        tmp1 = view(20480, D)
        junk_y = view(21504, D)
        xn2 = view(0, 4, D)
        G2 = view(0, 2, D)
        Ssel = view(4096, 2, 2, 512)
        Sg = view(6144, 2, 2, 512)
        h2T = view(8192, KD, T)
        XST = view(8192, KD, GROUP, 64)
        stg = view(10240, 2, 2, P)
        GT = view(10752, 2, SEQ)
        Yg = view(11264, 2, D)
        Ya = view(13312, 4, D)
        sgh = view(17408, 512)
        hid = view(17920, 512)
        hidT = view(18432, 512)
        tmp2 = view(18944, D)
        junk2 = view(19968, D)
        aff = view(20992, 4, N_EXP)
        lg = view(21056, 4, N_EXP)
        affT = view(21120, SEQ)
        wk = [view(21376 + 256 * b, SEQ) for b in range(2)]
        msk = view(21888, SEQ)
        csum = view(22144, SEQ)
        pmT = view(22400, 2, 32)

        ps = stack.enter_context(nc.psum_tensor("ps", [P, 8, 512], F32))
        COL_C, COL_GQ, COL_GKV, COL_GML = 0, 16, 20, 22

        def mod_col(l, vec, k, s):
            return modT[:, l, vec // 2, k % 4, 2 * (vec % 2) + k // 4, s:s + 1]

        SH1, SC1, GT1, SH2, SC2, GT2 = range(6)

        def w_slot(n):
            return ring[:, n % SLOTS, :]

        landed = [sem(f"weights_landed_{i}") for i in range(SLOTS)]
        used = sem("weights_used")
        small = sem("small_loaded")
        N_SMALL = 13

        block = stack.enter_context(nc.Block())

        @block.sync
        def _(sp):
            sp.dma_start(vrow[0:8, :], c.rearrange("a (k p) -> (a k) p", p=P)).then_inc(small, 16)
            sp.dma_start(vrow[8:16, :], c_ctx.rearrange("(k p) -> k p", p=P)).then_inc(small, 16)
            sp.dma_start(vrow[16:20, :], g_q.rearrange("l (k p) -> (l k) p", p=P)).then_inc(small, 16)
            sp.dma_start(vrow[20:22, :], g_kv).then_inc(small, 16)
            sp.dma_start(vrow[22:30, :], g_ml.rearrange("l (k p) -> (l k) p", p=P)).then_inc(small, 16)
            sp.dma_start(rope_t[64:96, :, :], rope).then_inc(small, 16)
            for s, src in ((1, x), (0, ctx)):
                sp.dma_start(X[:, 2 * s:2 * s + 2, :], src.rearrange("a (c p) d -> p (a c) d", p=P)).then_inc(sem("x_loaded"), 16)

            def load(n, dst, src):
                if n >= SLOTS:
                    sp.wait_ge(used, n - SLOTS + 1)
                sp.dma_start(dst, src).then_inc(landed[n % SLOTS], 16)

            for l in range(2):
                for i, (kind, lw, *a) in enumerate(weight_loads(l)):
                    n = BASE[l] + i
                    if kind == "mod":
                        load(n, w_slot(n), w_mod[lw, a[1] * P:(a[1] + 1) * P, a[0] * SLOT:(a[0] + 1) * SLOT])
                    elif kind == "in":
                        load(n, w_slot(n)[:, 0:KD * a[1]].rearrange("p (k n) -> p k n", k=KD),
                             w_in[lw, :, a[0]:a[0] + a[1]].rearrange("(k p) n -> p k n", p=P))
                    elif kind == "out":
                        load(n, w_slot(n).rearrange("p (k n) -> p k n", k=KD),
                             w_out[lw, :, a[0] * BLK:(a[0] + 1) * BLK].rearrange("(k p) n -> p k n", p=P))
                    else:
                        dst = w_slot(n).rearrange("p (k n) -> p k n", k=KD)
                        if n >= SLOTS:
                            sp.wait_ge(used, n - SLOTS + 1)
                        cols = slice(a[0] * BLK, (a[0] + 1) * BLK)
                        for k0, w in ((0, w_br_mla), (2, w_br_na), (4, w_br_ml)):
                            k1 = k0 + w.shape[1] // P
                            sp.dma_start(dst[:, k0:k1, :], w[lw, :, cols].rearrange("(k p) n -> p k n", p=P))\
                              .then_inc(sem(f"branch_landed_{a[0]}"), 16)
                with sp.Fori(0, LOOPS) as i:
                    for e in range(GROUP):
                        for m, w in enumerate((w_e1, w_e3, w_e2)):
                            we = w[l].rearrange("(i e) (q k p) n -> i e q p k n", e=GROUP, q=4, p=P)
                            for q in range(4):
                                n = LOOP_BASE[l] + e * EXP_LOADS + m * 4 + q
                                sp.wait_ge(used, i * LOOP_LOADS + (n - SLOTS + 1))
                                sp.dma_start(w_slot(n).rearrange("p (k n) -> p k n", k=2),
                                             we[bass.ds(i, 1), e, q].rearrange("i p k n -> p (i k) n"))\
                                  .then_inc(landed[n % SLOTS], 16)
            for s in range(2):
                sp.wait_ge(sem("x_post2"), before("x_post2", 1) + s + 1)
                sp.dma_start(out[0, s * P:(s + 1) * P, :], X[:, 2 + s, :]).then_inc(sem("out_stored"), 16)
            sp.wait_ge(sem("out_stored"), 32)

        @block.gpsimd
        def _(pool):
            done = [0]

            def own(ins):
                done[0] += 1
                ins.then_inc(sem("pool_own"), 1)
                pool.wait_ge(sem("pool_own"), done[0])

            own(pool.memset(ident[:, :], 0.0))
            pool.affine_select(out=ident[:, :], in_=ident[:, :], compare_op=ALU.not_equal, fill=1.0, base=0,
                               pattern=[[-1, P]], channel_multiplier=1).then_inc(sem("ident_ready"), 1)
            own(pool.memset(flip[:, :], 0.0))
            for r in range(2):
                v = flip[64 * r:64 * r + 64, :]
                own(pool.affine_select(out=v, in_=v, compare_op=ALU.not_equal, fill=1.0, base=-(64 * r + 63),
                                       pattern=[[1, P]], channel_multiplier=1))
            pool.memset(ones[:, :], 1.0)
            pool.memset(eps_t[:, :], EPS)
            own(pool.memset(one_add[:, :], 0.0))
            own(pool.memset(one_add[64:128, 0:1], 1.0))
            own(pool.memset(one_add[0:64, 2:3], 1.0))
            pool.memset(b_row[:, :], 0.0)
            pool.memset(g_row[:, :], 1.0)
            pool.memset(cT[:, :, :], 0.0)
            pool.memset(bml[:, :, :], 0.0)
            pool.memset(mask_f[:, :], 0.0)
            own(pool.memset(mask_b[:, :], 0.0))
            pool.affine_select(out=mask_f[:, 0:P], in_=mask_f[:, 0:P], compare_op=ALU.is_ge, fill=NEG, base=0,
                               pattern=[[1, P]], channel_multiplier=-1)
            pool.affine_select(out=mask_b[:, P:2 * P], in_=mask_b[:, P:2 * P], compare_op=ALU.is_ge, fill=NEG, base=0,
                               pattern=[[-1, P]], channel_multiplier=1)
            own(pool.iota(iota[:, :], pattern=[[1, CAP]], base=0, channel_multiplier=0,
                          allow_small_or_imprecise_dtypes=True))
            pool.nop().then_inc(sem("consts_ready"), 1)
            for d in range(2):
                for l in range(2):
                    pool.dma_start(bml[32 * d:32 * d + 4, l, :],
                                   b_ml_gates[l].rearrange("(d f h) -> d h f", d=2, f=2)[d],
                                   allow_slow_non_contiguous=True).then_inc(sem("bml_loaded"), 16)

            rows_loaded = [0]

            def mod_rows(o):
                l, g = MOD_GROUPS[o]
                if o:
                    pool.wait_ge(sem("mod_row"), o)
                gains = {0: (None, g_pre1), 1: (g_post1, None), 2: (g_pre2, g_post2)}[g]
                for half, src in enumerate(gains):
                    if src is None:
                        own(pool.memset(g_row[64 * half:64 * half + 64, :], 1.0))
                for r in range(2):
                    pool.dma_start(b_row[r:r + 97:32, :],
                                   b_mod[l, g * 2048:(g + 1) * 2048].rearrange("(j n) -> j n", j=4))\
                        .then_inc(sem("mod_rows_loaded"), 16)
                    rows_loaded[0] += 16
                    for half, src in enumerate(gains):
                        if src is not None:
                            p0 = 64 * half + r
                            pool.dma_start(g_row[p0:p0 + 33:32, :], src[l].rearrange("(j n) -> j n", j=2))\
                                .then_inc(sem("mod_rows_loaded"), 16)
                            rows_loaded[0] += 16
                pool.wait_ge(sem("mod_rows_loaded"), rows_loaded[0])
                pool.nop().then_inc(sem("mod_rows_ready"), 1)

            def params(l):
                if l:
                    pool.wait_ge(sem("attn_score"), 1)
                pool.dma_start(mgw[:, :, :], w_in[l, :, C_MG:C_BG].rearrange("(k p) n -> p k n", p=P))\
                    .then_inc(sem("params_mg"), 16)
                pool.dma_start(wuq[:, :, :], w_uq[l].rearrange("(k p) h e -> p k (h e)", p=P))\
                    .then_inc(sem("params"), 16)
                pool.dma_start(wukv[:, :], w_ukv[l].rearrange("p h e -> p (h e)")).then_inc(sem("params"), 16)

            def gates_weights(l):
                if l:
                    pool.wait_ge(sem("x_post2"), 4)
                pool.wait_ge(sem("params_mg"), before("params_mg", l) + 16)
                own(pool.memset(wgp[:, :, :, :, :], 0.0))
                for d in range(2):
                    for f in range(2):
                        at = (2 * d + f) * HEADS
                        own(pool.tensor_copy(wgp[:, :, f, d, 0:HEADS], mgw[:, :, at:at + HEADS]))
                pool.nop().then_inc(sem("wgp_ready"), 1)
                pool.wait_ge(sem("params"), before("params", l) + 32)
                for k in range(2):
                    q = wuq[:, k, :].rearrange("p (h e) -> p h e", h=HEADS)[:, :, NOPE:QK]\
                        .rearrange("p h (a b i) -> p h a b i", a=2, b=2)
                    r = wuqr[:, k, :, :].rearrange("p h (a b i) -> p h a b i", a=2, b=2)
                    for b in range(2):
                        own(pool.tensor_copy(r[:, :, :, b, :], q[:, :, :, 1 - b, :]))
                pool.nop().then_inc(sem("wuqr_ready"), 1)

            def v_ones(l):
                pool.wait_ge(sem("n1_tr"), before("n1_tr", l) + KD)
                pool.memset(mv1[:, :, :, ML_V:ML_V + 1], 1.0).then_inc(sem("v_ones"), 1)
                pool.wait_ge(sem("v_ones"), before("v_ones", l) + 1)

            def rel_bias(l):
                pool.wait_ge(sem("mlstm_out"), before("mlstm_out", l) + HEADS)
                for r in range(2):
                    for h in range(HEADS):
                        at = ((l * HEADS + h) * RPB_R + NA_KR - 1 - 2 - r) * RPB_C + NA_KC - GRID_W
                        src = bass.AP(rpb.tensor, at, [[1, GRID_W], [RPB_C, 6], [1, GRID_W]])
                        pool.dma_start(BT[64 * r:64 * r + 64, h, :, :], src).then_inc(sem("rel_loaded"), 16)
                pool.wait_ge(sem("rel_turned"), before("rel_turned", l) + 1)
                half = NA_KC // 2
                for r in range(2):
                    v = BT[64 * r:64 * r + 64].rearrange("p h d c -> p (h d) c")
                    a, b = v[:, :, 0:GRID_W - NA_KC], v[:, :, NA_KC:GRID_W]
                    own(pool.affine_select(out=a, in_=a, compare_op=ALU.is_ge, fill=NEG, base=half,
                                           pattern=[[0, 24], [1, GRID_W - NA_KC]], channel_multiplier=-1))
                    own(pool.affine_select(out=b, in_=b, compare_op=ALU.is_ge, fill=NEG, base=half - 1 - NA_KC,
                                           pattern=[[0, 24], [-1, GRID_W - NA_KC]], channel_multiplier=1))
                pool.nop().then_inc(sem("rel_ready"), 1)

            mod_rows(0)
            params(0)
            gates_weights(0)
            v_ones(0)
            mod_rows(1)
            mod_rows(2)
            mod_rows(3)
            pool.dma_start(wrt[:, :, :], w_router[0].rearrange("(k p) n -> p k n", p=P)).then_inc(sem("router_loaded"), 16)
            rel_bias(0)
            mod_rows(4)
            mod_rows(5)
            params(1)
            for l, L in enumerate(layers):
                pool.wait_ge(sem("routed"), before("routed", l) + 1)
                if l == 0:
                    pool.wait_ge(sem("logits"), 1)
                    pool.dma_start(wrt[:, :, :], w_router[1].rearrange("(k p) n -> p k n", p=P))\
                        .then_inc(sem("router_loaded"), 16)
                with pool.Fori(0, LOOPS) as i:
                    pool.wait_ge(sem("gathered"), before("gathered", l) + i * (2 * L.ns) + 1)
                    for si in range(L.ns):
                        for c2 in range(2):
                            ins = pool.tensor_copy(stg[:, si, c2, :], Sg[:, si, c2, bass.ds(i * P, P)])
                    ins.then_inc(sem("staged"), 1)
                if l == 0:
                    gates_weights(1)
                    v_ones(1)
                    rel_bias(1)

        @block.tensor
        def _(pe):
            taken = [0]

            def next_slot(extra=None):
                n = taken[0]
                taken[0] += 1
                pe.wait_ge(landed[n % SLOTS], 16 * uses(n))
                return w_slot(n)

            def transpose(o, i, n):
                return pe.transpose(o, i, ident[0:n, 0:n])

            def mod_group(o):
                l, g = MOD_GROUPS[o]
                if o:
                    pe.wait_ge(sem("mod_row"), o)
                for k in range(KD):
                    w = next_slot()
                    for j in range(4):
                        mm = pe.matmul(ps[32 * j:32 * j + 32, 6, :], cT[:, k, :], w[:, 512 * j:512 * j + 512],
                                       start=k == 0, stop=k == KD - 1)
                    mm.then_inc(used, 1)

            def mod_turn(o):
                l, g = MOD_GROUPS[o]
                src = mod_tmp[:, :] if g == 0 else gate_rows[:, 2 * l + g - 1, :]
                pe.wait_ge(sem("mod_row"), o + 1)
                if o:
                    pe.wait_ge(sem("mod_col"), o)
                for b in range(4):
                    mm = transpose(ps[:, 7, 128 * b:128 * b + 128], src[:, 128 * b:128 * b + 128], P)
                mm.then_inc(sem("mod_tr"), 1)

            def norm_turn(l, which, src, chunks):
                n = f"n{which}"
                pe.wait_ge(sem(f"{n}_xn"), before(f"{n}_xn", l) + len(chunks))
                for k in range(KD):
                    if k >= 2:
                        pe.wait_ge(sem(f"{n}_lat"), before(f"{n}_lat", l) + k - 1)
                        if 0 in chunks:
                            pe.wait_ge(sem(f"{n}_ctx"), before(f"{n}_ctx", l) + k - 1)
                    for t in chunks:
                        mm = transpose(ps[:, 2 * (t // 2) + k % 2, (t % 2) * P:(t % 2 + 1) * P], src[:, t, k * P:(k + 1) * P], P)
                    mm.then_inc(sem(f"{n}_tr"), 1)
                pe.wait_ge(sem(f"{n}_lat"), before(f"{n}_lat", l) + KD)
                if 0 in chunks:
                    pe.wait_ge(sem(f"{n}_ctx"), before(f"{n}_ctx", l) + KD)

            pj = [0]

            def project(l, o, pairs, release=False):
                i = pj[0]
                if i >= 4:
                    pe.wait_ge(sem("proj_taken"), i - 3)
                pj[0] += 1
                for k, (a, b) in enumerate(pairs):
                    mm = pe.matmul(o(ps[:, i % 4, :]), a, b, start=k == 0, stop=k == len(pairs) - 1)
                mm.then_inc(sem("proj_ready"), 1)
                if release:
                    pe.wait_ge(sem("proj_ready"), i + 1)
                    pe.nop().then_inc(used, 1)

            def blk(w, n=BLK):
                return w[:, 0:KD * n].rearrange("p (k n) -> p k n", k=KD)

            def feature_major(l, w, cols, tok, release):
                for j, c0 in enumerate(cols):
                    project(l, lambda b: b[:, tok], [(w[:, k, c0:c0 + P], hT[:, k, tok]) for k in range(KD)],
                            release and j == len(cols) - 1)

            def token_major(l, w):
                for t in range(4):
                    project(l, lambda b: b[:, 0:BLK], [(hT[:, k, t * P:(t + 1) * P], w[:, k, :]) for k in range(KD)],
                            t == 3)

            for l, L in enumerate(layers):
                tq = L.tq
                if l == 0:
                    pe.wait_ge(sem("ident_ready"), 1)
                    pe.wait_ge(sem("vrow_ready"), 1)
                    transpose(ps[:, 7, 0:30], vrow[0:30, :], 30).then_inc(sem("vrow_tr"), 1)
                    pe.wait_ge(sem("vcol_ready"), 1)
                    mod_group(0)
                    mod_turn(0)
                norm_turn(l, 1, xn1, range(4))
                feature_major(l, blk(next_slot()), (0, P), tq, True)
                feature_major(l, blk(next_slot()), (0, P), slice(0, T), True)
                for _ in range(2):
                    token_major(l, blk(next_slot()))
                pe.wait_ge(sem("wgp_ready"), before("wgp_ready", l) + 1)
                for f in range(2):
                    project(l, lambda b: b[0:64, :], [(wgp[:, k, f, :, :], hT[:, k, :]) for k in range(KD)])
                if l == 0:
                    for o in (1, 2):
                        mod_group(o)
                        mod_turn(o)
                pe.wait_ge(sem("rows_ready"), before("rows_ready", l) + 1)
                pe.wait_ge(sem("proj_taken"), pj[0])
                for r, j in ((0, 0), (1, 2)):
                    for t in range(4):
                        mm = transpose(ps[:, 4, 256 * r + 64 * t:256 * r + 64 * t + 64],
                                       R3[0:64, j, t * P:(t + 1) * P], 64)
                mm.then_inc(sem("rows_tr"), 1)
                pe.wait_ge(sem("cols_ready"), before("cols_ready", l) + 1)
                pe.wait_ge(sem("v_ones"), before("v_ones", l) + 1)

                def scores_ml(h):
                    if h:
                        pe.wait_ge(sem("p_ready"), before("p_ready", l) + 2 * h)
                    p0 = 64 * (h % 2)
                    for s in range(4):
                        o = ps[:, s, tq] if s < 2 else ps[:, 2, 256 * (s - 2):256 * (s - 2) + 256]
                        q0 = tq if s < 2 else slice(CTX, T)
                        mm = pe.matmul(o, mk[p0:p0 + 64, h // 2, s * P:(s + 1) * P], mq[p0:p0 + 64, h // 2, q0],
                                       start=True, stop=True)
                    mm.then_inc(sem("sc_ready"), 1)

                def spread_m(u):
                    h, d = L.pairs[u]
                    if u >= 2:
                        pe.wait_ge(sem("e1_ready"), before("e1_ready", l) + 4 * (u - 1))
                    r = 32 * d + h
                    pe.matmul(ps[:, 3 + d, tq], ident[0:64, r:r + 1].to_broadcast([64, P]), R3[0:64, 1, tq],
                              start=True, stop=True).then_inc(sem("nm_ready"), 1)

                def values_ml(u):
                    h, d = L.pairs[u]
                    for pi in range(L.nt // 2):
                        o = u * (L.nt // 2) + pi
                        if o >= 3:
                            pe.wait_ge(sem("num_used"), before("num_used", l) + o - 2)
                        for ti in range(2):
                            t = L.chunks[2 * pi + ti]
                            keys = keys_of(t, d)
                            for j, s in enumerate(keys):
                                mm = pe.matmul(ps[:, 5 + o % 3, ti * 129:ti * 129 + 129],
                                               E[u % 2][:, s, t * P:(t + 1) * P], mv1[:, s, h, :],
                                               start=j == 0, stop=j == len(keys) - 1)
                        mm.then_inc(sem("num_ready"), 1)

                if l == 0:
                    pe.wait_ge(sem("mod_col"), 3)
                scores_ml(0)
                spread_m(0)
                spread_m(1)
                for u, (h, d) in enumerate(L.pairs):
                    pe.wait_ge(sem("p_ready"), before("p_ready", l) + u + 1)
                    if d == 1 and h + 1 < HEADS:
                        scores_ml(h + 1)
                    values_ml(u)
                    if u + 2 < len(L.pairs):
                        spread_m(u + 2)
                pe.wait_ge(sem("e1_ready"), before("e1_ready", l) + 4 * len(L.pairs))
                for _ in range(2):
                    feature_major(l, blk(next_slot()), (0, P), tq, True)
                pe.wait_ge(sem("hn_ready"), before("hn_ready", l) + 1)
                for h in range(HEADS):
                    if h >= 2:
                        pe.wait_ge(sem("mlstm_out"), before("mlstm_out", l) + h - 1)
                    for t in L.chunks:
                        mm = transpose(ps[:, 4 + h % 2, t * P:(t + 1) * P], hml[:, t, h, :], P)
                    mm.then_inc(sem("hm_tr"), 1)
                pe.wait_ge(sem("mlstm_out"), before("mlstm_out", l) + HEADS)
                feature_major(l, blk(next_slot()), (0, P), tq, True)
                w = blk(next_slot(), C_NQ - C_CKV)
                feature_major(l, w, (0,), slice(0, T), False)
                project(l, lambda b: b[64:96, :], [(w[:, k, P:P + ROPE], hT[:, k, :]) for k in range(KD)])
                pe.wait_ge(sem("krw_ready"), before("krw_ready", l) + 1)
                project(l, lambda b: b[64:96, 0:SEQ], [(krw[:, k, :], hT[:, k, CTX:T]) for k in range(KD)], True)
                feature_major(l, blk(next_slot()), (0, P), tq, True)
                feature_major(l, blk(next_slot()), (0, P), slice(0, T), True)
                token_major(l, blk(next_slot()))
                pe.wait_ge(sem("sq_ready"), before("sq_ready", l) + 1)
                project(l, lambda b: b[:, tq], [(ones[:, :], sq[:, k, tq]) for k in range(2)])
                project(l, lambda b: b[:, :], [(ones[:, :], sq[:, 2, :])])
                pe.wait_ge(sem("lowrank_ready"), before("lowrank_ready", l) + 1)
                pe.wait_ge(sem("wuqr_ready"), before("wuqr_ready", l) + 1)
                for h in range(HEADS):
                    project(l, lambda b: b[0:QK, tq], [(wuq[:, k, h * QK:(h + 1) * QK], cq[:, k, tq]) for k in range(2)])
                for h in range(HEADS):
                    project(l, lambda b: b[64:96, 0:SEQ], [(wuqr[:, k, h, :], cq[:, k, CTX:T]) for k in range(2)])
                for h in range(HEADS):
                    project(l, lambda b: b[0:64, :], [(wukv[:, h * P:h * P + 64], ckv[:, :])])
                wv = wukv[:, :].rearrange("p (h e) -> p h e", h=HEADS)[:, :, 64:P]
                for t in range(4):
                    project(l, lambda b: b[:, 0:256].rearrange("p (h e) -> p h e", h=HEADS), [(ckv[:, t * P:(t + 1) * P], wv)])
                pe.wait_ge(sem("proj_taken"), pj[0])
                pe.wait_ge(sem("roped"), before("roped", l) + 1)
                pe.wait_ge(sem("rel_loaded"), before("rel_loaded", l) + 2 * HEADS * 16)
                bt = BT.rearrange("p h d c -> p (h d c)")
                for b in range(3):
                    mm = pe.matmul(ps[:, b, :], flip[:, :], bt[:, 512 * b:512 * b + 512], start=True, stop=True)
                mm.then_inc(sem("rel_mm"), 1)
                pe.wait_ge(sem("rel_turned"), before("rel_turned", l) + 1)
                if l == 0:
                    mod_group(3)
                    mod_turn(3)

                def score(i):
                    kind, h, t = L.units[i]
                    nkey = T if t >= 2 else CTX
                    if i >= 2:
                        pe.wait_ge(sem("attn_exp"), before("attn_exp", l) + i - 1)
                    p0 = 64 * (h % 2)
                    if kind == "mla":
                        a, b = qT[0:QK, h, t * P:(t + 1) * P], kT[0:QK, h, 0:nkey]
                    else:
                        a, b = nq[p0:p0 + 64, h // 2, t * P:(t + 1) * P], nk[p0:p0 + 64, h // 2, 0:nkey]
                    pe.matmul(ps[:, i % 2, 0:nkey], a, b, start=True, stop=True).then_inc(sem("attn_score"), 1)

                def turn(i):
                    kind, h, t = L.units[i]
                    nk_ = 4 if t >= 2 else 2
                    pe.wait_ge(sem("attn_p"), before("attn_p", l) + i + 1)
                    if i >= 2:
                        pe.wait_ge(sem("attn_pt"), before("attn_pt", l) + i - 1)
                    for j in range(nk_):
                        mm = transpose(ps[:, 2 + i % 2, j * P:(j + 1) * P], Pa[i % 2][:, j * P:(j + 1) * P], P)
                    mm.then_inc(sem("attn_tr"), 1)

                def values(i):
                    kind, h, t = L.units[i]
                    nk_ = 4 if t >= 2 else 2
                    v = vM if kind == "mla" else nv
                    pe.wait_ge(sem("attn_pt"), before("attn_pt", l) + i + 1)
                    if i >= 2:
                        pe.wait_ge(sem("attn_o"), before("attn_o", l) + i - 1)
                    p0 = 64 * (h % 2)
                    for j in range(nk_):
                        mm = pe.matmul(ps[p0:p0 + 64, 4 + i % 2, 0:P], v[:, j, h * 64:(h + 1) * 64],
                                       PT[i % 2][:, j * P:(j + 1) * P], start=j == 0, stop=j == nk_ - 1)
                    mm.then_inc(sem("attn_v"), 1)

                nu = len(L.units)
                for i in range(nu + 2):
                    if i < nu:
                        score(i)
                    if 1 <= i <= nu:
                        turn(i - 1)
                    if i >= 2:
                        values(i - 2)
                    if l == 0 and i in (nu // 3, 2 * nu // 3):
                        o = 4 + (i > nu // 3)
                        mod_group(o)
                        mod_turn(o)
                pe.wait_ge(sem("attn_o"), before("attn_o", l) + nu)
                u = 0
                for jp in range(KD // 2):
                    taken[0] += 1
                    wb = blk(w_slot(taken[0] - 1))
                    pe.wait_ge(sem(f"branch_landed_{jp}"), 48 * (l + 1))
                    for m in range(3):
                        wg = blk(next_slot())
                        for half in range(2):
                            if u >= 3:
                                pe.wait_ge(sem("mg_used"), before("mg_used", l) + u - 2)
                            cols = slice(half * P, (half + 1) * P)
                            for k in range(KD):
                                mm = pe.matmul(ps[:, u % 3, tq], wg[:, k, cols], hT[:, k, tq],
                                               start=k == 0, stop=k == KD - 1)
                            mm.then_inc(sem("mg_gate"), 1)
                            src = [(0, aT["mla"]), (2, aT["na"]), (4, mT)][m]
                            nk_ = 4 if m == 2 else 2
                            for k in range(nk_):
                                mm = pe.matmul(ps[:, 3 + u % 3, tq], wb[:, src[0] + k, cols], src[1][:, k, tq],
                                               start=k == 0, stop=k == nk_ - 1)
                            mm.then_inc(sem("mg_branch"), 1)
                            u += 1
                    pe.wait_ge(sem("mg_branch"), before("mg_branch", l) + u)
                    pe.nop().then_inc(used, 4)
                pe.wait_ge(sem("merged"), before("merged", l) + KD)
                o = 0
                for nb in range(4):
                    w = blk(next_slot())
                    for t in L.chunks:
                        if o >= 6:
                            pe.wait_ge(sem("wo_taken"), before("wo_taken", l) + o - 5)
                        for k in range(KD):
                            mm = pe.matmul(ps[:, o % 6, 0:BLK], merged[:, k, t * P:(t + 1) * P], w[:, k, :],
                                           start=k == 0, stop=k == KD - 1)
                        mm.then_inc(sem("wo_ready"), 1)
                        o += 1
                    pe.wait_ge(sem("wo_ready"), before("wo_ready", l) + o)
                    pe.nop().then_inc(used, 1)

                def spread_gate(which):
                    row = gate_rows[:, 2 * l + which - 1, :]
                    for si, s in enumerate(L.streams):
                        for half in range(2):
                            g = si * 2 + half
                            if g >= 2:
                                pe.wait_ge(sem(f"g{which}_taken"), before(f"g{which}_taken", l) + g - 1)
                            r = 32 * ((2 if which == 2 else 0) + half) + s
                            pe.matmul(ps[:, 6 + half, :], ident[:, r:r + 1].to_broadcast([P, P]), row,
                                      start=True, stop=True).then_inc(sem(f"g{which}_ready"), 1)

                pe.wait_ge(sem("mod_col"), 6)
                spread_gate(1)
                pe.wait_ge(sem("wo_taken"), before("wo_taken", l) + o)
                norm_turn(l, 2, xn2, L.chunks)
                pe.wait_ge(sem("router_loaded"), 16 * (l + 1))
                for c2 in range(2):
                    for si, s in enumerate(L.streams):
                        t = 2 * s + c2
                        at = (c2 * L.ns + si) * N_EXP
                        for k in range(KD):
                            mm = pe.matmul(ps[:, 0, at:at + N_EXP], h2T[:, k, t * P:(t + 1) * P], wrt[:, k, :],
                                           start=k == 0, stop=k == KD - 1)
                mm.then_inc(sem("logits"), 1)
                R = N_EXP * L.ns
                pe.wait_ge(sem("aff_ready"), before("aff_ready", l) + 1)
                for c2 in range(2):
                    mm = transpose(ps[0:R, 1, c2 * P:(c2 + 1) * P],
                                   aff[:, c2 * L.ns:(c2 + 1) * L.ns, :].rearrange("p s e -> p (s e)"), P)
                mm.then_inc(sem("affT_tr"), 1)
                pe.wait_ge(sem("rank_ready"), before("rank_ready", l) + 1)
                for c2 in range(2):
                    mm = transpose(ps[:, 2, 32 * c2:32 * c2 + R], csum[0:R, c2 * P:(c2 + 1) * P], R)
                mm.then_inc(sem("rank_tr"), 1)
                pe.wait_ge(sem("routed"), before("routed", l) + 1)
                M, NT, NW = L.M, L.NT, L.NW
                NB_ = 4 * L.ns
                with pe.Fori(0, LOOPS) as i:
                    pe.wait_ge(sem("ya_added"), before("ya_added", l) + i * NB_ + 1)
                    for si, s in enumerate(L.streams):
                        for k in range(KD):
                            for c2 in range(2):
                                mm = pe.matmul(ps[:, 2 * si + k // 4, (k % 4) * P:(k % 4 + 1) * P],
                                               xn2[:, 2 * s + c2, k * P:(k + 1) * P],
                                               Ssel[:, si, c2, bass.ds(i * P, P)], start=c2 == 0, stop=c2 == 1)
                            if k % 4 == 3:
                                mm.then_inc(sem("gathered"), 1)
                    pe.wait_ge(sem("staged"), before("staged", l) + i + 1)
                    for si in range(L.ns):
                        for c2 in range(2):
                            mm = transpose(ps[:, 4, (2 * si + c2) * P:(2 * si + c2 + 1) * P], stg[:, si, c2, :], P)
                    mm.then_inc(sem("gt_tr"), 1)
                    pe.wait_ge(sem("gt_ready"), before("gt_ready", l) + i + 1)
                    pe.wait_ge(sem("xs_lat"), before("xs_lat", l) + i + 1)
                    if L.ns == 2:
                        pe.wait_ge(sem("xs_ctx"), before("xs_ctx", l) + i + 1)

                    for e in range(GROUP):
                        def slot(j):
                            n = LOOP_BASE[l] + e * EXP_LOADS + j
                            pe.wait_ge(landed[n % SLOTS], i * (16 * LOOP_LOADS // SLOTS) + 16 * uses(n))
                            return w_slot(n).rearrange("p (k n) -> p k n", k=2)

                        b0 = 2 * (e % 2)
                        for m in range(2):
                            for q in range(4):
                                w = slot(4 * m + q)
                                for k in range(2):
                                    kk = 2 * q + k
                                    for j in range(NT):
                                        mm = pe.matmul(ps[M * j:M * j + M, b0 + m, 0:NW], XST[:, kk, e, 0:M],
                                                       w[:, k, j * NW:(j + 1) * NW], start=kk == 0, stop=kk == KD - 1)
                                mm.then_inc(used, 1)
                        pe.wait_ge(sem("hid_ready"), before("hid_ready", l) + i * GROUP + (e + 1))
                        nb = NW // P
                        for b in range(nb):
                            mm = transpose(ps[:, 4 + e % 2, b * P:(b + 1) * P], hid[:, b * P:(b + 1) * P], P)
                        mm.then_inc(sem("hid_tr"), 1)
                        pe.wait_ge(sem("hidT_ready"), before("hidT_ready", l) + i * GROUP + (e + 1))
                        if e >= 2:
                            pe.wait_ge(sem("y_taken"), before("y_taken", l) + i * GROUP + (e - 1))
                        for q in range(4):
                            w = slot(8 + q)
                            for k in range(2):
                                kk = 2 * q + k
                                lhs = hidT[:, (kk % nb) * P + (kk // nb) * M:(kk % nb) * P + (kk // nb) * M + M]
                                for j in range(NT):
                                    mm = pe.matmul(ps[M * j:M * j + M, 6 + e % 2, 0:NW], lhs,
                                                   w[:, k, j * NW:(j + 1) * NW], start=kk == 0, stop=kk == KD - 1)
                            mm.then_inc(used, 1)
                    pe.wait_ge(sem("y_taken"), before("y_taken", l) + i * GROUP + GROUP)
                    for o in range(NB_):
                        si, c2, half = o // 4, (o // 2) % 2, o % 2
                        if o >= 4:
                            pe.wait_ge(sem("ya_added"), before("ya_added", l) + i * NB_ + (o - 4 + 2))
                        pe.matmul(ps[:, o % 4, :], GT[:, si, c2 * P:(c2 + 1) * P], Yg[:, si, half * 512:(half + 1) * 512],
                                  start=True, stop=True).then_inc(sem("scattered"), 1)
                taken[0] += LOOPS * LOOP_LOADS
                spread_gate(2)
                if l == 0:
                    pe.wait_ge(sem("g2_taken"), 4)
                    pe.wait_ge(sem("ya_added"), 8 * LOOPS + 1)

        @block.scalar
        def _(act):
            done = [0]

            def own(ins):
                done[0] += 1
                ins.then_inc(sem("act_own"), 1)
                act.wait_ge(sem("act_own"), done[0])

            def copy(o, i):
                return act.activation(o, i, ACT.Copy)

            def rstd(o, i, n):
                own(act.activation(o, i, ACT.Ln, bias=eps_t[:, 0:1], scale=1.0 / n))
                return act.activation(o, o, ACT.Exp, scale=-0.5)

            def exp_ln():
                act.preload_act_table_set("natural_log_exp_and_others")

            def mod_cols(o):
                l, g = MOD_GROUPS[o]
                act.wait_ge(sem("mod_tr"), o + 1)
                src = ps[:, 7, :].rearrange("p (b j r) -> p b j r", b=4, r=32)[:, :, :, 0:2]
                copy(modT[:, l, g, :, :, :], src).then_inc(sem("mod_col"), 1)

            def norm(l, which, chunks, ready, junk):
                n = f"n{which}"
                for j, t in enumerate(chunks):
                    ready(j, t)
                    own(act.activation(junk, X[:, t, :], ACT.Square, accum_out=stat[:, t:t + 1]))
                    rstd(stat[:, t:t + 1], stat[:, t:t + 1], D).then_inc(sem(f"{n}_rstd"), 1)

            def norm_ctx(l, which, dst):
                n = f"n{which}"
                sc, sh = ((SC1, SH1), (SC2, SH2))[which - 1]
                for k in range(KD):
                    act.wait_ge(sem(f"{n}_tr"), before(f"{n}_tr", l) + k + 1)
                    act.activation(dst[:, k, 0:CTX], ps[:, k % 2, 0:CTX], ACT.Identity, bias=mod_col(l, sh, k, 0),
                                   scale=mod_col(l, sc, k, 0)).then_inc(sem(f"{n}_ctx"), 1)

            pj = [0]

            def bank():
                i = pj[0]
                pj[0] += 1
                act.wait_ge(sem("proj_ready"), i + 1)
                return ps[:, i % 4, :]

            def took(ins):
                ins.then_inc(sem("proj_taken"), 1)

            def took_plain(o, i, func=ACT.Copy, scale=1.0):
                took(act.activation(o, i, func, scale=scale))

            act.wait_ge(small, 16 * 6)
            act.activation(vrow[0:16, :], vrow[0:16, :], ACT.Silu).then_inc(sem("vrow_ready"), 1)
            act.wait_ge(sem("vrow_tr"), 1)
            act.wait_ge(sem("consts_ready"), 1)
            own(copy(vcol[:, 0:30], ps[:, 7, 0:30]))
            for s, at in ((1, 0), (0, 8)):
                ins = copy(cT[:, :, s:s + 1], vcol[:, at:at + 8].rearrange("p (k a) -> p k a", a=1))
            ins.then_inc(sem("vcol_ready"), 1)
            exp_ln()

            for l, L in enumerate(layers):
                tq, nt = L.tq, L.nt
                if l == 0:
                    norm(l, 1, range(4), lambda j, t: act.wait_ge(sem("x_loaded"), 32), junk1)
                    mod_cols(0)
                else:
                    norm(l, 1, range(4), lambda j, t: act.wait_ge(sem("x_post2"), t + 1), junk1)
                norm_ctx(l, 1, hT)
                for c2 in range(2):
                    took_plain(mq[:, c2, tq], bank()[:, tq])
                for c2 in range(2):
                    took_plain(mk[:, c2, :], bank(), scale=0.125)
                for half in range(2):
                    for t in range(4):
                        took_plain(mv1[:, t, 2 * half:2 * half + 2, 0:ML_V],
                                   bank()[:, 0:256].rearrange("p (h v) -> p h v", h=2))
                act.wait_ge(sem("bml_loaded"), 64)
                for f, row in enumerate((rI, rF)):
                    b = bank()
                    act.activation(row[0:32, :], b[0:32, :], ACT.Identity, bias=bml[0:32, l, f:f + 1])
                    took(act.activation(row[32:64, :].rearrange("p (s t) -> p s t", s=2)[:, :, ::-1],
                                        b[32:64, :].rearrange("p (s t) -> p s t", s=2), ACT.Identity,
                                        bias=bml[32:64, l, f:f + 1]))
                act.wait_ge(sem("abs_f"), before("abs_f", l) + 1)
                own(act.activation(rA[0:64, :], rA[0:64, :], ACT.Exp, scale=-1.0))
                act.activation(rA[0:64, :], rA[0:64, :], ACT.Ln, bias=1.0).then_inc(sem("log1p"), 1)
                if l == 0:
                    mod_cols(1)
                    mod_cols(2)
                act.wait_ge(sem("rows_tr"), before("rows_tr", l) + 1)
                copy(gcol, ps[:, 4, 0:256].rearrange("p (t r) -> p t r", t=4))
                act.activation(enm, ps[:, 4, 256:512].rearrange("p (t r) -> p t r", t=4), ACT.Exp, scale=-1.0)\
                    .then_inc(sem("cols_ready"), 1)
                for u in range(len(L.pairs)):
                    d = L.pairs[u][1]
                    for s in range(4):
                        act.wait_ge(sem("e1_ready"), before("e1_ready", l) + 4 * u + s + 1)
                        t0, t1, _ = span(L, d, s)
                        e = E[u % 2][:, s, t0 * P:t1 * P]
                        act.activation(e, e, ACT.Exp).then_inc(sem("exp_done"), 1)
                act.wait_ge(sem("num_used"), before("num_used", l) + len(L.pairs) * nt // 2)
                act.wait_ge(sem("act_own"), done[0])
                for t in L.chunks:
                    for h in range(HEADS):
                        ins = act.activation(E[0][:, t, 0:ML_V], hml[:, t, h, :], ACT.Square,
                                             accum_out=stat[:, 16 + 4 * t + h:17 + 4 * t + h])
                        own(ins)
                a = stat[:, 16 + 4 * L.chunks[0]:32]
                rstd(a, a, ML_V).then_inc(sem("head_rstd"), 1)
                for h in range(HEADS):
                    took_plain(sgo[:, h, tq], bank()[:, tq], ACT.Sigmoid)
                exp_ln()
                w = w_slot(BASE[l] + krw_load(l))[:, 0:KD * 160].rearrange("p (k n) -> p k n", k=KD)[:, :, P:160]\
                    .rearrange("p k (a b i) -> p k a b i", a=2, b=2)
                n = BASE[l] + krw_load(l)
                act.wait_ge(sem("mlstm_out"), before("mlstm_out", l) + HEADS)
                for c2 in range(2):
                    b = bank()
                    copy(cq[:, c2, tq], b[:, tq])
                    took(act.activation(sq[:, c2, tq], b[:, tq], ACT.Square))
                act.wait_ge(landed[n % SLOTS], 16 * uses(n))
                kr = krw[:, :, :].rearrange("p k (a b i) -> p k a b i", a=2, b=2)
                for b2 in range(2):
                    ins = copy(kr[:, :, :, b2, :], w[:, :, :, 1 - b2, :])
                ins.then_inc(sem("krw_ready"), 1)
                b = bank()
                copy(ckv, b)
                took(act.activation(sq[:, 2, :], b, ACT.Square))
                act.wait_ge(sem("proj_taken"), pj[0])
                act.nop().then_inc(sem("sq_ready"), 1)
                b = bank()
                copy(kT[64:96, :, 0:CTX], b[64:96, 0:CTX].rearrange("p (a t) -> p a t", a=1).to_broadcast([32, HEADS, CTX]))
                took(copy(kr_a, b[64:96, CTX:T]))
                took(copy(kr_b, bank()[64:96, 0:SEQ]))
                for c2 in range(2):
                    took_plain(nq[:, c2, tq], bank()[:, tq], scale=0.125)
                for c2 in range(2):
                    took_plain(nk[:, c2, :], bank())
                for t in range(4):
                    took_plain(nv[:, t, :], bank()[:, 0:256])
                for j, n_ in ((0, Q_RANK), (1, P)):
                    b = bank()
                    cols = tq if j == 0 else slice(0, T)
                    own(act.activation(rs2[:, j, cols], b[:, cols], ACT.Ln, bias=eps_t[:, 0:1], scale=1.0 / n_))
                    took(act.activation(rs2[:, j, cols], rs2[:, j, cols], ACT.Exp, scale=-0.5))
                scale = float(np.float32(QK) ** np.float32(-0.5))
                act.wait_ge(sem("lowrank_ready"), before("lowrank_ready", l) + 1)
                for h in range(HEADS):
                    took_plain(qT[0:QK, h, tq], bank()[0:QK, tq], scale=scale)
                for h in range(HEADS):
                    took_plain(qrt[64:96, h, :], bank()[64:96, 0:SEQ], scale=scale)
                for h in range(HEADS):
                    took_plain(kT[0:64, h, :], bank()[0:64, :])
                for t in range(4):
                    took_plain(vM[:, t, :], bank()[:, 0:256])
                if l == 0:
                    mod_cols(3)

                def pt_copy(i):
                    n_ = T if L.units[i][2] >= 2 else CTX
                    act.wait_ge(sem("attn_tr"), before("attn_tr", l) + i + 1)
                    if i >= 2:
                        act.wait_ge(sem("attn_v"), before("attn_v", l) + i - 1)
                    copy(PT[i % 2][:, 0:n_], ps[:, 2 + i % 2, 0:n_]).then_inc(sem("attn_pt"), 1)

                nu = len(L.units)
                for i in range(nu + 1):
                    if i < nu:
                        n_ = T if L.units[i][2] >= 2 else CTX
                        act.wait_ge(sem("attn_max"), before("attn_max", l) + i + 1)
                        if i >= 2:
                            act.wait_ge(sem("attn_tr"), before("attn_tr", l) + i - 1)
                        act.activation(Pa[i % 2][:, 0:n_], ps[:, i % 2, 0:n_], ACT.Exp, bias=stat[:, 32 + i % 2:33 + i % 2],
                                       accum_out=stat[:, 34 + i % 2:35 + i % 2]).then_inc(sem("attn_exp"), 1)
                    if i >= 1:
                        pt_copy(i - 1)
                    if l == 0 and i in (nu // 3 + 1, 2 * nu // 3 + 1):
                        mod_cols(4 + (i > nu // 3 + 1))
                for u in range(24):
                    act.wait_ge(sem("mg_gate"), before("mg_gate", l) + u + 1)
                    if u >= 3:
                        act.wait_ge(sem("mg_used"), before("mg_used", l) + u - 2)
                    act.activation(sg_m[u % 3][:, tq], ps[:, u % 3, tq], ACT.Sigmoid).then_inc(sem("mg_sig"), 1)
                exp_ln()
                o = 0
                for nb in range(4):
                    for t in L.chunks:
                        act.wait_ge(sem("wo_ready"), before("wo_ready", l) + o + 1)
                        copy(Ym[:, t, nb * BLK:(nb + 1) * BLK], ps[:, o % 6, 0:BLK]).then_inc(sem("wo_taken"), 1)
                        o += 1

                def gate_rows_taken(which, G):
                    for si, s in enumerate(L.streams):
                        for half in range(2):
                            act.wait_ge(sem(f"g{which}_ready"), before(f"g{which}_ready", l) + 2 * si + half + 1)
                            copy(G[:, s, 512 * half:512 * half + 512], ps[:, 6 + half, :]).then_inc(sem(f"g{which}_taken"), 1)

                def post_stats(which, Y, junk):
                    for j, t in enumerate(L.chunks):
                        own(act.activation(junk, Y[:, t, :], ACT.Square, accum_out=stat[:, 40 + t:41 + t]))
                        rstd(stat[:, 40 + t:41 + t], stat[:, 40 + t:41 + t], D).then_inc(sem(f"post{which}_rstd"), 1)

                gate_rows_taken(1, G1)
                act.wait_ge(sem("wo_taken"), before("wo_taken", l) + o)
                post_stats(1, Ym, junk_y)
                norm(l, 2, L.chunks, lambda j, t: act.wait_ge(sem("x_post1"), before("x_post1", l) + j + 1), junk_y)
                if l == 0:
                    norm_ctx(l, 2, h2T)
                act.wait_ge(sem("lg_shift"), before("lg_shift", l) + 1)
                act.activation(lg[:, 0:2 * L.ns, :], lg[:, 0:2 * L.ns, :], ACT.Exp).then_inc(sem("lg_exp"), 1)
                act.preload_act_table(ACT.Silu)
                M, NT, NW = L.M, L.NT, L.NW
                with act.Fori(0, LOOPS) as i:
                    if L.ns == 2:
                        for k in range(KD):
                            if k % 4 == 0:
                                act.wait_ge(sem("gathered"), before("gathered", l) + i * 4 + (k // 4 + 1))
                            ins = act.activation(XST[:, k, :, 0:CAP],
                                                 ps[:, k // 4, (k % 4) * P:(k % 4 + 1) * P].rearrange("p (e j) -> p e j", e=GROUP),
                                                 ACT.Identity, bias=mod_col(l, SH2, k, 0), scale=mod_col(l, SC2, k, 0))
                        ins.then_inc(sem("xs_ctx"), 1)
                    act.wait_ge(sem("gt_tr"), before("gt_tr", l) + i + 1)
                    copy(GT[:, 0:L.ns, :], ps[:, 4, 0:256 * L.ns].rearrange("p (s t) -> p s t", s=L.ns))\
                        .then_inc(sem("gt_ready"), 1)
                    for e in range(GROUP):
                        act.wait_ge(used, i * LOOP_LOADS + (LOOP_BASE[l] + e * EXP_LOADS + 4))
                        act.activation(sgh[:, 0:NW], ps[:, 2 * (e % 2), 0:NW], ACT.Silu).then_inc(sem("silu"), 1)
                        act.wait_ge(sem("hid_tr"), before("hid_tr", l) + i * GROUP + (e + 1))
                        copy(hidT[:, 0:NW], ps[:, 4 + e % 2, 0:NW]).then_inc(sem("hidT_ready"), 1)
                exp_ln()
                gate_rows_taken(2, G2)
                act.wait_ge(sem("ya_added"), before("ya_added", l) + 4 * L.ns * LOOPS + 1)
                post_stats(2, Ya, junk2)

        @block.vector
        def _(dve):
            done = [0]

            def own(ins):
                done[0] += 1
                ins.then_inc(sem("dve_own"), 1)
                dve.wait_ge(sem("dve_own"), done[0])

            def mod_row(o):
                l, g = MOD_GROUPS[o]
                dst = mod_tmp[:, :] if g == 0 else gate_rows[:, 2 * l + g - 1, :]
                dve.wait_ge(used, mod_load(o) + KD)
                dve.wait_ge(sem("mod_rows_ready"), o + 1)
                own(dve.tensor_tensor(dst, ps[:, 6, :], b_row[:, :], ALU.add))
                dve.scalar_tensor_tensor(out=dst, in0=dst, scalar=one_add[:, g:g + 1], in1=g_row[:, :],
                                         op0=ALU.add, op1=ALU.mult).then_inc(sem("mod_row"), 1)

            def norm(l, which, chunks, dst, hdst):
                n = f"n{which}"
                sc, sh = ((SC1, SH1), (SC2, SH2))[which - 1]
                for j, t in enumerate(chunks):
                    dve.wait_ge(sem(f"{n}_rstd"), before(f"{n}_rstd", l) + j + 1)
                    dve.tensor_scalar(dst[:, t, :], X[:, t, :], stat[:, t:t + 1], None, ALU.mult).then_inc(sem(f"{n}_xn"), 1)
                for k in range(KD):
                    dve.wait_ge(sem(f"{n}_tr"), before(f"{n}_tr", l) + k + 1)
                    dve.tensor_scalar(hdst[:, k, CTX:T], ps[:, 2 + k % 2, 0:SEQ], mod_col(l, sc, k, 1), mod_col(l, sh, k, 1),
                                      ALU.mult, ALU.add).then_inc(sem(f"{n}_lat"), 1)

            dve.wait_ge(sem("consts_ready"), 1)
            for l, L in enumerate(layers):
                tq, nt = L.tq, L.nt
                if l == 0:
                    mod_row(0)
                    dve.wait_ge(sem("mod_col"), 1)
                norm(l, 1, range(4), xn1, hT)
                dve.wait_ge(sem("proj_taken"), pj_base(l) + 14)
                dve.scalar_tensor_tensor(out=rA[0:64, :], in0=rF[0:64, :], scalar=-1.0, in1=rF[0:64, :],
                                         op0=ALU.mult, op1=ALU.max).then_inc(sem("abs_f"), 1)
                dve.wait_ge(sem("log1p"), before("log1p", l) + 1)
                own(dve.scalar_tensor_tensor(out=rS[0:64, :], in0=rF[0:64, :], scalar=0.0, in1=rA[0:64, :],
                                             op0=ALU.min, op1=ALU.subtract))
                own(dve.tensor_tensor_scan(out=rF[0:64, :], data0=ones[0:64, 0:1].to_broadcast([64, T]), data1=rS[0:64, :],
                                           initial=0.0, op0=ALU.mult, op1=ALU.add))
                own(dve.tensor_tensor(rG[0:64, :], rI[0:64, :], rF[0:64, :], ALU.subtract))
                own(dve.tensor_tensor_scan(out=rM[0:64, :], data0=rG[0:64, :], data1=rG[0:64, :], initial=0.0,
                                           op0=ALU.max, op1=ALU.max))
                for d in range(2):
                    rows = slice(32 * d, 32 * d + 32)

                    def natural(a):
                        v = a[rows, :].rearrange("p (s t) -> p s t", s=2)
                        return v[:, :, ::-1] if d else v

                    def plain(a):
                        return a[rows, :].rearrange("p (s t) -> p s t", s=2)

                    dve.tensor_copy(natural(R3[:, 0, :]), plain(rG))
                    dve.tensor_scalar(natural(R3[:, 1, :]), plain(rM), -1.0, None, ALU.mult)
                    ins = dve.tensor_tensor(natural(R3[:, 2, :]), plain(rF), plain(rM), ALU.add)
                ins.then_inc(sem("rows_ready"), 1)
                if l == 0:
                    mod_row(1)
                    mod_row(2)
                dve.wait_ge(sem("cols_ready"), before("cols_ready", l) + 1)

                def exponents(u):
                    h, d = L.pairs[u]
                    dve.wait_ge(sem("nm_ready"), before("nm_ready", l) + u + 1)
                    if u >= 2:
                        dve.wait_ge(sem("num_ready"), before("num_ready", l) + (u - 1) * (nt // 2))
                    for s in range(4):
                        t0, t1, m = span(L, d, s)
                        mask = (mask_f, mask_b)[d]
                        r = 32 * d + h
                        dve.scalar_tensor_tensor(out=E[u % 2][:, s, t0 * P:t1 * P], in0=ps[:, 3 + d, t0 * P:t1 * P],
                                                 scalar=gcol[:, s, r:r + 1], in1=mask[:, m:m + (t1 - t0) * P],
                                                 op0=ALU.add, op1=ALU.min).then_inc(sem("e1_ready"), 1)

                def weigh(u):
                    h, d = L.pairs[u]
                    dve.wait_ge(sem("sc_ready"), before("sc_ready", l) + h + 1)
                    for s in range(4):
                        t0, t1, m = span(L, d, s)
                        sc = ps[:, s, t0 * P:t1 * P] if s < 2 else \
                            ps[:, 2, 256 * (s - 2) + (t0 - 2) * P:256 * (s - 2) + (t1 - 2) * P]
                        e = E[u % 2][:, s, t0 * P:t1 * P]
                        dve.wait_ge(sem("exp_done"), before("exp_done", l) + 4 * u + s + 1)
                        ins = dve.tensor_tensor(e, sc, e, ALU.mult)
                    ins.then_inc(sem("p_ready"), 1)

                def head_out(u):
                    h, d = L.pairs[u]
                    r = 32 * d + h
                    for pi in range(nt // 2):
                        o = u * (nt // 2) + pi
                        ta = L.chunks[2 * pi]
                        b = ps[:, 5 + o % 3, 0:258].rearrange("p (t v) -> p t v", t=2)
                        den = b[:, :, ML_V:ML_V + 1]
                        z = stat[:, 48:50].rearrange("p (t v) -> p t v", v=1)
                        dve.wait_ge(sem("num_ready"), before("num_ready", l) + o + 1)
                        own(dve.scalar_tensor_tensor(out=z, in0=den, scalar=-1.0, in1=enm[:, ta:ta + 2, r:r + 1],
                                                     op0=ALU.mult, op1=ALU.max))
                        own(dve.scalar_tensor_tensor(out=z, in0=den, scalar=1.0, in1=z, op0=ALU.mult, op1=ALU.max))
                        own(dve.reciprocal(z, z))
                        for ti in range(2):
                            hh = hml[:, ta + ti, h, :]
                            if d == 0:
                                ins = dve.tensor_scalar(hh, b[:, ti, 0:ML_V], stat[:, 48 + ti:49 + ti], None, ALU.mult)
                            else:
                                ins = dve.scalar_tensor_tensor(out=hh, in0=b[:, ti, 0:ML_V], scalar=stat[:, 48 + ti:49 + ti],
                                                               in1=hh, op0=ALU.mult, op1=ALU.add)
                        ins.then_inc(sem("num_used"), 1)
                        dve.wait_ge(sem("num_used"), before("num_used", l) + o + 1)

                np_ = len(L.pairs)
                exponents(0)
                for u in range(np_):
                    if u + 1 < np_:
                        exponents(u + 1)
                    weigh(u)
                    if u:
                        head_out(u - 1)
                head_out(np_ - 1)
                c0 = L.chunks[0]
                hv = hml[:, c0:4, :, :].rearrange("p t h v -> p (t h) v")
                rb = stat[:, 16 + 4 * c0:32].rearrange("p (a v) -> p a v", v=1).to_broadcast([P, 4 * nt, ML_V])
                dve.wait_ge(sem("head_rstd"), before("head_rstd", l) + 1)
                dve.tensor_tensor(hv, hv, rb, ALU.mult).then_inc(sem("hn_ready"), 1)
                dve.wait_ge(sem("proj_taken"), pj_base(l) + 18)
                for h in range(HEADS):
                    dve.wait_ge(sem("hm_tr"), before("hm_tr", l) + h + 1)
                    at = COL_GML + 4 * l + h
                    dve.scalar_tensor_tensor(out=mT[:, h, tq], in0=ps[:, 4 + h % 2, tq], scalar=vcol[:, at:at + 1],
                                             in1=sgo[:, h, tq], op0=ALU.mult, op1=ALU.mult)\
                        .then_inc(sem("mlstm_out"), 1)
                dve.wait_ge(small, 16 * 6)
                cos, sin = rope_t[64:96, 0, :], rope_t[64:96, 1, :]
                dve.wait_ge(sem("proj_taken"), pj_base(l) + 23)
                own(dve.tensor_tensor(kr_a, kr_a, cos, ALU.mult))
                own(dve.tensor_tensor(kr_b, kr_b, sin, ALU.mult))

                def heads(a):
                    return a.rearrange("p (a t) -> p a t", a=1).to_broadcast([32, HEADS, SEQ])

                dve.tensor_tensor(kT[64:96, :, CTX:T], heads(kr_a), heads(kr_b), ALU.add)
                dve.wait_ge(sem("proj_taken"), pj_base(l) + 33)
                for c2 in range(2):
                    at = COL_GQ + 2 * l + c2
                    dve.scalar_tensor_tensor(out=cq[:, c2, tq], in0=cq[:, c2, tq], scalar=vcol[:, at:at + 1],
                                             in1=rs2[:, 0, tq], op0=ALU.mult, op1=ALU.mult)
                dve.scalar_tensor_tensor(out=ckv, in0=ckv, scalar=vcol[:, COL_GKV + l:COL_GKV + l + 1],
                                         in1=rs2[:, 1, :], op0=ALU.mult, op1=ALU.mult).then_inc(sem("lowrank_ready"), 1)
                dve.wait_ge(sem("proj_taken"), pj_base(l) + 33 + 2 * HEADS)
                ql = qT[64:96, :, CTX:T]
                own(dve.tensor_tensor(ql, ql, heads(cos), ALU.mult))
                own(dve.tensor_tensor(qrt[64:96, :, :], qrt[64:96, :, :], heads(sin), ALU.mult))
                dve.tensor_tensor(ql, ql, qrt[64:96, :, :], ALU.add).then_inc(sem("roped"), 1)
                dve.wait_ge(sem("rel_mm"), before("rel_mm", l) + 1)
                dve.tensor_copy(BT.rearrange("p h d c -> p (h d c)").rearrange("p (b n) -> p b n", b=3), ps[:, 0:3, :])\
                    .then_inc(sem("rel_turned"), 1)
                if l == 0:
                    mod_row(3)
                dve.wait_ge(sem("proj_taken"), pj_base(l + 1))

                def row_max(i):
                    kind, h, t = L.units[i]
                    n_ = T if t >= 2 else CTX
                    dve.wait_ge(sem("attn_score"), before("attn_score", l) + i + 1)
                    if kind == "na" and t >= 2:
                        d0 = 2 - 2 * (t - 2)
                        loc = ps[:, i % 2, CTX:T]
                        dve.wait_ge(sem("rel_ready"), before("rel_ready", l) + 1)
                        own(dve.tensor_tensor(loc, loc, BT[:, h, d0:d0 + 4, :].rearrange("p d c -> p (d c)"), ALU.add))
                    dve.tensor_reduce(stat[:, 32 + i % 2:33 + i % 2], ps[:, i % 2, 0:n_], AX.X, ALU.max, negate=True)\
                        .then_inc(sem("attn_max"), 1)

                def normalise(i):
                    n_ = T if L.units[i][2] >= 2 else CTX
                    dve.wait_ge(sem("attn_exp"), before("attn_exp", l) + i + 1)
                    own(dve.reciprocal(stat[:, 36 + i % 2:37 + i % 2], stat[:, 34 + i % 2:35 + i % 2]))
                    dve.tensor_scalar(Pa[i % 2][:, 0:n_], Pa[i % 2][:, 0:n_], stat[:, 36 + i % 2:37 + i % 2], None, ALU.mult)\
                        .then_inc(sem("attn_p"), 1)

                def head(i):
                    kind, h, t = L.units[i]
                    p0 = 64 * (h % 2)
                    dve.wait_ge(sem("attn_v"), before("attn_v", l) + i + 1)
                    dve.tensor_copy(aT[kind][p0:p0 + 64, h // 2, t * P:(t + 1) * P], ps[p0:p0 + 64, 4 + i % 2, 0:P])\
                        .then_inc(sem("attn_o"), 1)

                nu = len(L.units)
                for i in range(nu + 3):
                    if i < nu:
                        row_max(i)
                    if 1 <= i <= nu:
                        normalise(i - 1)
                    if i >= 3:
                        head(i - 3)
                    if l == 0 and i in (nu // 3, 2 * nu // 3):
                        mod_row(4 + (i > nu // 3))
                for u in range(24):
                    jp, m, half = u // 6, (u // 2) % 3, u % 2
                    dst = merged[:, 2 * jp + half, tq]
                    dve.wait_ge(sem("mg_sig"), before("mg_sig", l) + u + 1)
                    dve.wait_ge(sem("mg_branch"), before("mg_branch", l) + u + 1)
                    if m == 0:
                        dve.tensor_tensor(dst, sg_m[u % 3][:, tq], ps[:, 3 + u % 3, tq], ALU.mult).then_inc(sem("mg_used"), 1)
                    else:
                        dve.tensor_tensor(tmp_m[:, tq], sg_m[u % 3][:, tq], ps[:, 3 + u % 3, tq], ALU.mult)\
                            .then_inc(sem("mg_used"), 1)
                        dve.wait_ge(sem("mg_used"), before("mg_used", l) + u + 1)
                        ins = dve.tensor_tensor(dst, dst, tmp_m[:, tq], ALU.add)
                        if m == 2:
                            ins.then_inc(sem("merged"), 1)
                            dve.wait_ge(sem("merged"), before("merged", l) + 2 * jp + half + 1)
                        else:
                            own(ins)

                def post(which, Y, G, tmp):
                    for j, t in enumerate(L.chunks):
                        s = t // 2
                        if t % 2 == 0:
                            dve.wait_ge(sem(f"g{which}_taken"), before(f"g{which}_taken", l) + 2 * L.streams.index(s) + 2)
                        dve.wait_ge(sem(f"post{which}_rstd"), before(f"post{which}_rstd", l) + j + 1)
                        own(dve.scalar_tensor_tensor(out=tmp, in0=Y[:, t, :], scalar=stat[:, 40 + t:41 + t], in1=G[:, s, :],
                                                     op0=ALU.mult, op1=ALU.mult))
                        dve.tensor_tensor(X[:, t, :], X[:, t, :], tmp, ALU.add).then_inc(sem(f"x_post{which}"), 1)
                        dve.wait_ge(sem(f"x_post{which}"), before(f"x_post{which}", l) + j + 1)

                post(1, Ym, G1, tmp1)
                norm(l, 2, L.chunks, xn2, h2T)
                ns = L.ns
                R = N_EXP * ns
                lgp = ps[:, 0, 0:2 * R].rearrange("p (a e) -> p a e", e=N_EXP)
                lgs, af = lg[:, 0:2 * ns, :], aff[:, 0:2 * ns, :]

                def per_token(at):
                    return stat[:, at:at + 2 * ns].rearrange("p (a e) -> p a e", e=1).to_broadcast([P, 2 * ns, N_EXP])

                dve.wait_ge(sem("logits"), before("logits", l) + 1)
                own(dve.tensor_reduce(stat[:, 52:52 + 2 * ns], lgp, AX.X, ALU.max, negate=True))
                dve.tensor_tensor(lgs, lgp, per_token(52), ALU.add).then_inc(sem("lg_shift"), 1)
                dve.wait_ge(sem("lg_exp"), before("lg_exp", l) + 1)
                own(dve.tensor_reduce(stat[:, 56:56 + 2 * ns], lgs, AX.X, ALU.add))
                own(dve.reciprocal(stat[:, 60:60 + 2 * ns], stat[:, 56:56 + 2 * ns]))
                dve.tensor_tensor(af, lgs, per_token(60), ALU.mult).then_inc(sem("aff_ready"), 1)
                dve.wait_ge(sem("affT_tr"), before("affT_tr", l) + 1)
                own(dve.tensor_copy(wk[0][0:R, :], ps[0:R, 1, 0:SEQ]))
                for r in range(CAP // 8):
                    own(dve.max(top8[0:R, :], wk[r % 2][0:R, :]))
                    own(dve.match_replace(wk[(r + 1) % 2][0:R, :], top8[0:R, :], wk[r % 2][0:R, :], -1.0))
                own(dve.tensor_scalar(msk[0:R, :], wk[0][0:R, :], 0.0, None, ALU.is_lt))
                own(dve.tensor_tensor_scan(out=affT[0:R, :], data0=ones[0:R, 0:1].to_broadcast([R, SEQ]), data1=msk[0:R, :],
                                           initial=0.0, op0=ALU.mult, op1=ALU.add))
                own(dve.tensor_tensor(csum[0:R, :], affT[0:R, :], msk[0:R, :], ALU.mult))
                dve.tensor_scalar(csum[0:R, :], csum[0:R, :], -1.0, None, ALU.add).then_inc(sem("rank_ready"), 1)
                dve.wait_ge(sem("rank_tr"), before("rank_tr", l) + 1)
                own(dve.tensor_copy(pmT[:, :, 0:R], ps[:, 2, 0:64].rearrange("p (c r) -> p c r", c=2)[:, :, 0:R]))
                io = iota[:, :].rearrange("p (a j) -> p a j", a=1).to_broadcast([P, N_EXP, CAP])
                for si in range(ns):
                    for c2 in range(2):
                        s_ = Ssel[:, si, c2, :].rearrange("p (e j) -> p e j", e=N_EXP)
                        pm = pmT[:, c2, si * N_EXP:(si + 1) * N_EXP].rearrange("p (e j) -> p e j", j=1)
                        own(dve.tensor_tensor(s_, io, pm.to_broadcast([P, N_EXP, CAP]), ALU.is_equal))
                        g_ = aff[:, c2 * ns + si, :].rearrange("p (e j) -> p e j", j=1)
                        own(dve.tensor_tensor(Sg[:, si, c2, :].rearrange("p (e j) -> p e j", e=N_EXP), s_,
                                              g_.to_broadcast([P, N_EXP, CAP]), ALU.mult))
                dve.nop().then_inc(sem("routed"), 1)
                dve.memset(Ya[:, :, :], 0.0).then_inc(sem("ya_added"), 1)
                M, NT, NW = L.M, L.NT, L.NW
                NB_ = 4 * ns
                with dve.Fori(0, LOOPS) as i:
                    so = ns - 1
                    for k in range(KD):
                        if k % 4 == 0:
                            dve.wait_ge(sem("gathered"), before("gathered", l) + i * (2 * ns) + (2 * so + k // 4 + 1))
                        ins = dve.tensor_scalar(XST[:, k, :, so * CAP:(so + 1) * CAP],
                                                ps[:, 2 * so + k // 4, (k % 4) * P:(k % 4 + 1) * P].rearrange("p (e j) -> p e j", e=GROUP),
                                                mod_col(l, SC2, k, 1), mod_col(l, SH2, k, 1), ALU.mult, ALU.add)
                    ins.then_inc(sem("xs_lat"), 1)
                    for e in range(GROUP):
                        dve.wait_ge(sem("silu"), before("silu", l) + i * GROUP + (e + 1))
                        dve.wait_ge(used, i * LOOP_LOADS + (LOOP_BASE[l] + e * EXP_LOADS + 8))
                        dve.tensor_tensor(hid[:, 0:NW], sgh[:, 0:NW], ps[:, 2 * (e % 2) + 1, 0:NW], ALU.mult)\
                            .then_inc(sem("hid_ready"), 1)
                        dve.wait_ge(used, i * LOOP_LOADS + (LOOP_BASE[l] + (e + 1) * EXP_LOADS))
                        for j in range(4):
                            si, at = y_piece(L, j)
                            ins = dve.tensor_copy(Yg[e * CAP:(e + 1) * CAP, si, at:at + NW],
                                                  ps[j * CAP:(j + 1) * CAP, 6 + e % 2, 0:NW])
                        ins.then_inc(sem("y_taken"), 1)
                    for o in range(NB_):
                        si, c2, half = o // 4, (o // 2) % 2, o % 2
                        y = Ya[:, 2 * L.streams[si] + c2, half * 512:(half + 1) * 512]
                        dve.wait_ge(sem("scattered"), before("scattered", l) + i * NB_ + (o + 1))
                        dve.tensor_tensor(y, y, ps[:, o % 4, :], ALU.add).then_inc(sem("ya_added"), 1)
                dve.wait_ge(sem("ya_added"), before("ya_added", l) + NB_ * LOOPS + 1)
                post(2, Ya, G2, tmp2)
                if l == 0:
                    dve.wait_ge(sem("x_post2"), 4)


def uses(n):
    return USES[n]


def _uses():
    counts = [0] * SLOTS
    out = {}
    n = 0
    for l in range(2):
        for kind, *_ in weight_loads(l):
            if kind != "br":
                counts[n % SLOTS] += 1
            out[n] = counts[n % SLOTS]
            n += 1
        for _ in range(LOOPS * LOOP_LOADS):
            counts[n % SLOTS] += 1
            out[n] = counts[n % SLOTS]
            n += 1
    return out


USES = _uses()


def mod_load(o):
    l, g = MOD_GROUPS[o]
    return weight_loads(0).index(("mod", l, g, 0))


def krw_load(l):
    return weight_loads(l).index(("in", l, C_CKV, C_NQ - C_CKV))


PROJECTIONS = 2 + 2 + 8 + 2 + 4 + 2 + 1 + 1 + 1 + 2 + 2 + 4 + 2 + 3 * HEADS + 4


def pj_base(l):
    return l * PROJECTIONS


def keys_of(t, d):
    if t < 2:
        return [s for s in range(2) if (s <= t if d == 0 else s >= t)]
    return [0, 1] + [s for s in (2, 3) if (s <= t if d == 0 else s >= t)]


def span(L, d, s):
    if L.n and s < 2:
        return 2, 4, 2 * P if d else P
    if d == 0:
        return s, 4, 0
    if s < 2:
        return 0, 4, P - s * P
    return 2, s + 1, P if s == 2 else 0


def y_piece(L, j):
    return (j % 2, (j // 2) * L.NW) if L.ns == 2 else (0, j * L.NW)


_INS = ['x', 'c', 'ctx', 'c_ctx', 'w_mod', 'b_mod', 'g_pre1', 'g_post1', 'g_pre2', 'g_post2', 'w_in', 'g_q', 'g_kv',
        'w_uq', 'w_ukv', 'rpb', 'b_ml_gates', 'g_ml', 'w_br_mla', 'w_br_na', 'w_br_ml', 'w_out',
        'w_router', 'w_e1', 'w_e3', 'w_e2']


def kernel(**inputs):
    import numpy as _np
    import concourse.bacc as _bacc
    from concourse import mybir as _mybir
    from concourse.bass_utils import run_bass_kernel_spmd as _run

    nc = _bacc.Bacc("TRN2", target_bir_lowering=False, num_devices=1)
    arrays, args = {}, []
    for name in _INS:
        a = _np.ascontiguousarray(inputs[name])
        arrays[f"in_{name}_dram"] = a
        args.append(nc.dram_tensor(f"in_{name}_dram", a.shape, _mybir.dt.from_np(a.dtype), kind="ExternalInput").ap())
    a = rope_table()
    arrays["rope_dram"] = a
    args.append(nc.dram_tensor("rope_dram", a.shape, _mybir.dt.from_np(a.dtype), kind="ExternalInput").ap())
    args.append(nc.dram_tensor("out_0_dram", (1, SEQ, D), _mybir.dt.from_np(_np.dtype("float32")), kind="ExternalOutput").ap())
    backbone(nc, *args)
    r = _run(nc, [arrays], core_ids=[0])
    return r.results[0]["out_0_dram"]
```

```python
from contextlib import ExitStack

import numpy as np

import concourse.bass as bass
from concourse import mybir

F32 = mybir.dt.float32
ALU = mybir.AluOpType
ACT = mybir.ActivationFunctionType
AX = mybir.AxisListType

P = 128
D = 1024
KD = D // P
CTX = 256
SEQ = 256
T = CTX + SEQ
EPS = 1e-6
NEG = -1e30
GRID_W = 64
HEADS = 4
Q_RANK = 256
NOPE = 64
ROPE = 32
QK = NOPE + ROPE
NA_KR, NA_KC = 8, 16
RPB_R, RPB_C = 2 * NA_KR - 1, 2 * NA_KC - 1
ML_V = 128
N_EXP = 16
CAP = 32
GROUP = P // CAP
SLOTS = 8
SLOT = 2048
BLK = SLOT // KD

C_CQ, C_CKV, C_NQ, C_NK, C_NV = 0, 256, 416, 672, 928
C_MQ, C_MK, C_MV, C_MO, C_MG, C_BG = 1184, 1440, 1696, 2208, 2720, 2736


MOD_GROUPS = [(l, g) for l in range(2) for g in range(3)]
MERGE_STEPS = 3 * KD // 2


def rope_table():
    t = np.arange(SEQ)
    pos = np.stack([t // GRID_W, t % GRID_W], 0).astype(np.float32)
    nf = ROPE // 4
    inv = (np.float32(10000.0) ** (-np.arange(nf, dtype=np.float32) / np.float32(nf))).astype(np.float32)
    ang = (pos[:, None, :] * inv[None, :, None]).astype(np.float32)
    cos = np.repeat(np.cos(ang)[:, None], 2, 1).reshape(ROPE, SEQ)
    sin = np.stack([-np.sin(ang), np.sin(ang)], 1).reshape(ROPE, SEQ)
    return np.stack([cos, sin], 1).astype(np.float32)


class Layer:

    def __init__(self, n):
        self.n = n
        self.streams = [0, 1] if n == 0 else [1]
        self.chunks = [2 * s + c for s in self.streams for c in range(2)]
        self.t0 = self.chunks[0] * P
        self.tq = slice(self.t0, T)
        self.nt = len(self.chunks)
        self.ns = len(self.streams)
        self.units = [(kind, h, t) for kind in ("mla", "na") for h in range(HEADS) for t in self.chunks]
        self.pairs = [(h, d) for h in range(HEADS) for d in range(2)]
        self.M = CAP * self.ns
        self.NT = P // self.M
        self.NW = D // self.NT


UNITS0, PAIRS0 = 32, 8
LAYER0 = dict(
    params_mg=16, params=32, wgp_ready=1, wuqr_ready=1, v_ones=1, rel_loaded=16 * 2 * HEADS, rel_mm=1, rel_turned=1, rel_ready=1,
    n1_rstd=4, n1_xn=4, n1_tr=KD, n1_lat=KD, n1_ctx=KD, n2_rstd=4, n2_xn=4, n2_tr=KD, n2_lat=KD, n2_ctx=KD,
    abs_f=1, log1p=1, rows_ready=1, rows_tr=1, cols_ready=1, sc_ready=HEADS, nm_ready=PAIRS0, e1_ready=4 * PAIRS0,
    exp_done=4 * PAIRS0, p_ready=PAIRS0, num_ready=2 * PAIRS0, num_used=2 * PAIRS0, head_rstd=1, hn_ready=1,
    hm_tr=HEADS, mlstm_out=HEADS, krw_ready=1, sq_ready=1, lowrank_ready=1, roped=1,
    attn_score=UNITS0, attn_max=UNITS0, attn_exp=UNITS0, attn_p=UNITS0, attn_tr=UNITS0, attn_pt=UNITS0,
    attn_v=UNITS0, attn_o=UNITS0, mg_gate=18, mg_sig=24, mg_branch=24, mg_used=24, merged=KD,
    wo_ready=16, wo_taken=16, g1_ready=4, g1_taken=4, g2_ready=4, g2_taken=4, post1_rstd=4, post2_rstd=4,
    x_post1=4, x_post2=4, logits=1, lg_shift=1, lg_exp=1, aff_ready=1, affT_tr=1, rank_ready=1, rank_tr=1,
    routed=1, gathered=16, staged=4, gt_tr=4, gt_ready=4, xs_lat=4, xs_ctx=4, silu=N_EXP,
    hid_ready=N_EXP, hid_tr=N_EXP, hidT_ready=N_EXP, y_taken=N_EXP,
    scattered=32, ya_added=33,
)


def before(name, l):
    return LAYER0[name] * l


def mod_steps(step):
    n = 5 * KD
    return range(n * step // MERGE_STEPS, n * (step + 1) // MERGE_STEPS)


def mod_step(o):
    return next(s for s in range(MERGE_STEPS) if o * KD - 1 in mod_steps(s))


def weight_loads(layer):
    loads = [("mod", 0, 0, k) for k in range(KD)] if layer == 0 else []
    loads += [("in", layer, c, BLK) for c in (C_MQ, C_MK, C_MV, C_MV + BLK, C_NQ, C_NK, C_NV, C_MO, C_MO + BLK, C_CQ)]
    loads += [("in", layer, C_CKV, C_NQ - C_CKV)]
    loads += [("in", layer, C_BG + m * D, BLK) for m in range(3)]
    loads += [("branch", layer, jp) for jp in range(2)]
    for jp in range(KD // 2):
        for m in range(3):
            if jp:
                loads += [("in", layer, C_BG + m * D + jp * BLK, BLK)]
            if layer == 0:
                loads += [("mod", *MOD_GROUPS[1 + n // KD], n % KD) for n in mod_steps(3 * jp + m)]
        if 1 <= jp < KD // 2 - 1:
            loads += [("branch", layer, jp + 1)]
    return loads + [("out", layer, nb) for nb in range(D // BLK)]


def ring_loads(layer):
    return [w for w in weight_loads(layer) if w[0] != "branch"]


PJ = ["gate_row0", "gate_row1", "mq0", "mq1", "mk0", "mk1", *(f"mv{h}{t}" for h in range(2) for t in range(4)),
      "nq0", "nq1", "nk0", "nk1", *(f"nv{t}" for t in range(4)), *(f"mo{h}" for h in range(HEADS)),
      "cq0", "cq1", "ckv", "kr", "kr_pair", "cq_sum", "ckv_sum",
      *(f"{n}{i}" for n in ("q", "q_pair", "k", "v") for i in range(4)), *(f"gate{f}" for f in range(6))]
PJ_BANK, PJ_BEFORE = [], []


def _pj_banks():
    turn = 0
    for name in 2 * PJ:
        if name[:2] in ("nq", "nk", "nv"):
            b = 7
        elif name[:4] == "gate" and name[4] != "_":
            b = 6 + int(name[4]) % 2
        else:
            b = turn % 4
            turn += 1
        same = [i for i, c in enumerate(PJ_BANK) if c == b]
        PJ_BEFORE.append(same[-1] if same else None)
        PJ_BANK.append(b)


_pj_banks()


def pj_index(l, name):
    return l * len(PJ) + PJ.index(name)


EXP_LOADS = 12
LOOP_LOADS = GROUP * EXP_LOADS
LOOPS = N_EXP // GROUP
BASE = []
_n = 0
for _l in range(2):
    BASE.append(_n)
    _n += len(ring_loads(_l)) + LOOPS * LOOP_LOADS
LOOP_BASE = [BASE[l] + len(ring_loads(l)) for l in range(2)]


def backbone(nc, x, c, ctx, c_ctx, w_mod, b_mod, g_pre1, g_post1, g_pre2, g_post2, w_in, g_q, g_kv, w_uq, w_ukv,
             rpb, b_ml_gates, g_ml, w_br_mla, w_br_na, w_br_ml, w_out, w_router, w_e1, w_e3, w_e2, rope, out):
    with ExitStack() as stack:
        def sb(name, *shape):
            return stack.enter_context(nc.sbuf_tensor(name, [P, *shape], F32))

        sems = {}

        def sem(name):
            if name not in sems:
                sems[name] = stack.enter_context(nc.semaphore(name))
            return sems[name]

        layers = [Layer(0), Layer(1)]

        X = sb("X", 4, D)
        ring = sb("ring", SLOTS, SLOT)
        gate_rows = sb("gate_rows", 4, 512)
        mod_tmp = sb("mod_tmp", 512)
        b_row = sb("b_row", 512)
        g_row = sb("g_row", 512)
        ident = sb("ident", P)
        ones = sb("ones", P)
        flip = sb("flip", P)
        mask_f = sb("mask_f", 512)
        mask_b = sb("mask_b", 640)
        rope_t = sb("rope_t", 2, SEQ)
        iota = sb("iota", CAP)
        wuq = sb("wuq", 2, HEADS * QK)
        wuqr = sb("wuqr", 2, HEADS, ROPE)
        wukv = sb("wukv", HEADS * P)
        wrt = sb("wrt", KD, N_EXP)
        mgw = sb("mgw", KD, 16)
        krw = sb("krw", KD, ROPE)
        vrow = sb("vrow", P)
        vcol = sb("vcol", 32)
        cT = sb("cT", KD, 32)
        modT = sb("modT", 2, 3, 4, 4, 2)
        bml = sb("bml", 2, 2)
        one_add = sb("one_add", 3)
        eps_t = sb("eps_t", 1)
        stat = sb("stat", 64)
        top8 = sb("top8", 8)
        ARENA = 23568
        arena = sb("arena", ARENA)

        def view(at, *dims):
            n = int(np.prod(dims))
            assert at + n <= ARENA, (at, dims)
            v = arena[:, at:at + n]
            if len(dims) == 1:
                return v
            names = "abcde"[:len(dims)]
            return v.rearrange(f"p ({' '.join(names)}) -> p {' '.join(names)}",
                               **{k: d for k, d in zip(names, dims)})

        hT = view(0, KD, T)
        mT = view(4096, HEADS, T)
        wgp = view(6144, KD, 2, 2, 32)
        aT = {"mla": view(6144, 2, T), "na": view(7168, 2, T)}
        mq = view(8192, 2, T)
        mk = view(9216, 2, T)
        sgo = view(8192, HEADS, T)
        mv1 = view(10240, 4, HEADS, ML_V + 1)
        hml = view(12304, 4, HEADS, ML_V)
        E = [view(14352 + 2048 * b, 4, T) for b in range(2)]
        rI, rF, rA, rS, rG = (view(18448 + 512 * b, T) for b in range(5))
        rM = rA
        R3 = view(21008, 3, T)
        gcol = view(22544, 4, 64)
        enm = view(22800, 4, 64)
        xn1 = view(12304, 4, D)
        junk1 = view(21056, D)
        cq = view(10240, 2, T)
        ckv = view(11264, T)
        sq = view(11776, 3, T)
        rs2 = view(13312, 2, T)
        qT = view(14336, HEADS, T)
        kT = view(16384, HEADS, T)
        vM = view(21520, 4, HEADS * 64)
        krt = view(9728, 2, SEQ)
        kr_a, kr_b = (krt[64:96, b, :] for b in range(2))
        qrt = view(12800, HEADS, SEQ)
        nq = view(18448, 2, T)
        nk = view(19472, 2, T)
        nv = view(20496, 4, HEADS * 64)
        early = [view(at, T) for at in (10240, 10752, 11264, 13824, 22544, 23056)]
        BT = view(8192, HEADS, 6, GRID_W)
        Pa = [view(11776 + 512 * b, T) for b in range(2)]
        PT = [view(12800 + 512 * b, T) for b in range(2)]
        branches = [view(14336 + SLOT * b, SLOT).rearrange("p (k n) -> p k n", k=KD) for b in range(2)]
        merged = view(8192, KD, T)
        sg_m = [view(12288 + 512 * b, T) for b in range(3)]
        tmp_m = view(20480, T)
        Ym = view(14336, 4, D)
        G1 = view(18432, 2, D)
        tmp1 = view(20480, D)
        junk_y = view(21504, D)
        xn2 = view(0, 4, D)
        G2 = view(18944, 2, D)
        Ssel = view(4096, 2, 2, 512)
        Sg = view(6144, 2, 2, 512)
        h2T = view(8192, KD, T)
        XST = view(8192, KD, GROUP, 64)
        stg = view(10240, 2, 2, P)
        GT = view(10752, 2, SEQ)
        Yg = view(11264, 2, D)
        Ya = view(13312, 4, D)
        sgh = view(17408, 512)
        hid = view(17920, 512)
        hidT = view(18432, 512)
        tmp2 = view(9216, D)
        junk2 = view(8192, D)
        aff = view(20992, 4, N_EXP)
        lg = view(21056, 4, N_EXP)
        affT = view(21120, SEQ)
        wk = [view(21376 + 256 * b, SEQ) for b in range(2)]
        msk = view(21888, SEQ)
        csum = view(22144, SEQ)
        pmT = view(22400, 2, 32)

        ps = stack.enter_context(nc.psum_tensor("ps", [P, 8, 512], F32))
        COL_C, COL_GQ, COL_GKV, COL_GML = 0, 16, 20, 22

        def mod_col(l, vec, k, s):
            return modT[:, l, vec // 2, k % 4, 2 * (vec % 2) + k // 4, s:s + 1]

        SH1, SC1, GT1, SH2, SC2, GT2 = range(6)

        def w_slot(n):
            return ring[:, n % SLOTS, :]

        landed = [sem(f"weights_landed_{i}") for i in range(SLOTS)]
        used = sem("weights_used")
        small = sem("small_loaded")
        N_SMALL = 13

        block = stack.enter_context(nc.Block())

        @block.sync
        def _(sp):
            sp.dma_start(vrow[0:8, :], c.rearrange("a (k p) -> (a k) p", p=P)).then_inc(small, 16)
            sp.dma_start(vrow[8:16, :], c_ctx.rearrange("(k p) -> k p", p=P)).then_inc(small, 16)
            sp.dma_start(vrow[16:20, :], g_q.rearrange("l (k p) -> (l k) p", p=P)).then_inc(small, 16)
            sp.dma_start(vrow[20:22, :], g_kv).then_inc(small, 16)
            sp.dma_start(vrow[22:30, :], g_ml.rearrange("l (k p) -> (l k) p", p=P)).then_inc(small, 16)
            sp.dma_start(rope_t[64:96, :, :], rope).then_inc(small, 16)
            for s, src in ((1, x), (0, ctx)):
                sp.dma_start(X[:, 2 * s:2 * s + 2, :], src.rearrange("a (c p) d -> p (a c) d", p=P)).then_inc(sem("x_loaded"), 16)

            def load(n, dst, src):
                if n >= SLOTS:
                    sp.wait_ge(used, n - SLOTS + 1)
                sp.dma_start(dst, src).then_inc(landed[n % SLOTS], 16)

            for l in range(2):
                n = BASE[l]
                for kind, lw, *a in weight_loads(l):
                    if kind == "branch":
                        jp = a[0]
                        if jp < 2:
                            sp.wait_ge(sem("attn_score"), before("attn_score", l) + len(layers[l].units) // 2 + 1)
                        else:
                            sp.wait_ge(sem("mg_branch"), before("mg_branch", l) + 6 * (jp - 1))
                        cols = slice(jp * BLK, (jp + 1) * BLK)
                        for k0, w in ((0, w_br_mla), (2, w_br_na), (4, w_br_ml)):
                            k1 = k0 + w.shape[1] // P
                            sp.dma_start(branches[jp % 2][:, k0:k1, :], w[lw, :, cols].rearrange("(k p) n -> p k n", p=P))\
                              .then_inc(sem(f"branch_landed_{jp % 2}"), 16)
                        continue
                    if kind == "mod":
                        load(n, w_slot(n), w_mod[lw, a[1] * P:(a[1] + 1) * P, a[0] * SLOT:(a[0] + 1) * SLOT])
                    elif kind == "in":
                        load(n, w_slot(n)[:, 0:KD * a[1]].rearrange("p (k n) -> p k n", k=KD),
                             w_in[lw, :, a[0]:a[0] + a[1]].rearrange("(k p) n -> p k n", p=P))
                    else:
                        load(n, w_slot(n).rearrange("p (k n) -> p k n", k=KD),
                             w_out[lw, :, a[0] * BLK:(a[0] + 1) * BLK].rearrange("(k p) n -> p k n", p=P))
                    n += 1
                with sp.Fori(0, LOOPS) as i:
                    for e in range(GROUP):
                        for m, w in enumerate((w_e1, w_e3, w_e2)):
                            we = w[l].rearrange("(i e) (q k p) n -> i e q p k n", e=GROUP, q=4, p=P)
                            for q in range(4):
                                n = LOOP_BASE[l] + e * EXP_LOADS + m * 4 + q
                                sp.wait_ge(used, i * LOOP_LOADS + (n - SLOTS + 1))
                                sp.dma_start(w_slot(n).rearrange("p (k n) -> p k n", k=2),
                                             we[bass.ds(i, 1), e, q].rearrange("i p k n -> p (i k) n"))\
                                  .then_inc(landed[n % SLOTS], 16)
            for s in range(2):
                sp.wait_ge(sem("x_post2"), before("x_post2", 1) + s + 1)
                sp.dma_start(out[0, s * P:(s + 1) * P, :], X[:, 2 + s, :]).then_inc(sem("out_stored"), 16)
            sp.wait_ge(sem("out_stored"), 32)

        @block.gpsimd
        def _(pool):
            done = [0]

            def own(ins):
                done[0] += 1
                ins.then_inc(sem("pool_own"), 1)
                pool.wait_ge(sem("pool_own"), done[0])

            own(pool.memset(ident[:, :], 0.0))
            pool.affine_select(out=ident[:, :], in_=ident[:, :], compare_op=ALU.not_equal, fill=1.0, base=0,
                               pattern=[[-1, P]], channel_multiplier=1).then_inc(sem("ident_ready"), 1)
            own(pool.memset(flip[:, :], 0.0))
            for r in range(2):
                v = flip[64 * r:64 * r + 64, :]
                own(pool.affine_select(out=v, in_=v, compare_op=ALU.not_equal, fill=1.0, base=-(64 * r + 63),
                                       pattern=[[1, P]], channel_multiplier=1))
            pool.memset(ones[:, :], 1.0)
            pool.memset(eps_t[:, :], EPS)
            own(pool.memset(one_add[:, :], 0.0))
            own(pool.memset(one_add[64:128, 0:1], 1.0))
            own(pool.memset(one_add[0:64, 2:3], 1.0))
            pool.memset(b_row[:, :], 0.0)
            pool.memset(g_row[:, :], 1.0)
            pool.memset(cT[:, :, :], 0.0)
            pool.memset(bml[:, :, :], 0.0)
            pool.memset(mask_f[:, :], 0.0)
            own(pool.memset(mask_b[:, :], 0.0))
            pool.affine_select(out=mask_f[:, 0:P], in_=mask_f[:, 0:P], compare_op=ALU.is_ge, fill=NEG, base=0,
                               pattern=[[1, P]], channel_multiplier=-1)
            pool.affine_select(out=mask_b[:, P:2 * P], in_=mask_b[:, P:2 * P], compare_op=ALU.is_ge, fill=NEG, base=0,
                               pattern=[[-1, P]], channel_multiplier=1)
            own(pool.iota(iota[:, :], pattern=[[1, CAP]], base=0, channel_multiplier=0,
                          allow_small_or_imprecise_dtypes=True))
            pool.nop().then_inc(sem("consts_ready"), 1)
            for d in range(2):
                for l in range(2):
                    pool.dma_start(bml[32 * d:32 * d + 4, l, :],
                                   b_ml_gates[l].rearrange("(d f h) -> d h f", d=2, f=2)[d],
                                   allow_slow_non_contiguous=True).then_inc(sem("bml_loaded"), 16)

            rows_loaded = [0]

            def mod_rows(o):
                l, g = MOD_GROUPS[o]
                if o:
                    pool.wait_ge(sem("mod_row"), o)
                gains = {0: (None, g_pre1), 1: (g_post1, None), 2: (g_pre2, g_post2)}[g]
                for half, src in enumerate(gains):
                    if src is None:
                        own(pool.memset(g_row[64 * half:64 * half + 64, :], 1.0))
                for r in range(2):
                    pool.dma_start(b_row[r:r + 97:32, :],
                                   b_mod[l, g * 2048:(g + 1) * 2048].rearrange("(j n) -> j n", j=4))\
                        .then_inc(sem("mod_rows_loaded"), 16)
                    rows_loaded[0] += 16
                    for half, src in enumerate(gains):
                        if src is not None:
                            p0 = 64 * half + r
                            pool.dma_start(g_row[p0:p0 + 33:32, :], src[l].rearrange("(j n) -> j n", j=2))\
                                .then_inc(sem("mod_rows_loaded"), 16)
                            rows_loaded[0] += 16
                pool.wait_ge(sem("mod_rows_loaded"), rows_loaded[0])
                pool.nop().then_inc(sem("mod_rows_ready"), 1)

            def params(l):
                if l:
                    pool.wait_ge(sem("attn_score"), 1)
                pool.dma_start(mgw[:, :, :], w_in[l, :, C_MG:C_BG].rearrange("(k p) n -> p k n", p=P))\
                    .then_inc(sem("params_mg"), 16)
                pool.dma_start(wuq[:, :, :], w_uq[l].rearrange("(k p) h e -> p k (h e)", p=P))\
                    .then_inc(sem("params"), 16)
                pool.dma_start(wukv[:, :], w_ukv[l].rearrange("p h e -> p (h e)")).then_inc(sem("params"), 16)

            def gates_weights(l):
                if l:
                    pool.wait_ge(sem("x_post2"), 4)
                pool.wait_ge(sem("params_mg"), before("params_mg", l) + 16)
                own(pool.memset(wgp[:, :, :, :, :], 0.0))
                for d in range(2):
                    for f in range(2):
                        at = (2 * d + f) * HEADS
                        own(pool.tensor_copy(wgp[:, :, f, d, 0:HEADS], mgw[:, :, at:at + HEADS]))
                pool.nop().then_inc(sem("wgp_ready"), 1)
                pool.wait_ge(sem("params"), before("params", l) + 32)
                for k in range(2):
                    q = wuq[:, k, :].rearrange("p (h e) -> p h e", h=HEADS)[:, :, NOPE:QK]\
                        .rearrange("p h (a b i) -> p h a b i", a=2, b=2)
                    r = wuqr[:, k, :, :].rearrange("p h (a b i) -> p h a b i", a=2, b=2)
                    for b in range(2):
                        own(pool.tensor_copy(r[:, :, :, b, :], q[:, :, :, 1 - b, :]))
                pool.nop().then_inc(sem("wuqr_ready"), 1)

            def v_ones(l):
                pool.wait_ge(sem("n1_tr"), before("n1_tr", l) + KD)
                pool.memset(mv1[:, :, :, ML_V:ML_V + 1], 1.0).then_inc(sem("v_ones"), 1)
                pool.wait_ge(sem("v_ones"), before("v_ones", l) + 1)

            def rel_bias(l):
                pool.wait_ge(sem("mlstm_out"), before("mlstm_out", l) + HEADS)
                for r in range(2):
                    for h in range(HEADS):
                        at = ((l * HEADS + h) * RPB_R + NA_KR - 1 - 2 - r) * RPB_C + NA_KC - GRID_W
                        src = bass.AP(rpb.tensor, at, [[1, GRID_W], [RPB_C, 6], [1, GRID_W]])
                        pool.dma_start(BT[64 * r:64 * r + 64, h, :, :], src).then_inc(sem("rel_loaded"), 16)
                pool.wait_ge(sem("rel_turned"), before("rel_turned", l) + 1)
                half = NA_KC // 2
                for r in range(2):
                    v = BT[64 * r:64 * r + 64].rearrange("p h d c -> p (h d) c")
                    a, b = v[:, :, 0:GRID_W - NA_KC], v[:, :, NA_KC:GRID_W]
                    own(pool.affine_select(out=a, in_=a, compare_op=ALU.is_ge, fill=NEG, base=half,
                                           pattern=[[0, 24], [1, GRID_W - NA_KC]], channel_multiplier=-1))
                    own(pool.affine_select(out=b, in_=b, compare_op=ALU.is_ge, fill=NEG, base=half - 1 - NA_KC,
                                           pattern=[[0, 24], [-1, GRID_W - NA_KC]], channel_multiplier=1))
                pool.nop().then_inc(sem("rel_ready"), 1)

            mod_rows(0)
            params(0)
            gates_weights(0)
            v_ones(0)
            mod_rows(1)
            pool.dma_start(wrt[:, :, :], w_router[0].rearrange("(k p) n -> p k n", p=P)).then_inc(sem("router_loaded"), 16)
            rel_bias(0)
            for o in range(2, 6):
                mod_rows(o)
            params(1)
            for l, L in enumerate(layers):
                pool.wait_ge(sem("routed"), before("routed", l) + 1)
                if l == 0:
                    pool.wait_ge(sem("logits"), 1)
                    pool.dma_start(wrt[:, :, :], w_router[1].rearrange("(k p) n -> p k n", p=P))\
                        .then_inc(sem("router_loaded"), 16)
                for si in range(L.ns):
                    for c2 in range(2):
                        g_ = aff[:, c2 * L.ns + si, :].rearrange("p (e j) -> p e j", j=1).to_broadcast([P, N_EXP, CAP])
                        own(pool.tensor_tensor(Sg[:, si, c2, :].rearrange("p (e j) -> p e j", e=N_EXP),
                                               Ssel[:, si, c2, :].rearrange("p (e j) -> p e j", e=N_EXP), g_, ALU.mult))
                with pool.Fori(0, LOOPS) as i:
                    pool.wait_ge(sem("gathered"), before("gathered", l) + i * (2 * L.ns) + 1)
                    for si in range(L.ns):
                        for c2 in range(2):
                            ins = pool.tensor_copy(stg[:, si, c2, :], Sg[:, si, c2, bass.ds(i * P, P)])
                    ins.then_inc(sem("staged"), 1)
                if l == 0:
                    gates_weights(1)
                    v_ones(1)
                    rel_bias(1)

        @block.tensor
        def _(pe):
            taken = [0]

            def next_slot(extra=None):
                n = taken[0]
                taken[0] += 1
                pe.wait_ge(landed[n % SLOTS], 16 * uses(n))
                return w_slot(n)

            def transpose(o, i, n):
                return pe.transpose(o, i, ident[0:n, 0:n])

            def mod_product(o, k):
                w = next_slot()
                for j in range(4):
                    mm = pe.matmul(ps[32 * j:32 * j + 32, 6, :], cT[:, k, :], w[:, 512 * j:512 * j + 512],
                                   start=k == 0, stop=k == KD - 1, skip_group_check=True)
                mm.then_inc(used, 1)

            def merge_mods(step):
                for n in mod_steps(step):
                    o, k = 1 + n // KD, n % KD
                    if k == 0:
                        pe.wait_ge(sem("mod_row"), o)
                    mod_product(o, k)
                for o in range(1, 6):
                    if mod_step(o) == step - 1:
                        mod_turn(o)

            def mod_turn(o):
                l, g = MOD_GROUPS[o]
                src = mod_tmp[:, :] if g == 0 else gate_rows[:, 2 * l + g - 1, :]
                pe.wait_ge(sem("mod_row"), o + 1)
                if o:
                    pe.wait_ge(sem("mod_col"), o)
                for b in range(4):
                    mm = transpose(ps[:, 7, 128 * b:128 * b + 128], src[:, 128 * b:128 * b + 128], P)
                mm.then_inc(sem("mod_tr"), 1)

            def norm_turn(l, which, src, chunks):
                n = f"n{which}"
                pe.wait_ge(sem(f"{n}_xn"), before(f"{n}_xn", l) + len(chunks))
                for k in range(KD):
                    if k >= 2:
                        pe.wait_ge(sem(f"{n}_lat"), before(f"{n}_lat", l) + k - 1)
                        if 0 in chunks:
                            pe.wait_ge(sem(f"{n}_ctx"), before(f"{n}_ctx", l) + k - 1)
                    for t in chunks:
                        mm = transpose(ps[:, 2 * (t // 2) + k % 2, (t % 2) * P:(t % 2 + 1) * P], src[:, t, k * P:(k + 1) * P], P)
                    mm.then_inc(sem(f"{n}_tr"), 1)
                pe.wait_ge(sem(f"{n}_lat"), before(f"{n}_lat", l) + KD)
                if 0 in chunks:
                    pe.wait_ge(sem(f"{n}_ctx"), before(f"{n}_ctx", l) + KD)

            pj = [0]

            def project(l, name, o, pairs, release=False):
                i = pj_index(l, name)
                assert i == pj[0]
                pj[0] += 1
                if PJ_BEFORE[i] is not None:
                    pe.wait_ge(sem("proj_taken"), PJ_BEFORE[i] + 1)
                for k, (a, b) in enumerate(pairs):
                    mm = pe.matmul(o(ps[:, PJ_BANK[i], :]), a, b, start=k == 0, stop=k == len(pairs) - 1)
                mm.then_inc(sem("proj_ready"), 1)
                if release:
                    pe.wait_ge(sem("proj_ready"), i + 1)
                    pe.nop().then_inc(used, 1)

            def blk(w, n=BLK):
                return w[:, 0:KD * n].rearrange("p (k n) -> p k n", k=KD)

            def feature_major(l, name, w, j, tok, release):
                project(l, name, lambda b: b[:, tok],
                        [(w[:, k, j * P:(j + 1) * P], hT[:, k, tok]) for k in range(KD)], release)

            def token_major(l, name, w, t):
                project(l, name, lambda b: b[:, 0:BLK],
                        [(hT[:, k, t * P:(t + 1) * P], w[:, k, :]) for k in range(KD)], t == 3)

            for l, L in enumerate(layers):
                tq = L.tq
                if l == 0:
                    pe.wait_ge(sem("ident_ready"), 1)
                    pe.wait_ge(sem("vrow_ready"), 1)
                    transpose(ps[:, 7, 0:30], vrow[0:30, :], 30).then_inc(sem("vrow_tr"), 1)
                    pe.wait_ge(sem("vcol_ready"), 1)
                    for k in range(KD):
                        mod_product(0, k)
                    mod_turn(0)
                norm_turn(l, 1, xn1, range(4))
                pe.wait_ge(sem("wgp_ready"), before("wgp_ready", l) + 1)
                for f in range(2):
                    project(l, f"gate_row{f}", lambda b: b[0:64, :],
                            [(wgp[:, k, f, :, :], hT[:, k, :]) for k in range(KD)])
                for name, tok in (("mq", tq), ("mk", slice(0, T))):
                    w = blk(next_slot())
                    for j in range(2):
                        feature_major(l, f"{name}{j}", w, j, tok, j == 1)
                pe.wait_ge(sem("rows_ready"), before("rows_ready", l) + 1)
                for r in range(2):
                    for t in range(4):
                        mm = transpose(ps[:, 4, 256 * r + 64 * t:256 * r + 64 * t + 64],
                                       R3[0:64, r, t * P:(t + 1) * P], 64)
                mm.then_inc(sem("rows_tr"), 1)
                for half in range(2):
                    w = blk(next_slot())
                    for t in range(4):
                        token_major(l, f"mv{half}{t}", w, t)
                pe.wait_ge(sem("cols_ready"), before("cols_ready", l) + 1)
                pe.wait_ge(sem("v_ones"), before("v_ones", l) + 1)
                pe.wait_ge(sem("proj_taken"), pj[0])

                def scores_ml(h):
                    if h:
                        pe.wait_ge(sem("p_ready"), before("p_ready", l) + 2 * h)
                    p0 = 64 * (h % 2)
                    for s in range(4):
                        o = ps[:, s, tq] if s < 2 else ps[:, 2, 256 * (s - 2):256 * (s - 2) + 256]
                        q0 = tq if s < 2 else slice(CTX, T)
                        mm = pe.matmul(o, mk[p0:p0 + 64, h // 2, s * P:(s + 1) * P], mq[p0:p0 + 64, h // 2, q0],
                                       start=True, stop=True)
                    mm.then_inc(sem("sc_ready"), 1)

                def spread_m(u):
                    h, d = L.pairs[u]
                    if u >= 2:
                        pe.wait_ge(sem("e1_ready"), before("e1_ready", l) + 4 * (u - 1))
                    r = 32 * d + h
                    pe.matmul(ps[:, 3 + d, tq], ident[0:64, r:r + 1].to_broadcast([64, P]), R3[0:64, 2, tq],
                              start=True, stop=True).then_inc(sem("nm_ready"), 1)

                def values_ml(u):
                    h, d = L.pairs[u]
                    for pi in range(L.nt // 2):
                        o = u * (L.nt // 2) + pi
                        if o >= 2:
                            pe.wait_ge(sem("num_used"), before("num_used", l) + o - 1)
                        for ti in range(2):
                            t = L.chunks[2 * pi + ti]
                            keys = keys_of(t, d)
                            for j, s in enumerate(keys):
                                mm = pe.matmul(ps[:, 5 + o % 2, ti * 129:ti * 129 + 129],
                                               E[u % 2][:, s, t * P:(t + 1) * P], mv1[:, s, h, :],
                                               start=j == 0, stop=j == len(keys) - 1)
                        mm.then_inc(sem("num_ready"), 1)

                na_w = [None]
                scores_ml(0)
                spread_m(0)
                spread_m(1)
                for u, (h, d) in enumerate(L.pairs):
                    if u < 5:
                        na_w[0] = blk(next_slot()) if u in (0, 2, 4) else na_w[0]
                    if u < 4:
                        feature_major(l, ("nq", "nk")[u // 2] + str(u % 2), na_w[0], u % 2, (tq, slice(0, T))[u // 2], u % 2 == 1)
                    else:
                        token_major(l, f"nv{u - 4}", na_w[0], u - 4)
                    pe.wait_ge(sem("p_ready"), before("p_ready", l) + u + 1)
                    if d == 1 and h + 1 < HEADS:
                        scores_ml(h + 1)
                    values_ml(u)
                    if u + 2 < len(L.pairs):
                        spread_m(u + 2)
                pe.wait_ge(sem("e1_ready"), before("e1_ready", l) + 4 * len(L.pairs))
                for half in range(2):
                    w = blk(next_slot())
                    for j in range(2):
                        feature_major(l, f"mo{2 * half + j}", w, j, tq, j == 1)
                pe.wait_ge(sem("hn_ready"), before("hn_ready", l) + 1)
                for h in range(HEADS):
                    if h >= 2:
                        pe.wait_ge(sem("mlstm_out"), before("mlstm_out", l) + h - 1)
                    for t in L.chunks:
                        mm = transpose(ps[:, 4 + h % 2, t * P:(t + 1) * P], hml[:, t, h, :], P)
                    mm.then_inc(sem("hm_tr"), 1)
                pe.wait_ge(sem("mlstm_out"), before("mlstm_out", l) + HEADS)
                w = blk(next_slot())
                for j in range(2):
                    feature_major(l, f"cq{j}", w, j, tq, j == 1)
                w = blk(next_slot(), C_NQ - C_CKV)
                feature_major(l, "ckv", w, 0, slice(0, T), False)
                project(l, "kr", lambda b: b[64:96, :], [(w[:, k, P:P + ROPE], hT[:, k, :]) for k in range(KD)])
                pe.wait_ge(sem("krw_ready"), before("krw_ready", l) + 1)
                project(l, "kr_pair", lambda b: b[64:96, 0:SEQ], [(krw[:, k, :], hT[:, k, CTX:T]) for k in range(KD)], True)
                pe.wait_ge(sem("sq_ready"), before("sq_ready", l) + 1)
                project(l, "cq_sum", lambda b: b[:, tq], [(ones[:, :], sq[:, k, tq]) for k in range(2)])
                project(l, "ckv_sum", lambda b: b[:, :], [(ones[:, :], sq[:, 2, :])])
                pe.wait_ge(sem("lowrank_ready"), before("lowrank_ready", l) + 1)
                pe.wait_ge(sem("wuqr_ready"), before("wuqr_ready", l) + 1)
                for h in range(HEADS):
                    project(l, f"q{h}", lambda b: b[0:QK, tq],
                            [(wuq[:, k, h * QK:(h + 1) * QK], cq[:, k, tq]) for k in range(2)])
                for h in range(HEADS):
                    project(l, f"q_pair{h}", lambda b: b[64:96, 0:SEQ], [(wuqr[:, k, h, :], cq[:, k, CTX:T]) for k in range(2)])
                for h in range(HEADS):
                    project(l, f"k{h}", lambda b: b[0:64, :], [(wukv[:, h * P:h * P + 64], ckv[:, :])])
                wv = wukv[:, :].rearrange("p (h e) -> p h e", h=HEADS)[:, :, 64:P]
                for t in range(4):
                    project(l, f"v{t}", lambda b: b[:, 0:256].rearrange("p (h e) -> p h e", h=HEADS),
                            [(ckv[:, t * P:(t + 1) * P], wv)])
                pe.wait_ge(sem("proj_taken"), pj[0])
                pe.wait_ge(sem("roped"), before("roped", l) + 1)
                pe.wait_ge(sem("rel_loaded"), before("rel_loaded", l) + 2 * HEADS * 16)
                bt = BT.rearrange("p h d c -> p (h d c)")
                for b in range(3):
                    mm = pe.matmul(ps[:, b, :], flip[:, :], bt[:, 512 * b:512 * b + 512], start=True, stop=True)
                mm.then_inc(sem("rel_mm"), 1)
                pe.wait_ge(sem("rel_turned"), before("rel_turned", l) + 1)

                def score(i):
                    kind, h, t = L.units[i]
                    nkey = T if t >= 2 else CTX
                    if i >= 2:
                        pe.wait_ge(sem("attn_exp"), before("attn_exp", l) + i - 1)
                    p0 = 64 * (h % 2)
                    if kind == "mla":
                        a, b = qT[0:QK, h, t * P:(t + 1) * P], kT[0:QK, h, 0:nkey]
                    else:
                        a, b = nq[p0:p0 + 64, h // 2, t * P:(t + 1) * P], nk[p0:p0 + 64, h // 2, 0:nkey]
                    pe.matmul(ps[:, i % 2, 0:nkey], a, b, start=True, stop=True).then_inc(sem("attn_score"), 1)

                def turn(i):
                    kind, h, t = L.units[i]
                    nk_ = 4 if t >= 2 else 2
                    pe.wait_ge(sem("attn_p"), before("attn_p", l) + i + 1)
                    if i >= 2:
                        pe.wait_ge(sem("attn_pt"), before("attn_pt", l) + i - 1)
                    for j in range(nk_):
                        mm = transpose(ps[:, 2 + i % 2, j * P:(j + 1) * P], Pa[i % 2][:, j * P:(j + 1) * P], P)
                    mm.then_inc(sem("attn_tr"), 1)

                def values(i):
                    kind, h, t = L.units[i]
                    nk_ = 4 if t >= 2 else 2
                    v = vM if kind == "mla" else nv
                    pe.wait_ge(sem("attn_pt"), before("attn_pt", l) + i + 1)
                    if i >= 2:
                        pe.wait_ge(sem("attn_o"), before("attn_o", l) + i - 1)
                    p0 = 64 * (h % 2)
                    for j in range(nk_):
                        mm = pe.matmul(ps[p0:p0 + 64, 4 + i % 2, 0:P], v[:, j, h * 64:(h + 1) * 64],
                                       PT[i % 2][:, j * P:(j + 1) * P], start=j == 0, stop=j == nk_ - 1)
                    mm.then_inc(sem("attn_v"), 1)

                def gate_products(n0, n1):
                    for n in range(n0, n1):
                        f, k = divmod(n, KD)
                        g = pj_index(l, f"gate{f}")
                        if n % (2 * KD) == 0:
                            gate_w[0] = blk(next_slot())
                        if k == 0:
                            assert g == pj[0]
                            pj[0] += 1
                            if PJ_BEFORE[g] is not None:
                                pe.wait_ge(sem("proj_taken"), PJ_BEFORE[g] + 1)
                        mm = pe.matmul(ps[:, PJ_BANK[g], tq], gate_w[0][:, k, (f % 2) * P:(f % 2 + 1) * P], hT[:, k, tq],
                                       start=k == 0, stop=k == KD - 1, skip_group_check=True)
                        if k == KD - 1:
                            mm.then_inc(sem("proj_ready"), 1)
                        if n % (2 * KD) == 2 * KD - 1:
                            pe.wait_ge(sem("proj_ready"), g + 1)
                            pe.nop().then_inc(used, 1)

                gate_w = [None]
                nu = len(L.units)
                for i in range(nu + 2):
                    if i < nu:
                        score(i)
                    if 1 <= i <= nu:
                        turn(i - 1)
                    if i < nu:
                        gate_products(6 * KD * i // nu, 6 * KD * (i + 1) // nu)
                    if i >= 2:
                        values(i - 2)
                pe.wait_ge(sem("attn_o"), before("attn_o", l) + nu)
                pe.wait_ge(sem("proj_taken"), pj[0])
                u = 0
                for jp in range(KD // 2):
                    wb = branches[jp % 2]
                    pe.wait_ge(sem(f"branch_landed_{jp % 2}"), 48 * (2 * l + jp // 2 + 1))
                    for m in range(3):
                        if jp:
                            wg = blk(next_slot())
                        for half in range(2):
                            if u >= 3:
                                pe.wait_ge(sem("mg_used"), before("mg_used", l) + u - 2)
                            cols = slice(half * P, (half + 1) * P)
                            if jp:
                                for k in range(KD):
                                    mm = pe.matmul(ps[:, u % 3, tq], wg[:, k, cols], hT[:, k, tq],
                                                   start=k == 0, stop=k == KD - 1)
                                mm.then_inc(sem("mg_gate"), 1)
                            k0, src = ((0, aT["mla"]), (2, aT["na"]), (4, mT))[m]
                            nk_ = 4 if m == 2 else 2
                            for k in range(nk_):
                                mm = pe.matmul(ps[:, 3 + u % 3, tq], wb[:, k0 + k, cols], src[:, k, tq],
                                               start=k == 0, stop=k == nk_ - 1)
                                if k == 0 and jp and half:
                                    mm.then_inc(used, 1)
                            mm.then_inc(sem("mg_branch"), 1)
                            u += 1
                        if l == 0:
                            merge_mods(3 * jp + m)

                def spread_gate(which):
                    row = gate_rows[:, 2 * l + which - 1, :]
                    for si, s in enumerate(L.streams):
                        for half in range(2):
                            g = si * 2 + half
                            if g >= 2:
                                pe.wait_ge(sem(f"g{which}_taken"), before(f"g{which}_taken", l) + g - 1)
                            r = 32 * ((2 if which == 2 else 0) + half) + s
                            pe.matmul(ps[:, 6 + half, :], ident[:, r:r + 1].to_broadcast([P, P]), row,
                                      start=True, stop=True).then_inc(sem(f"g{which}_ready"), 1)

                if l == 0:
                    mod_turn(5)
                    pe.wait_ge(sem("mod_col"), 6)
                spread_gate(1)
                pe.wait_ge(sem("merged"), before("merged", l) + KD)
                wo = [blk(next_slot()) for nb in range(D // BLK)]
                o = 0
                for t in L.chunks:
                    for nb in range(D // BLK):
                        if o >= 6:
                            pe.wait_ge(sem("wo_taken"), before("wo_taken", l) + o - 5)
                        for k in range(KD):
                            mm = pe.matmul(ps[:, o % 6, 0:BLK], merged[:, k, t * P:(t + 1) * P], wo[nb][:, k, :],
                                           start=k == 0, stop=k == KD - 1)
                        mm.then_inc(sem("wo_ready"), 1)
                        o += 1
                pe.wait_ge(sem("wo_ready"), before("wo_ready", l) + o)
                pe.nop().then_inc(used, D // BLK)
                pe.wait_ge(sem("wo_taken"), before("wo_taken", l) + o)
                norm_turn(l, 2, xn2, L.chunks)
                pe.wait_ge(sem("router_loaded"), 16 * (l + 1))
                for c2 in range(2):
                    for si, s in enumerate(L.streams):
                        t = 2 * s + c2
                        at = (c2 * L.ns + si) * N_EXP
                        for k in range(KD):
                            mm = pe.matmul(ps[:, 0, at:at + N_EXP], h2T[:, k, t * P:(t + 1) * P], wrt[:, k, :],
                                           start=k == 0, stop=k == KD - 1)
                mm.then_inc(sem("logits"), 1)
                R = N_EXP * L.ns
                pe.wait_ge(sem("aff_ready"), before("aff_ready", l) + 1)
                for c2 in range(2):
                    mm = transpose(ps[0:R, 1, c2 * P:(c2 + 1) * P],
                                   aff[:, c2 * L.ns:(c2 + 1) * L.ns, :].rearrange("p s e -> p (s e)"), P)
                mm.then_inc(sem("affT_tr"), 1)
                spread_gate(2)
                pe.wait_ge(sem("rank_ready"), before("rank_ready", l) + 1)
                for c2 in range(2):
                    mm = transpose(ps[:, 2, 32 * c2:32 * c2 + R], csum[0:R, c2 * P:(c2 + 1) * P], R)
                mm.then_inc(sem("rank_tr"), 1)
                pe.wait_ge(sem("g2_taken"), before("g2_taken", l) + 2 * L.ns)
                pe.wait_ge(sem("routed"), before("routed", l) + 1)
                M, NT, NW = L.M, L.NT, L.NW
                NB_ = 4 * L.ns
                with pe.Fori(0, LOOPS) as i:
                    pe.wait_ge(sem("ya_added"), before("ya_added", l) + i * NB_ + 1)
                    for si, s in enumerate(L.streams):
                        for k in range(KD):
                            for c2 in range(2):
                                mm = pe.matmul(ps[:, 2 * si + k // 4, (k % 4) * P:(k % 4 + 1) * P],
                                               xn2[:, 2 * s + c2, k * P:(k + 1) * P],
                                               Ssel[:, si, c2, bass.ds(i * P, P)], start=c2 == 0, stop=c2 == 1)
                            if k % 4 == 3:
                                mm.then_inc(sem("gathered"), 1)
                    pe.wait_ge(sem("staged"), before("staged", l) + i + 1)
                    for si in range(L.ns):
                        for c2 in range(2):
                            mm = transpose(ps[:, 4, (2 * si + c2) * P:(2 * si + c2 + 1) * P], stg[:, si, c2, :], P)
                    mm.then_inc(sem("gt_tr"), 1)
                    pe.wait_ge(sem("gt_ready"), before("gt_ready", l) + i + 1)
                    pe.wait_ge(sem("xs_lat"), before("xs_lat", l) + i + 1)
                    if L.ns == 2:
                        pe.wait_ge(sem("xs_ctx"), before("xs_ctx", l) + i + 1)

                    for e in range(GROUP):
                        def slot(j):
                            n = LOOP_BASE[l] + e * EXP_LOADS + j
                            pe.wait_ge(landed[n % SLOTS], i * (16 * LOOP_LOADS // SLOTS) + 16 * uses(n))
                            return w_slot(n).rearrange("p (k n) -> p k n", k=2)

                        b0 = 2 * (e % 2)
                        for m in range(2):
                            for q in range(4):
                                w = slot(4 * m + q)
                                for k in range(2):
                                    kk = 2 * q + k
                                    for j in range(NT):
                                        mm = pe.matmul(ps[M * j:M * j + M, b0 + m, 0:NW], XST[:, kk, e, 0:M],
                                                       w[:, k, j * NW:(j + 1) * NW], start=kk == 0, stop=kk == KD - 1)
                                mm.then_inc(used, 1)
                        pe.wait_ge(sem("hid_ready"), before("hid_ready", l) + i * GROUP + (e + 1))
                        nb = NW // P
                        for b in range(nb):
                            mm = transpose(ps[:, 4 + e % 2, b * P:(b + 1) * P], hid[:, b * P:(b + 1) * P], P)
                        mm.then_inc(sem("hid_tr"), 1)
                        pe.wait_ge(sem("hidT_ready"), before("hidT_ready", l) + i * GROUP + (e + 1))
                        if e >= 2:
                            pe.wait_ge(sem("y_taken"), before("y_taken", l) + i * GROUP + (e - 1))
                        for q in range(4):
                            w = slot(8 + q)
                            for k in range(2):
                                kk = 2 * q + k
                                lhs = hidT[:, (kk % nb) * P + (kk // nb) * M:(kk % nb) * P + (kk // nb) * M + M]
                                for j in range(NT):
                                    mm = pe.matmul(ps[M * j:M * j + M, 6 + e % 2, 0:NW], lhs,
                                                   w[:, k, j * NW:(j + 1) * NW], start=kk == 0, stop=kk == KD - 1)
                            mm.then_inc(used, 1)
                    pe.wait_ge(sem("y_taken"), before("y_taken", l) + i * GROUP + GROUP)
                    for o in range(NB_):
                        si, c2, half = o // 4, (o // 2) % 2, o % 2
                        if o >= 4:
                            pe.wait_ge(sem("ya_added"), before("ya_added", l) + i * NB_ + (o - 4 + 2))
                        pe.matmul(ps[:, o % 4, :], GT[:, si, c2 * P:(c2 + 1) * P], Yg[:, si, half * 512:(half + 1) * 512],
                                  start=True, stop=True).then_inc(sem("scattered"), 1)
                taken[0] += LOOPS * LOOP_LOADS
                if l == 0:
                    pe.wait_ge(sem("ya_added"), 8 * LOOPS + 1)

        @block.scalar
        def _(act):
            done = [0]

            def own(ins):
                done[0] += 1
                ins.then_inc(sem("act_own"), 1)
                act.wait_ge(sem("act_own"), done[0])

            def copy(o, i):
                return act.activation(o, i, ACT.Copy)

            def rstd(o, i, n):
                own(act.activation(o, i, ACT.Ln, bias=eps_t[:, 0:1], scale=1.0 / n))
                return act.activation(o, o, ACT.Exp, scale=-0.5)

            def exp_ln():
                act.preload_act_table_set("natural_log_exp_and_others")

            def mod_cols(o):
                l, g = MOD_GROUPS[o]
                act.wait_ge(sem("mod_tr"), o + 1)
                src = ps[:, 7, :].rearrange("p (b j r) -> p b j r", b=4, r=32)[:, :, :, 0:2]
                copy(modT[:, l, g, :, :, :], src).then_inc(sem("mod_col"), 1)

            def norm_stat(which, t, junk):
                own(act.activation(junk, X[:, t, :], ACT.Square, accum_out=stat[:, t:t + 1]))
                rstd(stat[:, t:t + 1], stat[:, t:t + 1], D).then_inc(sem(f"n{which}_rstd"), 1)

            def norm_ctx(l, which, dst):
                n = f"n{which}"
                sc, sh = ((SC1, SH1), (SC2, SH2))[which - 1]
                for k in range(KD):
                    act.wait_ge(sem(f"{n}_tr"), before(f"{n}_tr", l) + k + 1)
                    act.activation(dst[:, k, 0:CTX], ps[:, k % 2, 0:CTX], ACT.Identity, bias=mod_col(l, sh, k, 0),
                                   scale=mod_col(l, sc, k, 0)).then_inc(sem(f"{n}_ctx"), 1)

            pj = [0]

            def bank(l, name):
                i = pj_index(l, name)
                assert i == pj[0]
                pj[0] += 1
                act.wait_ge(sem("proj_ready"), i + 1)
                return ps[:, PJ_BANK[i], :]

            def took(ins):
                ins.then_inc(sem("proj_taken"), 1)

            def took_plain(o, i, func=ACT.Copy, scale=1.0):
                took(act.activation(o, i, func, scale=scale))

            act.wait_ge(small, 16 * 6)
            act.activation(vrow[0:16, :], vrow[0:16, :], ACT.Silu).then_inc(sem("vrow_ready"), 1)
            act.wait_ge(sem("vrow_tr"), 1)
            act.wait_ge(sem("consts_ready"), 1)
            own(copy(vcol[:, 0:30], ps[:, 7, 0:30]))
            for s, at in ((1, 0), (0, 8)):
                ins = copy(cT[:, :, s:s + 1], vcol[:, at:at + 8].rearrange("p (k a) -> p k a", a=1))
            ins.then_inc(sem("vcol_ready"), 1)
            exp_ln()

            for l, L in enumerate(layers):
                tq, nt = L.tq, L.nt
                if l == 0:
                    act.wait_ge(sem("x_loaded"), 32)
                for t in range(4):
                    if l:
                        act.wait_ge(sem("x_post2"), t + 1)
                    norm_stat(1, t, junk1)
                if l == 0:
                    mod_cols(0)
                norm_ctx(l, 1, hT)
                act.wait_ge(sem("bml_loaded"), 64)
                for f, row in enumerate((rI, rF)):
                    b = bank(l, f"gate_row{f}")
                    act.activation(row[0:32, :], b[0:32, :], ACT.Identity, bias=bml[0:32, l, f:f + 1])
                    took(act.activation(row[32:64, :].rearrange("p (s t) -> p s t", s=2)[:, :, ::-1],
                                        b[32:64, :].rearrange("p (s t) -> p s t", s=2), ACT.Identity,
                                        bias=bml[32:64, l, f:f + 1]))
                act.wait_ge(sem("abs_f"), before("abs_f", l) + 1)
                own(act.activation(rA[0:64, :], rA[0:64, :], ACT.Exp, scale=-1.0))
                act.activation(rA[0:64, :], rA[0:64, :], ACT.Ln, bias=1.0).then_inc(sem("log1p"), 1)
                for c2 in range(2):
                    took_plain(mq[:, c2, tq], bank(l, f"mq{c2}")[:, tq])
                for c2 in range(2):
                    took_plain(mk[:, c2, :], bank(l, f"mk{c2}"), scale=0.125)
                act.wait_ge(sem("rows_tr"), before("rows_tr", l) + 1)
                copy(gcol, ps[:, 4, 0:256].rearrange("p (t r) -> p t r", t=4))
                act.activation(enm, ps[:, 4, 256:512].rearrange("p (t r) -> p t r", t=4), ACT.Exp, scale=-1.0)\
                    .then_inc(sem("cols_ready"), 1)
                for half in range(2):
                    for t in range(4):
                        took_plain(mv1[:, t, 2 * half:2 * half + 2, 0:ML_V],
                                   bank(l, f"mv{half}{t}")[:, 0:256].rearrange("p (h v) -> p h v", h=2))
                for u in range(len(L.pairs)):
                    d = L.pairs[u][1]
                    for s in range(4):
                        act.wait_ge(sem("e1_ready"), before("e1_ready", l) + 4 * u + s + 1)
                        t0, t1, _ = span(L, d, s)
                        e = E[u % 2][:, s, t0 * P:t1 * P]
                        act.activation(e, e, ACT.Exp).then_inc(sem("exp_done"), 1)
                    if u < 2:
                        took_plain(nq[:, u, tq], bank(l, f"nq{u}")[:, tq], scale=0.125)
                    elif u < 4:
                        took_plain(nk[:, u - 2, :], bank(l, f"nk{u - 2}"))
                    else:
                        took_plain(nv[:, u - 4, :], bank(l, f"nv{u - 4}")[:, 0:256])
                act.wait_ge(sem("num_used"), before("num_used", l) + len(L.pairs) * nt // 2)
                act.wait_ge(sem("act_own"), done[0])
                for t in L.chunks:
                    for h in range(HEADS):
                        ins = act.activation(E[0][:, t, 0:ML_V], hml[:, t, h, :], ACT.Square,
                                             accum_out=stat[:, 16 + 4 * t + h:17 + 4 * t + h])
                        own(ins)
                a = stat[:, 16 + 4 * L.chunks[0]:32]
                rstd(a, a, ML_V).then_inc(sem("head_rstd"), 1)
                for h in range(HEADS):
                    took_plain(sgo[:, h, tq], bank(l, f"mo{h}")[:, tq], ACT.Sigmoid)
                exp_ln()
                w = w_slot(BASE[l] + krw_load(l))[:, 0:KD * 160].rearrange("p (k n) -> p k n", k=KD)[:, :, P:160]\
                    .rearrange("p k (a b i) -> p k a b i", a=2, b=2)
                n = BASE[l] + krw_load(l)
                act.wait_ge(sem("mlstm_out"), before("mlstm_out", l) + HEADS)
                for c2 in range(2):
                    b = bank(l, f"cq{c2}")
                    copy(cq[:, c2, tq], b[:, tq])
                    took(act.activation(sq[:, c2, tq], b[:, tq], ACT.Square))
                act.wait_ge(landed[n % SLOTS], 16 * uses(n))
                kr = krw[:, :, :].rearrange("p k (a b i) -> p k a b i", a=2, b=2)
                for b2 in range(2):
                    ins = copy(kr[:, :, :, b2, :], w[:, :, :, 1 - b2, :])
                ins.then_inc(sem("krw_ready"), 1)
                b = bank(l, "ckv")
                copy(ckv, b)
                took(act.activation(sq[:, 2, :], b, ACT.Square))
                act.wait_ge(sem("proj_taken"), pj[0])
                act.nop().then_inc(sem("sq_ready"), 1)
                b = bank(l, "kr")
                copy(kT[64:96, :, 0:CTX], b[64:96, 0:CTX].rearrange("p (a t) -> p a t", a=1).to_broadcast([32, HEADS, CTX]))
                took(copy(kr_a, b[64:96, CTX:T]))
                took(copy(kr_b, bank(l, "kr_pair")[64:96, 0:SEQ]))
                for j, (name, n_) in enumerate((("cq_sum", Q_RANK), ("ckv_sum", P))):
                    b = bank(l, name)
                    cols = tq if j == 0 else slice(0, T)
                    own(act.activation(rs2[:, j, cols], b[:, cols], ACT.Ln, bias=eps_t[:, 0:1], scale=1.0 / n_))
                    took(act.activation(rs2[:, j, cols], rs2[:, j, cols], ACT.Exp, scale=-0.5))
                scale = float(np.float32(QK) ** np.float32(-0.5))
                act.wait_ge(sem("lowrank_ready"), before("lowrank_ready", l) + 1)
                for h in range(HEADS):
                    took_plain(qT[0:QK, h, tq], bank(l, f"q{h}")[0:QK, tq], scale=scale)
                for h in range(HEADS):
                    took_plain(qrt[64:96, h, :], bank(l, f"q_pair{h}")[64:96, 0:SEQ], scale=scale)
                for h in range(HEADS):
                    took_plain(kT[0:64, h, :], bank(l, f"k{h}")[0:64, :])
                for t in range(4):
                    took_plain(vM[:, t, :], bank(l, f"v{t}")[:, 0:256])

                def pt_copy(i):
                    n_ = T if L.units[i][2] >= 2 else CTX
                    act.wait_ge(sem("attn_tr"), before("attn_tr", l) + i + 1)
                    if i >= 2:
                        act.wait_ge(sem("attn_v"), before("attn_v", l) + i - 1)
                    copy(PT[i % 2][:, 0:n_], ps[:, 2 + i % 2, 0:n_]).then_inc(sem("attn_pt"), 1)

                nu = len(L.units)
                for i in range(nu + 1):
                    if i < nu:
                        n_ = T if L.units[i][2] >= 2 else CTX
                        act.wait_ge(sem("attn_max"), before("attn_max", l) + i + 1)
                        if i >= 2:
                            act.wait_ge(sem("attn_tr"), before("attn_tr", l) + i - 1)
                        act.activation(Pa[i % 2][:, 0:n_], ps[:, i % 2, 0:n_], ACT.Exp, bias=stat[:, 32 + i % 2:33 + i % 2],
                                       accum_out=stat[:, 34 + i % 2:35 + i % 2]).then_inc(sem("attn_exp"), 1)
                    if i >= 1:
                        pt_copy(i - 1)
                    for f in range(6):
                        if i < nu and gate_step(f, nu) == i:
                            took_plain(early[f][:, tq], bank(l, f"gate{f}")[:, tq])
                act.wait_ge(sem("attn_o"), before("attn_o", l) + nu)
                act.wait_ge(sem("proj_taken"), pj[0])
                for u in range(24):
                    if u >= 3:
                        act.wait_ge(sem("mg_used"), before("mg_used", l) + u - 2)
                    if u >= 6:
                        act.wait_ge(sem("mg_gate"), before("mg_gate", l) + u - 5)
                    src = early[u] if u < 6 else ps[:, u % 3, :]
                    act.activation(sg_m[u % 3][:, tq], src[:, tq], ACT.Sigmoid).then_inc(sem("mg_sig"), 1)
                    for o in range(1, 6):
                        if l == 0 and u % 2 and mod_step(o) == u // 2 - 1:
                            mod_cols(o)
                if l == 0:
                    mod_cols(5)
                exp_ln()

                def gate_rows_taken(which, G):
                    for si, s in enumerate(L.streams):
                        for half in range(2):
                            act.wait_ge(sem(f"g{which}_ready"), before(f"g{which}_ready", l) + 2 * si + half + 1)
                            copy(G[:, s, 512 * half:512 * half + 512], ps[:, 6 + half, :]).then_inc(sem(f"g{which}_taken"), 1)

                def post_stat(which, t, Y, junk):
                    own(act.activation(junk, Y[:, t, :], ACT.Square, accum_out=stat[:, 40 + t:41 + t]))
                    rstd(stat[:, 40 + t:41 + t], stat[:, 40 + t:41 + t], D).then_inc(sem(f"post{which}_rstd"), 1)

                gate_rows_taken(1, G1)
                o = 0
                for j, t in enumerate(L.chunks):
                    for nb in range(4):
                        act.wait_ge(sem("wo_ready"), before("wo_ready", l) + o + 1)
                        copy(Ym[:, t, nb * BLK:(nb + 1) * BLK], ps[:, o % 6, 0:BLK]).then_inc(sem("wo_taken"), 1)
                        o += 1
                    act.wait_ge(sem("wo_taken"), before("wo_taken", l) + o)
                    post_stat(1, t, Ym, junk_y)
                    if j:
                        act.wait_ge(sem("x_post1"), before("x_post1", l) + j)
                        norm_stat(2, L.chunks[j - 1], junk_y)
                act.wait_ge(sem("x_post1"), before("x_post1", l) + nt)
                norm_stat(2, L.chunks[-1], junk_y)
                if l == 0:
                    norm_ctx(l, 2, h2T)
                act.wait_ge(sem("lg_shift"), before("lg_shift", l) + 1)
                act.activation(lg[:, 0:2 * L.ns, :], lg[:, 0:2 * L.ns, :], ACT.Exp).then_inc(sem("lg_exp"), 1)
                gate_rows_taken(2, G2)
                act.preload_act_table(ACT.Silu)
                M, NT, NW = L.M, L.NT, L.NW
                with act.Fori(0, LOOPS) as i:
                    if L.ns == 2:
                        for k in range(KD):
                            if k % 4 == 0:
                                act.wait_ge(sem("gathered"), before("gathered", l) + i * 4 + (k // 4 + 1))
                            ins = act.activation(XST[:, k, :, 0:CAP],
                                                 ps[:, k // 4, (k % 4) * P:(k % 4 + 1) * P].rearrange("p (e j) -> p e j", e=GROUP),
                                                 ACT.Identity, bias=mod_col(l, SH2, k, 0), scale=mod_col(l, SC2, k, 0))
                        ins.then_inc(sem("xs_ctx"), 1)
                    act.wait_ge(sem("gt_tr"), before("gt_tr", l) + i + 1)
                    copy(GT[:, 0:L.ns, :], ps[:, 4, 0:256 * L.ns].rearrange("p (s t) -> p s t", s=L.ns))\
                        .then_inc(sem("gt_ready"), 1)
                    for e in range(GROUP):
                        act.wait_ge(used, i * LOOP_LOADS + (LOOP_BASE[l] + e * EXP_LOADS + 4))
                        act.activation(sgh[:, 0:NW], ps[:, 2 * (e % 2), 0:NW], ACT.Silu).then_inc(sem("silu"), 1)
                        act.wait_ge(sem("hid_tr"), before("hid_tr", l) + i * GROUP + (e + 1))
                        copy(hidT[:, 0:NW], ps[:, 4 + e % 2, 0:NW]).then_inc(sem("hidT_ready"), 1)
                exp_ln()
                for j, t in enumerate(L.chunks):
                    act.wait_ge(sem("ya_added"), before("ya_added", l) + 4 * L.ns * (LOOPS - 1) + 2 * (j + 1) + 1)
                    post_stat(2, t, Ya, junk2)

        @block.vector
        def _(dve):
            done = [0]

            def own(ins):
                done[0] += 1
                ins.then_inc(sem("dve_own"), 1)
                dve.wait_ge(sem("dve_own"), done[0])

            def mod_row(o):
                l, g = MOD_GROUPS[o]
                dst = mod_tmp[:, :] if g == 0 else gate_rows[:, 2 * l + g - 1, :]
                dve.wait_ge(used, mod_loaded(o))
                dve.wait_ge(sem("mod_rows_ready"), o + 1)
                own(dve.tensor_tensor(dst, ps[:, 6, :], b_row[:, :], ALU.add))
                dve.scalar_tensor_tensor(out=dst, in0=dst, scalar=one_add[:, g:g + 1], in1=g_row[:, :],
                                         op0=ALU.add, op1=ALU.mult).then_inc(sem("mod_row"), 1)

            def norm_rows(l, which, j, t, dst):
                n = f"n{which}"
                dve.wait_ge(sem(f"{n}_rstd"), before(f"{n}_rstd", l) + j + 1)
                dve.tensor_scalar(dst[:, t, :], X[:, t, :], stat[:, t:t + 1], None, ALU.mult).then_inc(sem(f"{n}_xn"), 1)

            def norm_lat(l, which, hdst):
                n = f"n{which}"
                sc, sh = ((SC1, SH1), (SC2, SH2))[which - 1]
                for k in range(KD):
                    dve.wait_ge(sem(f"{n}_tr"), before(f"{n}_tr", l) + k + 1)
                    dve.tensor_scalar(hdst[:, k, CTX:T], ps[:, 2 + k % 2, 0:SEQ], mod_col(l, sc, k, 1), mod_col(l, sh, k, 1),
                                      ALU.mult, ALU.add).then_inc(sem(f"{n}_lat"), 1)

            dve.wait_ge(sem("consts_ready"), 1)
            for l, L in enumerate(layers):
                tq, nt = L.tq, L.nt
                if l == 0:
                    mod_row(0)
                    dve.wait_ge(sem("mod_col"), 1)
                for t in range(4):
                    norm_rows(l, 1, t, t, xn1)
                norm_lat(l, 1, hT)
                dve.wait_ge(sem("proj_taken"), pj_index(l, "gate_row1") + 1)
                dve.scalar_tensor_tensor(out=rA[0:64, :], in0=rF[0:64, :], scalar=-1.0, in1=rF[0:64, :],
                                         op0=ALU.mult, op1=ALU.max).then_inc(sem("abs_f"), 1)
                dve.wait_ge(sem("log1p"), before("log1p", l) + 1)
                own(dve.scalar_tensor_tensor(out=rS[0:64, :], in0=rF[0:64, :], scalar=0.0, in1=rA[0:64, :],
                                             op0=ALU.min, op1=ALU.subtract))
                own(dve.tensor_tensor_scan(out=rF[0:64, :], data0=ones[0:64, 0:1].to_broadcast([64, T]), data1=rS[0:64, :],
                                           initial=0.0, op0=ALU.mult, op1=ALU.add))
                own(dve.tensor_tensor(rG[0:64, :], rI[0:64, :], rF[0:64, :], ALU.subtract))
                own(dve.tensor_tensor_scan(out=rM[0:64, :], data0=rG[0:64, :], data1=rG[0:64, :], initial=0.0,
                                           op0=ALU.max, op1=ALU.max))
                for d in range(2):
                    rows = slice(32 * d, 32 * d + 32)

                    def natural(a):
                        v = a[rows, :].rearrange("p (s t) -> p s t", s=2)
                        return v[:, :, ::-1] if d else v

                    def plain(a):
                        return a[rows, :].rearrange("p (s t) -> p s t", s=2)

                    dve.tensor_copy(natural(R3[:, 0, :]), plain(rG))
                    dve.tensor_tensor(natural(R3[:, 1, :]), plain(rF), plain(rM), ALU.add)
                    ins = dve.tensor_scalar(natural(R3[:, 2, :]), plain(rM), -1.0, None, ALU.mult)
                ins.then_inc(sem("rows_ready"), 1)
                dve.wait_ge(sem("cols_ready"), before("cols_ready", l) + 1)

                def exponents(u):
                    h, d = L.pairs[u]
                    dve.wait_ge(sem("nm_ready"), before("nm_ready", l) + u + 1)
                    if u >= 2:
                        dve.wait_ge(sem("num_ready"), before("num_ready", l) + (u - 1) * (nt // 2))
                    for s in range(4):
                        t0, t1, m = span(L, d, s)
                        mask = (mask_f, mask_b)[d]
                        r = 32 * d + h
                        dve.scalar_tensor_tensor(out=E[u % 2][:, s, t0 * P:t1 * P], in0=ps[:, 3 + d, t0 * P:t1 * P],
                                                 scalar=gcol[:, s, r:r + 1], in1=mask[:, m:m + (t1 - t0) * P],
                                                 op0=ALU.add, op1=ALU.min).then_inc(sem("e1_ready"), 1)

                def weigh(u):
                    h, d = L.pairs[u]
                    dve.wait_ge(sem("sc_ready"), before("sc_ready", l) + h + 1)
                    for s in range(4):
                        t0, t1, m = span(L, d, s)
                        sc = ps[:, s, t0 * P:t1 * P] if s < 2 else \
                            ps[:, 2, 256 * (s - 2) + (t0 - 2) * P:256 * (s - 2) + (t1 - 2) * P]
                        e = E[u % 2][:, s, t0 * P:t1 * P]
                        dve.wait_ge(sem("exp_done"), before("exp_done", l) + 4 * u + s + 1)
                        ins = dve.tensor_tensor(e, sc, e, ALU.mult)
                    ins.then_inc(sem("p_ready"), 1)

                def head_out(u):
                    h, d = L.pairs[u]
                    r = 32 * d + h
                    for pi in range(nt // 2):
                        o = u * (nt // 2) + pi
                        ta = L.chunks[2 * pi]
                        b = ps[:, 5 + o % 2, 0:258].rearrange("p (t v) -> p t v", t=2)
                        den = b[:, :, ML_V:ML_V + 1]
                        z = stat[:, 48:50].rearrange("p (t v) -> p t v", v=1)
                        dve.wait_ge(sem("num_ready"), before("num_ready", l) + o + 1)
                        own(dve.scalar_tensor_tensor(out=z, in0=den, scalar=-1.0, in1=enm[:, ta:ta + 2, r:r + 1],
                                                     op0=ALU.mult, op1=ALU.max))
                        own(dve.scalar_tensor_tensor(out=z, in0=den, scalar=1.0, in1=z, op0=ALU.mult, op1=ALU.max))
                        own(dve.reciprocal(z, z))
                        for ti in range(2):
                            hh = hml[:, ta + ti, h, :]
                            if d == 0:
                                ins = dve.tensor_scalar(hh, b[:, ti, 0:ML_V], stat[:, 48 + ti:49 + ti], None, ALU.mult)
                            else:
                                ins = dve.scalar_tensor_tensor(out=hh, in0=b[:, ti, 0:ML_V], scalar=stat[:, 48 + ti:49 + ti],
                                                               in1=hh, op0=ALU.mult, op1=ALU.add)
                        ins.then_inc(sem("num_used"), 1)
                        dve.wait_ge(sem("num_used"), before("num_used", l) + o + 1)

                np_ = len(L.pairs)
                exponents(0)
                for u in range(np_):
                    if u + 1 < np_:
                        exponents(u + 1)
                    weigh(u)
                    if u:
                        head_out(u - 1)
                head_out(np_ - 1)
                c0 = L.chunks[0]
                hv = hml[:, c0:4, :, :].rearrange("p t h v -> p (t h) v")
                rb = stat[:, 16 + 4 * c0:32].rearrange("p (a v) -> p a v", v=1).to_broadcast([P, 4 * nt, ML_V])
                dve.wait_ge(sem("head_rstd"), before("head_rstd", l) + 1)
                dve.tensor_tensor(hv, hv, rb, ALU.mult).then_inc(sem("hn_ready"), 1)
                dve.wait_ge(sem("proj_taken"), pj_index(l, "mo3") + 1)
                for h in range(HEADS):
                    dve.wait_ge(sem("hm_tr"), before("hm_tr", l) + h + 1)
                    at = COL_GML + 4 * l + h
                    dve.scalar_tensor_tensor(out=mT[:, h, tq], in0=ps[:, 4 + h % 2, tq], scalar=vcol[:, at:at + 1],
                                             in1=sgo[:, h, tq], op0=ALU.mult, op1=ALU.mult)\
                        .then_inc(sem("mlstm_out"), 1)
                dve.wait_ge(small, 16 * 6)
                cos, sin = rope_t[64:96, 0, :], rope_t[64:96, 1, :]
                dve.wait_ge(sem("proj_taken"), pj_index(l, "kr_pair") + 1)
                own(dve.tensor_tensor(kr_a, kr_a, cos, ALU.mult))
                own(dve.tensor_tensor(kr_b, kr_b, sin, ALU.mult))

                def heads(a):
                    return a.rearrange("p (a t) -> p a t", a=1).to_broadcast([32, HEADS, SEQ])

                dve.tensor_tensor(kT[64:96, :, CTX:T], heads(kr_a), heads(kr_b), ALU.add)
                dve.wait_ge(sem("proj_taken"), pj_index(l, "ckv_sum") + 1)
                for c2 in range(2):
                    at = COL_GQ + 2 * l + c2
                    dve.scalar_tensor_tensor(out=cq[:, c2, tq], in0=cq[:, c2, tq], scalar=vcol[:, at:at + 1],
                                             in1=rs2[:, 0, tq], op0=ALU.mult, op1=ALU.mult)
                dve.scalar_tensor_tensor(out=ckv, in0=ckv, scalar=vcol[:, COL_GKV + l:COL_GKV + l + 1],
                                         in1=rs2[:, 1, :], op0=ALU.mult, op1=ALU.mult).then_inc(sem("lowrank_ready"), 1)
                dve.wait_ge(sem("proj_taken"), pj_index(l, "q_pair3") + 1)
                ql = qT[64:96, :, CTX:T]
                own(dve.tensor_tensor(ql, ql, heads(cos), ALU.mult))
                own(dve.tensor_tensor(qrt[64:96, :, :], qrt[64:96, :, :], heads(sin), ALU.mult))
                dve.tensor_tensor(ql, ql, qrt[64:96, :, :], ALU.add).then_inc(sem("roped"), 1)
                dve.wait_ge(sem("rel_mm"), before("rel_mm", l) + 1)
                dve.tensor_copy(BT.rearrange("p h d c -> p (h d c)").rearrange("p (b n) -> p b n", b=3), ps[:, 0:3, :])\
                    .then_inc(sem("rel_turned"), 1)
                dve.wait_ge(sem("proj_taken"), pj_index(l, "v3") + 1)

                def row_max(i):
                    kind, h, t = L.units[i]
                    n_ = T if t >= 2 else CTX
                    dve.wait_ge(sem("attn_score"), before("attn_score", l) + i + 1)
                    if kind == "na" and t >= 2:
                        d0 = 2 - 2 * (t - 2)
                        loc = ps[:, i % 2, CTX:T]
                        dve.wait_ge(sem("rel_ready"), before("rel_ready", l) + 1)
                        own(dve.tensor_tensor(loc, loc, BT[:, h, d0:d0 + 4, :].rearrange("p d c -> p (d c)"), ALU.add))
                    dve.tensor_reduce(stat[:, 32 + i % 2:33 + i % 2], ps[:, i % 2, 0:n_], AX.X, ALU.max, negate=True)\
                        .then_inc(sem("attn_max"), 1)

                def normalise(i):
                    n_ = T if L.units[i][2] >= 2 else CTX
                    dve.wait_ge(sem("attn_exp"), before("attn_exp", l) + i + 1)
                    own(dve.reciprocal(stat[:, 36 + i % 2:37 + i % 2], stat[:, 34 + i % 2:35 + i % 2]))
                    dve.tensor_scalar(Pa[i % 2][:, 0:n_], Pa[i % 2][:, 0:n_], stat[:, 36 + i % 2:37 + i % 2], None, ALU.mult)\
                        .then_inc(sem("attn_p"), 1)

                def head(i):
                    kind, h, t = L.units[i]
                    p0 = 64 * (h % 2)
                    dve.wait_ge(sem("attn_v"), before("attn_v", l) + i + 1)
                    dve.tensor_copy(aT[kind][p0:p0 + 64, h // 2, t * P:(t + 1) * P], ps[p0:p0 + 64, 4 + i % 2, 0:P])\
                        .then_inc(sem("attn_o"), 1)

                nu = len(L.units)
                for i in range(nu + 3):
                    if i < nu:
                        row_max(i)
                    if 1 <= i <= nu:
                        normalise(i - 1)
                    if i >= 3:
                        head(i - 3)
                for u in range(24):
                    jp, m, half = u // 6, (u // 2) % 3, u % 2
                    dst = merged[:, 2 * jp + half, tq]
                    dve.wait_ge(sem("mg_sig"), before("mg_sig", l) + u + 1)
                    dve.wait_ge(sem("mg_branch"), before("mg_branch", l) + u + 1)
                    if m == 0:
                        dve.tensor_tensor(dst, sg_m[u % 3][:, tq], ps[:, 3 + u % 3, tq], ALU.mult).then_inc(sem("mg_used"), 1)
                    else:
                        dve.tensor_tensor(tmp_m[:, tq], sg_m[u % 3][:, tq], ps[:, 3 + u % 3, tq], ALU.mult)\
                            .then_inc(sem("mg_used"), 1)
                        dve.wait_ge(sem("mg_used"), before("mg_used", l) + u + 1)
                        ins = dve.tensor_tensor(dst, dst, tmp_m[:, tq], ALU.add)
                        if m == 2:
                            ins.then_inc(sem("merged"), 1)
                            dve.wait_ge(sem("merged"), before("merged", l) + 2 * jp + half + 1)
                        else:
                            own(ins)
                    for o in range(1, 6):
                        if l == 0 and u % 2 and mod_step(o) == u // 2:
                            mod_row(o)

                def post(which, j, t, Y, G, tmp):
                    s = t // 2
                    if t % 2 == 0:
                        dve.wait_ge(sem(f"g{which}_taken"), before(f"g{which}_taken", l) + 2 * L.streams.index(s) + 2)
                    dve.wait_ge(sem(f"post{which}_rstd"), before(f"post{which}_rstd", l) + j + 1)
                    own(dve.scalar_tensor_tensor(out=tmp, in0=Y[:, t, :], scalar=stat[:, 40 + t:41 + t], in1=G[:, s, :],
                                                 op0=ALU.mult, op1=ALU.mult))
                    dve.tensor_tensor(X[:, t, :], X[:, t, :], tmp, ALU.add).then_inc(sem(f"x_post{which}"), 1)
                    dve.wait_ge(sem(f"x_post{which}"), before(f"x_post{which}", l) + j + 1)

                for j, t in enumerate(L.chunks):
                    post(1, j, t, Ym, G1, tmp1)
                    if j:
                        norm_rows(l, 2, j - 1, L.chunks[j - 1], xn2)
                norm_rows(l, 2, nt - 1, L.chunks[-1], xn2)
                norm_lat(l, 2, h2T)
                ns = L.ns
                R = N_EXP * ns
                lgp = ps[:, 0, 0:2 * R].rearrange("p (a e) -> p a e", e=N_EXP)
                lgs, af = lg[:, 0:2 * ns, :], aff[:, 0:2 * ns, :]

                def per_token(at):
                    return stat[:, at:at + 2 * ns].rearrange("p (a e) -> p a e", e=1).to_broadcast([P, 2 * ns, N_EXP])

                dve.wait_ge(sem("logits"), before("logits", l) + 1)
                own(dve.tensor_reduce(stat[:, 52:52 + 2 * ns], lgp, AX.X, ALU.max, negate=True))
                dve.tensor_tensor(lgs, lgp, per_token(52), ALU.add).then_inc(sem("lg_shift"), 1)
                dve.wait_ge(sem("lg_exp"), before("lg_exp", l) + 1)
                own(dve.tensor_reduce(stat[:, 56:56 + 2 * ns], lgs, AX.X, ALU.add))
                own(dve.reciprocal(stat[:, 60:60 + 2 * ns], stat[:, 56:56 + 2 * ns]))
                dve.tensor_tensor(af, lgs, per_token(60), ALU.mult).then_inc(sem("aff_ready"), 1)
                dve.wait_ge(sem("affT_tr"), before("affT_tr", l) + 1)
                own(dve.tensor_copy(wk[0][0:R, :], ps[0:R, 1, 0:SEQ]))
                for r in range(CAP // 8):
                    own(dve.max(top8[0:R, :], wk[r % 2][0:R, :]))
                    own(dve.match_replace(wk[(r + 1) % 2][0:R, :], top8[0:R, :], wk[r % 2][0:R, :], -1.0))
                own(dve.tensor_scalar(msk[0:R, :], wk[0][0:R, :], 0.0, None, ALU.is_lt))
                own(dve.tensor_tensor_scan(out=affT[0:R, :], data0=ones[0:R, 0:1].to_broadcast([R, SEQ]), data1=msk[0:R, :],
                                           initial=0.0, op0=ALU.mult, op1=ALU.add))
                own(dve.tensor_tensor(csum[0:R, :], affT[0:R, :], msk[0:R, :], ALU.mult))
                dve.tensor_scalar(csum[0:R, :], csum[0:R, :], -1.0, None, ALU.add).then_inc(sem("rank_ready"), 1)
                dve.wait_ge(sem("rank_tr"), before("rank_tr", l) + 1)
                own(dve.tensor_copy(pmT[:, :, 0:R], ps[:, 2, 0:64].rearrange("p (c r) -> p c r", c=2)[:, :, 0:R]))
                io = iota[:, :].rearrange("p (a j) -> p a j", a=1).to_broadcast([P, N_EXP, CAP])
                for si in range(ns):
                    for c2 in range(2):
                        s_ = Ssel[:, si, c2, :].rearrange("p (e j) -> p e j", e=N_EXP)
                        pm = pmT[:, c2, si * N_EXP:(si + 1) * N_EXP].rearrange("p (e j) -> p e j", j=1)
                        own(dve.tensor_tensor(s_, io, pm.to_broadcast([P, N_EXP, CAP]), ALU.is_equal))
                dve.nop().then_inc(sem("routed"), 1)
                dve.memset(Ya[:, :, :], 0.0).then_inc(sem("ya_added"), 1)
                M, NT, NW = L.M, L.NT, L.NW
                NB_ = 4 * ns
                with dve.Fori(0, LOOPS) as i:
                    so = ns - 1
                    for k in range(KD):
                        if k % 4 == 0:
                            dve.wait_ge(sem("gathered"), before("gathered", l) + i * (2 * ns) + (2 * so + k // 4 + 1))
                        ins = dve.tensor_scalar(XST[:, k, :, so * CAP:(so + 1) * CAP],
                                                ps[:, 2 * so + k // 4, (k % 4) * P:(k % 4 + 1) * P].rearrange("p (e j) -> p e j", e=GROUP),
                                                mod_col(l, SC2, k, 1), mod_col(l, SH2, k, 1), ALU.mult, ALU.add)
                    ins.then_inc(sem("xs_lat"), 1)
                    for e in range(GROUP):
                        dve.wait_ge(sem("silu"), before("silu", l) + i * GROUP + (e + 1))
                        dve.wait_ge(used, i * LOOP_LOADS + (LOOP_BASE[l] + e * EXP_LOADS + 8))
                        dve.tensor_tensor(hid[:, 0:NW], sgh[:, 0:NW], ps[:, 2 * (e % 2) + 1, 0:NW], ALU.mult)\
                            .then_inc(sem("hid_ready"), 1)
                        dve.wait_ge(used, i * LOOP_LOADS + (LOOP_BASE[l] + (e + 1) * EXP_LOADS))
                        for j in range(4):
                            si, at = y_piece(L, j)
                            ins = dve.tensor_copy(Yg[e * CAP:(e + 1) * CAP, si, at:at + NW],
                                                  ps[j * CAP:(j + 1) * CAP, 6 + e % 2, 0:NW])
                        ins.then_inc(sem("y_taken"), 1)
                    for o in range(NB_):
                        si, c2, half = o // 4, (o // 2) % 2, o % 2
                        y = Ya[:, 2 * L.streams[si] + c2, half * 512:(half + 1) * 512]
                        dve.wait_ge(sem("scattered"), before("scattered", l) + i * NB_ + (o + 1))
                        dve.tensor_tensor(y, y, ps[:, o % 4, :], ALU.add).then_inc(sem("ya_added"), 1)
                dve.wait_ge(sem("ya_added"), before("ya_added", l) + NB_ * LOOPS + 1)
                for j, t in enumerate(L.chunks):
                    post(2, j, t, Ya, G2, tmp2)
                if l == 0:
                    dve.wait_ge(sem("x_post2"), 4)


def uses(n):
    return n // SLOTS + 1


def mod_loaded(o):
    return ring_loads(0).index(("mod", *MOD_GROUPS[o], KD - 1)) + 1


def gate_step(f, nu):
    return next(i for i in range(nu) if (f + 1) * KD <= 6 * KD * (i + 1) // nu)


def krw_load(l):
    return ring_loads(l).index(("in", l, C_CKV, C_NQ - C_CKV))


def keys_of(t, d):
    if t < 2:
        return [s for s in range(2) if (s <= t if d == 0 else s >= t)]
    return [0, 1] + [s for s in (2, 3) if (s <= t if d == 0 else s >= t)]


def span(L, d, s):
    if L.n and s < 2:
        return 2, 4, 2 * P if d else P
    if d == 0:
        return s, 4, 0
    if s < 2:
        return 0, 4, P - s * P
    return 2, s + 1, P if s == 2 else 0


def y_piece(L, j):
    return (j % 2, (j // 2) * L.NW) if L.ns == 2 else (0, j * L.NW)


_INS = ['x', 'c', 'ctx', 'c_ctx', 'w_mod', 'b_mod', 'g_pre1', 'g_post1', 'g_pre2', 'g_post2', 'w_in', 'g_q', 'g_kv',
        'w_uq', 'w_ukv', 'rpb', 'b_ml_gates', 'g_ml', 'w_br_mla', 'w_br_na', 'w_br_ml', 'w_out',
        'w_router', 'w_e1', 'w_e3', 'w_e2']


def kernel(**inputs):
    import numpy as _np
    import concourse.bacc as _bacc
    from concourse import mybir as _mybir
    from concourse.bass_utils import run_bass_kernel_spmd as _run

    nc = _bacc.Bacc("TRN2", target_bir_lowering=False, num_devices=1)
    arrays, args = {}, []
    for name in _INS:
        a = _np.ascontiguousarray(inputs[name])
        arrays[f"in_{name}_dram"] = a
        args.append(nc.dram_tensor(f"in_{name}_dram", a.shape, _mybir.dt.from_np(a.dtype), kind="ExternalInput").ap())
    a = rope_table()
    arrays["rope_dram"] = a
    args.append(nc.dram_tensor("rope_dram", a.shape, _mybir.dt.from_np(a.dtype), kind="ExternalInput").ap())
    args.append(nc.dram_tensor("out_0_dram", (1, SEQ, D), _mybir.dt.from_np(_np.dtype("float32")), kind="ExternalOutput").ap())
    backbone(nc, *args)
    r = _run(nc, [arrays], core_ids=[0])
    return r.results[0]["out_0_dram"]
```

```python
from contextlib import ExitStack

import numpy as np

import concourse.bass as bass
from concourse import mybir

F32 = mybir.dt.float32
ALU = mybir.AluOpType
ACT = mybir.ActivationFunctionType
AX = mybir.AxisListType

P = 128
D = 1024
KD = D // P
CTX = 256
SEQ = 256
T = CTX + SEQ
EPS = 1e-6
NEG = -1e30
GRID_W = 64
HEADS = 4
Q_RANK = 256
NOPE = 64
ROPE = 32
QK = NOPE + ROPE
NA_KR, NA_KC = 8, 16
RPB_R, RPB_C = 2 * NA_KR - 1, 2 * NA_KC - 1
ML_V = 128
N_EXP = 16
CAP = 32
GROUP = P // CAP
SLOTS = 8
SLOT = 2048
BLK = SLOT // KD

C_CQ, C_CKV, C_NQ, C_NK, C_NV = 0, 256, 416, 672, 928
C_MQ, C_MK, C_MV, C_MO, C_MG, C_BG = 1184, 1440, 1696, 2208, 2720, 2736


MOD_GROUPS = [(l, g) for l in range(2) for g in range(3)]
MERGE_STEPS = 3 * KD // 2


def rope_table():
    t = np.arange(SEQ)
    pos = np.stack([t // GRID_W, t % GRID_W], 0).astype(np.float32)
    nf = ROPE // 4
    inv = (np.float32(10000.0) ** (-np.arange(nf, dtype=np.float32) / np.float32(nf))).astype(np.float32)
    ang = (pos[:, None, :] * inv[None, :, None]).astype(np.float32)
    cos = np.repeat(np.cos(ang)[:, None], 2, 1).reshape(ROPE, SEQ)
    sin = np.stack([-np.sin(ang), np.sin(ang)], 1).reshape(ROPE, SEQ)
    return np.stack([cos, sin], 1).astype(np.float32)




class Layer:

    def __init__(self, n):
        self.n = n
        self.streams = [0, 1] if n == 0 else [1]
        self.chunks = [2 * s + c for s in self.streams for c in range(2)]
        self.t0 = self.chunks[0] * P
        self.tq = slice(self.t0, T)
        self.nt = len(self.chunks)
        self.ns = len(self.streams)
        self.units = [(kind, 2 * hp + i, t) for kind in ("mla", "na") for hp in range(HEADS // 2) for t in self.chunks
                      for i in range(2)]
        self.pairs = [(h, d) for h in range(HEADS) for d in range(2)]
        self.M = CAP * self.ns
        self.NT = P // self.M
        self.NW = D // self.NT


UNITS0, PAIRS0 = 32, 8
LAYER0 = dict(
    params_mg=16, params=64, wgp_ready=1, wuqr_ready=1, v_ones=1, rel_loaded=16 * 2 * HEADS, rel_mm=1, rel_turned=1, rel_ready=1,
    n1_rstd=4, n1_xn=4, n1_tr=KD, n1_lat=KD, n1_ctx=KD, n2_rstd=4, n2_xn=4, n2_tr=KD, n2_lat=KD, n2_ctx=KD,
    abs_f=1, log1p=1, rows_ready=1, rows_tr=1, cols_ready=1, sc_ready=HEADS, nm_ready=PAIRS0, e1_ready=4 * PAIRS0,
    exp_done=4 * PAIRS0, p_ready=PAIRS0, num_ready=2 * PAIRS0, num_used=2 * PAIRS0, head_rstd=1, hn_ready=1,
    hm_tr=HEADS, mlstm_out=HEADS, krw_ready=1, sq_ready=1, lowrank_ready=1, roped=1,
    attn_score=UNITS0, attn_max=UNITS0, attn_exp=UNITS0, attn_p=UNITS0, attn_tr=UNITS0, attn_pt=UNITS0,
    attn_v=UNITS0 // 2, attn_o=UNITS0 // 2, mg_gate=18, mg_sig=24, mg_branch=24, mg_used=24, merged=KD,
    wo_ready=16, wo_taken=16, g1_ready=4, g1_taken=4, g2_ready=4, g2_taken=4, post1_rstd=4, post2_rstd=4,
    x_post1=4, x_post2=4, logit_parts=1, lgT_ready=1, logits=1, lg_shift=1, lg_exp=1, aff_ready=1, affT_tr=1, rank_ready=1, rank_tr=1,
    routed=4, gathered=16, staged=4, gt_tr=4, gt_ready=4, xs_lat=8, xs_ctx=8, silu=N_EXP,
    hid_ready=N_EXP, hid_tr=N_EXP, hidT_ready=N_EXP, y_taken=N_EXP,
    scattered=32, ya_added=33,
)


def before(name, l):
    return LAYER0[name] * l


def mod_steps(step):
    n = 3 * KD
    return range(n * step // MERGE_STEPS, n * (step + 1) // MERGE_STEPS)


def mod_step(o):
    return next(s for s in range(MERGE_STEPS) if o * KD - 1 in mod_steps(s))


def weight_loads(layer):
    loads = [("mod", *MOD_GROUPS[5 if layer else 0], k) for k in range(KD)]
    loads += [("in", layer, c, BLK) for c in (C_MQ, C_MK, C_MV, C_MV + BLK, C_NQ, C_NK, C_NV, C_MO, C_MO + BLK, C_CQ)]
    loads += [("in", layer, C_CKV, C_NQ - C_CKV)]
    loads += [("in", layer, C_BG + m * D, BLK) for m in range(3)]
    loads += [("branch", layer, jp) for jp in range(2)]
    for jp in range(KD // 2):
        for m in range(3):
            if jp:
                loads += [("in", layer, C_BG + m * D + jp * BLK, BLK)]
            if layer == 0:
                loads += [("mod", *MOD_GROUPS[1 + n // KD], n % KD) for n in mod_steps(3 * jp + m)]
        if 1 <= jp < KD // 2 - 1:
            loads += [("branch", layer, jp + 1)]
    loads += [("out", layer, nb) for nb in range(D // BLK)]
    if layer == 0:
        loads += [("mod", *MOD_GROUPS[4], k) for k in range(KD)]
    return loads


def ring_loads(layer):
    return [w for w in weight_loads(layer) if w[0] != "branch"]


PROJECTIONS = ["gate_rows", "mq0", "mq1", "mk0", "mk1", *(f"mv{h}{t}" for h in range(2) for t in range(4)),
      "nq0", "nq1", "nk0", "nk1", *(f"nv{t}" for t in range(4)), *(f"mo{h}" for h in range(HEADS)),
      "cq0", "cq1", "ckv", "kr", "cq_sum", "ckv_sum",
      *(f"q{h}" for h in range(HEADS)), "k0", "k1", *(f"v{t}" for t in range(4)), *(f"gate{f}" for f in range(6))]
PROJECTION_BANK, BANK_USED_BY = [], []


def _assign_banks():
    turn = 0
    for name in 2 * PROJECTIONS:
        if name[:2] in ("nq", "nk", "nv"):
            b = 7
        elif name[:4] == "gate" and name[4] != "_":
            b = 6 + int(name[4]) % 2
        else:
            b = turn % 4
            turn += 1
        same = [i for i, c in enumerate(PROJECTION_BANK) if c == b]
        BANK_USED_BY.append(same[-1] if same else None)
        PROJECTION_BANK.append(b)


_assign_banks()


def pj_index(l, name):
    return l * len(PROJECTIONS) + PROJECTIONS.index(name)


EXP_LOADS = 12
LOOP_LOADS = GROUP * EXP_LOADS
LOOPS = N_EXP // GROUP
BASE = []
_n = 0
for _l in range(2):
    BASE.append(_n)
    _n += len(ring_loads(_l)) + LOOPS * LOOP_LOADS
LOOP_BASE = [BASE[l] + len(ring_loads(l)) for l in range(2)]


def backbone(nc, x, c, ctx, c_ctx, w_mod, b_mod, g_pre1, g_post1, g_pre2, g_post2, w_in, g_q, g_kv, w_uq, w_ukv,
             rpb, b_ml_gates, g_ml, w_br_mla, w_br_na, w_br_ml, w_out, w_router, w_e1, w_e3, w_e2, rope, out):
    with ExitStack() as stack:
        def sb(name, *shape):
            return stack.enter_context(nc.sbuf_tensor(name, [P, *shape], F32))

        sems = {}

        def sem(name):
            if name not in sems:
                sems[name] = stack.enter_context(nc.semaphore(name))
            return sems[name]

        layers = [Layer(0), Layer(1)]

        X = sb("X", 4, D)
        ring = sb("ring", SLOTS, SLOT)
        gate_rows = sb("gate_rows", 4, 512)
        mod_tmp = sb("mod_tmp", 512)
        b_row = sb("b_row", 512)
        g_row = sb("g_row", 512)
        ident = sb("ident", P)
        ones = sb("ones", P)
        flip = sb("flip", P)
        mask_f = sb("mask_f", 512)
        mask_b = sb("mask_b", 640)
        rope_t = sb("rope_t", 2, SEQ)
        iota = sb("iota", CAP)
        wuq = sb("wuq", 2, HEADS, QK + ROPE)
        wukv = sb("wukv", 2, HEADS * 64)
        wrt = sb("wrt", KD, 2 * N_EXP)
        sum4 = sb("sum4", N_EXP)
        mgw = sb("mgw", KD, 16)
        krw = sb("krw", KD, ROPE)
        vrow = sb("vrow", P)
        vcol = sb("vcol", 32)
        cT = sb("cT", KD, 32)
        modT = sb("modT", 2, 3, 4, 4, 2)
        bml = sb("bml", 2)
        one_add = sb("one_add", 3)
        eps_t = sb("eps_t", 1)
        stat = sb("stat", 64)
        top8 = sb("top8", 8)
        ARENA = 23568
        arena = sb("arena", ARENA)

        def view(at, *dims):
            n = int(np.prod(dims))
            assert at + n <= ARENA, (at, dims)
            v = arena[:, at:at + n]
            if len(dims) == 1:
                return v
            names = "abcde"[:len(dims)]
            return v.rearrange(f"p ({' '.join(names)}) -> p {' '.join(names)}",
                               **{k: d for k, d in zip(names, dims)})

        hT = view(0, KD, T)
        mT = view(4096, HEADS, T)
        wgp = view(6144, KD, 2, 2, 32)
        aT = {"mla": view(6144, 2, T), "na": view(7168, 2, T)}
        mq = view(8192, 2, T)
        mk = view(9216, 2, T)
        sgo = view(8192, HEADS, T)
        mv1 = view(10240, 4, HEADS, ML_V + 1)
        hml = view(12304, 4, HEADS, ML_V)
        E = [view(14352 + 2048 * b, 4, T) for b in range(2)]
        rI, rF, rA, rS, rG = (view(18448 + 512 * b, T) for b in range(5))
        rM = rA
        R3 = view(21008, 3, T)
        gcol = view(22544, 4, 64)
        enm = view(22800, 4, 64)
        xn1 = view(12304, 4, D)
        junk1 = view(21056, D)
        cq = view(10240, 2, T)
        ckv = view(11264, T)
        sq = view(11776, 3, T)
        rs2 = view(13312, 2, T)
        qT = view(14336, HEADS, T)
        kT = view(16384, HEADS, T)
        vM = view(21520, 4, HEADS * 64)
        krt = view(9728, 2, SEQ)
        kr_a, kr_b = (krt[64:96, b, :] for b in range(2))
        qrt = view(12800, HEADS, SEQ)
        nq = view(18448, 2, T)
        nk = view(19472, 2, T)
        nv = view(20496, 4, HEADS * 64)
        early = [view(at, T) for at in (10240, 10752, 11264, 13824, 22544, 23056)]
        BT = view(8192, HEADS, 6, GRID_W)
        Pa = [view(11776 + 512 * b, T) for b in range(2)]
        PT = [view(12800 + 512 * b, T) for b in range(2)]
        branches = [view(14336 + SLOT * b, SLOT).rearrange("p (k n) -> p k n", k=KD) for b in range(2)]
        merged = view(8192, KD, T)
        sg_m = [view(12288 + 512 * b, T) for b in range(3)]
        tmp_m = view(20480, T)
        Ym = view(14336, 4, D)
        G1 = view(18432, 2, D)
        tmp1 = view(20480, D)
        junk_y = view(21504, D)
        xn2 = view(0, 4, D)
        G2 = view(18944, 2, D)
        Ssel = view(4096, 2, 2, 512)
        Sg = view(6144, 2, 2, 512)
        h2T = view(8192, KD, T)
        XST = view(8192, KD, GROUP, 64)
        stg = view(10240, 2, 2, P)
        GT = view(10752, 2, SEQ)
        Yg = view(11264, 2, D)
        Ya = view(13312, 4, D)
        sgh = view(17408, 512)
        hid = view(17920, 512)
        hidT = view(18432, 512)
        tmp2 = view(9216, D)
        junk2 = view(8192, D)
        aff = view(20992, 4, N_EXP)
        lg = view(21056, 4, N_EXP)
        affT = view(21120, SEQ)
        lgT = view(21376, T)
        wk = [view(21376 + 256 * b, SEQ) for b in range(2)]
        msk = view(21888, SEQ)
        csum = view(22144, SEQ)
        pmT = view(22400, 2, 32)

        ps = stack.enter_context(nc.psum_tensor("ps", [P, 8, 512], F32))
        COL_C, COL_GQ, COL_GKV, COL_GML = 0, 16, 20, 22

        def mod_col(l, vec, k, s):
            return modT[:, l, vec // 2, k % 4, 2 * (vec % 2) + k // 4, s:s + 1]

        SH1, SC1, GT1, SH2, SC2, GT2 = range(6)

        def w_slot(n):
            return ring[:, n % SLOTS, :]

        landed = [sem(f"weights_landed_{i}") for i in range(SLOTS)]
        used = sem("weights_used")
        small = sem("small_loaded")

        block = stack.enter_context(nc.Block())

        @block.sync
        def _(sp):
            sp.dma_start(vrow[0:8, :], c.rearrange("a (k p) -> (a k) p", p=P)).then_inc(small, 16)
            sp.dma_start(vrow[8:16, :], c_ctx.rearrange("(k p) -> k p", p=P)).then_inc(small, 16)
            sp.dma_start(vrow[16:20, :], g_q.rearrange("l (k p) -> (l k) p", p=P)).then_inc(small, 16)
            sp.dma_start(vrow[20:22, :], g_kv).then_inc(small, 16)
            sp.dma_start(vrow[22:30, :], g_ml.rearrange("l (k p) -> (l k) p", p=P)).then_inc(small, 16)
            sp.dma_start(rope_t[64:96, :, :], rope).then_inc(small, 16)
            for s, src in ((1, x), (0, ctx)):
                sp.dma_start(X[:, 2 * s:2 * s + 2, :], src.rearrange("a (c p) d -> p (a c) d", p=P)).then_inc(sem("x_loaded"), 16)

            def load(n, dst, src):
                if n >= SLOTS:
                    sp.wait_ge(used, n - SLOTS + 1)
                sp.dma_start(dst, src).then_inc(landed[n % SLOTS], 16)

            for l in range(2):
                n = BASE[l]
                for kind, lw, *a in weight_loads(l):
                    if kind == "branch":
                        jp = a[0]
                        if jp < 2:
                            sp.wait_ge(sem("attn_score"), before("attn_score", l) + len(layers[l].units) // 2 + 1)
                        else:
                            sp.wait_ge(sem("mg_branch"), before("mg_branch", l) + 6 * (jp - 1))
                        cols = slice(jp * BLK, (jp + 1) * BLK)
                        for k0, w in ((0, w_br_mla), (2, w_br_na), (4, w_br_ml)):
                            k1 = k0 + w.shape[1] // P
                            sp.dma_start(branches[jp % 2][:, k0:k1, :], w[lw, :, cols].rearrange("(k p) n -> p k n", p=P))\
                              .then_inc(sem(f"branch_landed_{jp % 2}"), 16)
                        continue
                    if kind == "mod":
                        load(n, w_slot(n), w_mod[lw, a[1] * P:(a[1] + 1) * P, a[0] * SLOT:(a[0] + 1) * SLOT])
                    elif kind == "in":
                        load(n, w_slot(n)[:, 0:KD * a[1]].rearrange("p (k n) -> p k n", k=KD),
                             w_in[lw, :, a[0]:a[0] + a[1]].rearrange("(k p) n -> p k n", p=P))
                    else:
                        load(n, w_slot(n).rearrange("p (k n) -> p k n", k=KD),
                             w_out[lw, :, a[0] * BLK:(a[0] + 1) * BLK].rearrange("(k p) n -> p k n", p=P))
                    n += 1
                with sp.Fori(0, LOOPS) as i:
                    for e in range(GROUP):
                        for m, w in enumerate((w_e1, w_e3, w_e2)):
                            we = w[l].rearrange("(i e) (q k p) n -> i e q p k n", e=GROUP, q=4, p=P)
                            for q in range(4):
                                n = LOOP_BASE[l] + e * EXP_LOADS + m * 4 + q
                                sp.wait_ge(used, i * LOOP_LOADS + (n - SLOTS + 1))
                                sp.dma_start(w_slot(n).rearrange("p (k n) -> p k n", k=2),
                                             we[bass.ds(i, 1), e, q].rearrange("i p k n -> p (i k) n"))\
                                  .then_inc(landed[n % SLOTS], 16)
            for s in range(2):
                sp.wait_ge(sem("x_post2"), before("x_post2", 1) + s + 1)
                sp.dma_start(out[0, s * P:(s + 1) * P, :], X[:, 2 + s, :]).then_inc(sem("out_stored"), 16)
            sp.wait_ge(sem("out_stored"), 32)

        @block.gpsimd
        def _(pool):
            done = [0]

            def own(ins):
                done[0] += 1
                ins.then_inc(sem("pool_own"), 1)
                pool.wait_ge(sem("pool_own"), done[0])

            def params(l):
                if l:
                    pool.wait_ge(sem("attn_score"), 1)
                pool.dma_start(mgw[:, :, :], w_in[l, :, C_MG:C_BG].rearrange("(k p) n -> p k n", p=P))\
                    .then_inc(sem("params_mg"), 16)
                for k in range(2):
                    pool.dma_start(wuq[:, k, :, 0:QK], w_uq[l, k * P:(k + 1) * P, :, :]).then_inc(sem("params"), 16)
                for part in range(2):
                    pool.dma_start(wukv[:, part, :].rearrange("p (h e) -> p h e", h=HEADS),
                                   w_ukv[l, :, :, 64 * part:64 * part + 64]).then_inc(sem("params"), 16)

            rows_loaded = [0]

            def mod_rows_load(o):
                l, g = MOD_GROUPS[o]
                if o:
                    pool.wait_ge(sem("mod_row"), o)
                gains = {0: (None, g_pre1), 1: (g_post1, None), 2: (g_pre2, g_post2)}[g]
                for half, src in enumerate(gains):
                    if src is None:
                        own(pool.memset(g_row[64 * half:64 * half + 64, :], 1.0))
                for r in range(2):
                    pool.dma_start(b_row[r:r + 97:32, :],
                                   b_mod[l, g * 2048:(g + 1) * 2048].rearrange("(j n) -> j n", j=4))\
                        .then_inc(sem("mod_rows_loaded"), 16)
                    rows_loaded[0] += 16
                    for half, src in enumerate(gains):
                        if src is not None:
                            p0 = 64 * half + r
                            pool.dma_start(g_row[p0:p0 + 33:32, :], src[l].rearrange("(j n) -> j n", j=2))\
                                .then_inc(sem("mod_rows_loaded"), 16)
                            rows_loaded[0] += 16

            def mod_rows_wait():
                pool.wait_ge(sem("mod_rows_loaded"), rows_loaded[0])
                pool.nop().then_inc(sem("mod_rows_ready"), 1)

            def mod_rows(o):
                mod_rows_load(o)
                mod_rows_wait()

            own(pool.memset(b_row[:, :], 0.0))
            own(pool.memset(g_row[:, :], 1.0))
            mod_rows_load(0)
            params(0)
            own(pool.memset(ident[:, :], 0.0))
            pool.affine_select(out=ident[:, :], in_=ident[:, :], compare_op=ALU.not_equal, fill=1.0, base=0,
                               pattern=[[-1, P]], channel_multiplier=1).then_inc(sem("ident_ready"), 1)
            own(pool.memset(flip[:, :], 0.0))
            for r in range(2):
                v = flip[64 * r:64 * r + 64, :]
                own(pool.affine_select(out=v, in_=v, compare_op=ALU.not_equal, fill=1.0, base=-(64 * r + 63),
                                       pattern=[[1, P]], channel_multiplier=1))
            pool.memset(ones[:, :], 1.0)
            pool.memset(eps_t[:, :], EPS)
            own(pool.memset(one_add[:, :], 0.0))
            own(pool.memset(one_add[64:128, 0:1], 1.0))
            own(pool.memset(one_add[0:64, 2:3], 1.0))
            own(pool.tensor_copy(sum4[:, :], ident[:, 0:N_EXP]))
            for j in range(1, 4):
                own(pool.tensor_tensor(sum4[:, :], sum4[:, :], ident[:, 32 * j:32 * j + N_EXP], ALU.add))
            own(pool.memset(wrt[:, :, :], 0.0))
            pool.memset(cT[:, :, :], 0.0)
            pool.memset(bml[:, :], 0.0)
            pool.memset(mask_f[:, :], 0.0)
            own(pool.memset(mask_b[:, :], 0.0))
            pool.affine_select(out=mask_f[:, 0:P], in_=mask_f[:, 0:P], compare_op=ALU.is_ge, fill=NEG, base=0,
                               pattern=[[1, P]], channel_multiplier=-1)
            pool.affine_select(out=mask_b[:, P:2 * P], in_=mask_b[:, P:2 * P], compare_op=ALU.is_ge, fill=NEG, base=0,
                               pattern=[[-1, P]], channel_multiplier=1)
            own(pool.iota(iota[:, :], pattern=[[1, CAP]], base=0, channel_multiplier=0,
                          allow_small_or_imprecise_dtypes=True))
            pool.nop().then_inc(sem("consts_ready"), 1)

            def gates_weights(l):
                if l:
                    pool.wait_ge(sem("x_post2"), 4)
                pool.wait_ge(sem("params_mg"), before("params_mg", l) + 16)
                own(pool.memset(wgp[:, :, :, :, :], 0.0))
                for d in range(2):
                    for f in range(2):
                        at = (2 * d + f) * HEADS
                        own(pool.tensor_copy(wgp[:, :, f, d, 0:HEADS], mgw[:, :, at:at + HEADS]))
                pool.nop().then_inc(sem("wgp_ready"), 1)
                pool.wait_ge(sem("params"), before("params", l) + 64)
                for k in range(2):
                    q, r = (wuq[:, k, :, at:at + ROPE].rearrange("p h (a b i) -> p h a b i", a=2, b=2) for at in (NOPE, QK))
                    for b in range(2):
                        own(pool.tensor_copy(r[:, :, :, b, :], q[:, :, :, 1 - b, :]))
                pool.nop().then_inc(sem("wuqr_ready"), 1)

            def v_ones(l):
                pool.wait_ge(sem("n1_tr"), before("n1_tr", l) + KD)
                pool.memset(mv1[:, :, :, ML_V:ML_V + 1], 1.0).then_inc(sem("v_ones"), 1)
                pool.wait_ge(sem("v_ones"), before("v_ones", l) + 1)

            def rel_bias(l):
                pool.wait_ge(sem("mlstm_out"), before("mlstm_out", l) + HEADS)
                for r in range(2):
                    for h in range(HEADS):
                        at = ((l * HEADS + h) * RPB_R + NA_KR - 1 - 2 - r) * RPB_C + NA_KC - GRID_W
                        src = bass.AP(rpb.tensor, at, [[1, GRID_W], [RPB_C, 6], [1, GRID_W]])
                        pool.dma_start(BT[64 * r:64 * r + 64, h, :, :], src).then_inc(sem("rel_loaded"), 16)
                pool.wait_ge(sem("rel_turned"), before("rel_turned", l) + 1)
                half = NA_KC // 2
                for r in range(2):
                    v = BT[64 * r:64 * r + 64].rearrange("p h d c -> p (h d) c")
                    a, b = v[:, :, 0:GRID_W - NA_KC], v[:, :, NA_KC:GRID_W]
                    own(pool.affine_select(out=a, in_=a, compare_op=ALU.is_ge, fill=NEG, base=half,
                                           pattern=[[0, 24], [1, GRID_W - NA_KC]], channel_multiplier=-1))
                    own(pool.affine_select(out=b, in_=b, compare_op=ALU.is_ge, fill=NEG, base=half - 1 - NA_KC,
                                           pattern=[[0, 24], [-1, GRID_W - NA_KC]], channel_multiplier=1))
                pool.nop().then_inc(sem("rel_ready"), 1)

            mod_rows_wait()
            for l in range(2):
                for f in range(2):
                    for d in range(2):
                        p0 = 64 * f + 32 * d
                        at = (2 * d + f) * HEADS
                        pool.dma_start(bml[p0:p0 + HEADS, l:l + 1], b_ml_gates[l, at:at + HEADS].rearrange("(h a) -> h a", a=1))\
                            .then_inc(sem("bml_loaded"), 16)
            gates_weights(0)
            v_ones(0)
            mod_rows(1)
            pool.dma_start(wrt[:, :, 0:N_EXP], w_router[0].rearrange("(k p) n -> p k n", p=P)).then_inc(sem("router_loaded"), 16)
            rel_bias(0)
            for o in range(2, 5):
                mod_rows(o)
            for l, L in enumerate(layers):
                pool.wait_ge(sem("x_post1"), before("x_post1", l) + L.nt)
                pool.memset(Ya[:, :, :], 0.0).then_inc(sem("ya_added"), 1)
                if l == 0:
                    mod_rows(5)
                    params(1)
                pool.wait_ge(sem("routed"), before("routed", l) + 2 * L.ns)
                if l == 0:
                    pool.wait_ge(sem("logits"), 1)
                    pool.dma_start(wrt[:, :, 0:N_EXP], w_router[1].rearrange("(k p) n -> p k n", p=P))\
                        .then_inc(sem("router_loaded"), 16)
                for si in range(L.ns):
                    for c2 in range(2):
                        g_ = aff[:, c2 * L.ns + si, :].rearrange("p (e j) -> p e j", j=1).to_broadcast([P, N_EXP, CAP])
                        own(pool.tensor_tensor(Sg[:, si, c2, :].rearrange("p (e j) -> p e j", e=N_EXP),
                                               Ssel[:, si, c2, :].rearrange("p (e j) -> p e j", e=N_EXP), g_, ALU.mult))
                with pool.Fori(0, LOOPS) as i:
                    pool.wait_ge(sem("gathered"), before("gathered", l) + i * (2 * L.ns) + 1)
                    for si in range(L.ns):
                        for c2 in range(2):
                            ins = pool.tensor_copy(stg[:, si, c2, :], Sg[:, si, c2, bass.ds(i * P, P)])
                    ins.then_inc(sem("staged"), 1)
                if l == 0:
                    gates_weights(1)
                    v_ones(1)
                    rel_bias(1)

        @block.tensor
        def _(pe):
            taken = [0]

            def next_slot():
                n = taken[0]
                taken[0] += 1
                pe.wait_ge(landed[n % SLOTS], 16 * uses(n))
                return w_slot(n)

            def transpose(o, i, n):
                return pe.transpose(o, i, ident[0:n, 0:n])

            def mod_product(o, k):
                w = next_slot()
                for j in range(4):
                    mm = pe.matmul(ps[32 * j:32 * j + 32, 6, :], cT[:, k, :], w[:, 512 * j:512 * j + 512],
                                   start=k == 0, stop=k == KD - 1, skip_group_check=True)
                mm.then_inc(used, 1)

            def merge_mods(step):
                for n in mod_steps(step):
                    o, k = 1 + n // KD, n % KD
                    if k == 0:
                        pe.wait_ge(sem("mod_row"), o)
                    mod_product(o, k)
                for o in range(1, 4):
                    if mod_step(o) == step - 1:
                        mod_turn(o)

            def mod_turn(o):
                l, g = MOD_GROUPS[o]
                src = mod_tmp[:, :] if g == 0 else gate_rows[:, 2 * l + g - 1, :]
                pe.wait_ge(sem("mod_row"), o + 1)
                if o:
                    pe.wait_ge(sem("mod_col"), o)
                for b in range(4):
                    mm = transpose(ps[:, 7, 128 * b:128 * b + 128], src[:, 128 * b:128 * b + 128], P)
                mm.then_inc(sem("mod_tr"), 1)

            def norm_turn(l, which, src, chunks):
                n = f"n{which}"
                pe.wait_ge(sem(f"{n}_xn"), before(f"{n}_xn", l) + len(chunks))
                for k in range(KD):
                    if k >= 2:
                        pe.wait_ge(sem(f"{n}_lat"), before(f"{n}_lat", l) + k - 1)
                        if 0 in chunks:
                            pe.wait_ge(sem(f"{n}_ctx"), before(f"{n}_ctx", l) + k - 1)
                    for t in chunks:
                        mm = transpose(ps[:, 2 * (t // 2) + k % 2, (t % 2) * P:(t % 2 + 1) * P], src[:, t, k * P:(k + 1) * P], P)
                    mm.then_inc(sem(f"{n}_tr"), 1)
                pe.wait_ge(sem(f"{n}_lat"), before(f"{n}_lat", l) + KD)
                if 0 in chunks:
                    pe.wait_ge(sem(f"{n}_ctx"), before(f"{n}_ctx", l) + KD)

            pj = [0]

            slot_done = [False]

            def project(l, name, o, pairs, release=False):
                i = pj_index(l, name)
                assert i == pj[0]
                pj[0] += 1
                if BANK_USED_BY[i] is not None:
                    pe.wait_ge(sem("proj_taken"), BANK_USED_BY[i] + 1)
                for k, (a, b) in enumerate(pairs):
                    mm = pe.matmul(o(ps[:, PROJECTION_BANK[i], :]), a, b, start=k == 0, stop=k == len(pairs) - 1)
                    if k == 0 and slot_done[0]:
                        mm.then_inc(used, 1)
                        slot_done[0] = False
                mm.then_inc(sem("proj_ready"), 1)
                slot_done[0] |= release

            def blk(w, n=BLK):
                return w[:, 0:KD * n].rearrange("p (k n) -> p k n", k=KD)

            def feature_major(l, name, w, j, tok, release):
                project(l, name, lambda b: b[:, tok],
                        [(w[:, k, j * P:(j + 1) * P], hT[:, k, tok]) for k in range(KD)], release)

            def token_major(l, name, w, t):
                project(l, name, lambda b: b[:, 0:BLK],
                        [(hT[:, k, t * P:(t + 1) * P], w[:, k, :]) for k in range(KD)], t == 3)

            for l, L in enumerate(layers):
                tq = L.tq
                if l == 0:
                    pe.wait_ge(sem("ident_ready"), 1)
                    pe.wait_ge(sem("vrow_ready"), 1)
                    transpose(ps[:, 7, 0:30], vrow[0:30, :], 30).then_inc(sem("vrow_tr"), 1)
                    pe.wait_ge(sem("vcol_ready"), 1)
                    for k in range(KD):
                        mod_product(0, k)
                    mod_turn(0)
                else:
                    for k in range(KD):
                        mod_product(5, k)
                norm_turn(l, 1, xn1, range(4))
                if l:
                    mod_turn(5)
                pe.wait_ge(sem("wgp_ready"), before("wgp_ready", l) + 1)
                wg_ = wgp.rearrange("p k f d h -> p k (f d h)")
                project(l, "gate_rows", lambda b: b[:, :], [(wg_[:, k, :], hT[:, k, :]) for k in range(KD)])
                for name, tok in (("mq", tq), ("mk", slice(0, T))):
                    w = blk(next_slot())
                    for j in range(2):
                        feature_major(l, f"{name}{j}", w, j, tok, j == 1)
                pe.wait_ge(sem("rows_ready"), before("rows_ready", l) + 1)
                for r in range(2):
                    for t in range(4):
                        mm = transpose(ps[:, 4, 256 * r + 64 * t:256 * r + 64 * t + 64],
                                       R3[0:64, r, t * P:(t + 1) * P], 64)
                mm.then_inc(sem("rows_tr"), 1)
                for half in range(2):
                    w = blk(next_slot())
                    for t in range(4):
                        token_major(l, f"mv{half}{t}", w, t)
                pe.wait_ge(sem("cols_ready"), before("cols_ready", l) + 1)
                pe.wait_ge(sem("v_ones"), before("v_ones", l) + 1)
                pe.wait_ge(sem("proj_taken"), pj[0])

                def scores_ml(h):
                    if h:
                        pe.wait_ge(sem("p_ready"), before("p_ready", l) + 2 * h)
                    p0 = 64 * (h % 2)
                    for s in range(4):
                        o = ps[:, s, tq] if s < 2 else ps[:, 2, 256 * (s - 2):256 * (s - 2) + 256]
                        q0 = tq if s < 2 else slice(CTX, T)
                        mm = pe.matmul(o, mk[p0:p0 + 64, h // 2, s * P:(s + 1) * P], mq[p0:p0 + 64, h // 2, q0],
                                       start=True, stop=True)
                    mm.then_inc(sem("sc_ready"), 1)

                def spread_m(u):
                    h, d = L.pairs[u]
                    if u >= 2:
                        pe.wait_ge(sem("e1_ready"), before("e1_ready", l) + 4 * (u - 1))
                    r = 32 * d + h
                    pe.matmul(ps[:, 3 + d, tq], ident[0:64, r:r + 1].to_broadcast([64, P]), R3[0:64, 2, tq],
                              start=True, stop=True).then_inc(sem("nm_ready"), 1)

                def values_ml(u):
                    h, d = L.pairs[u]
                    for pi in range(L.nt // 2):
                        o = u * (L.nt // 2) + pi
                        if o >= 2:
                            pe.wait_ge(sem("num_used"), before("num_used", l) + o - 1)
                        for ti in range(2):
                            t = L.chunks[2 * pi + ti]
                            keys = keys_of(t, d)
                            for j, s in enumerate(keys):
                                mm = pe.matmul(ps[:, 5 + o % 2, ti * 129:ti * 129 + 129],
                                               E[u % 2][:, s, t * P:(t + 1) * P], mv1[:, s, h, :],
                                               start=j == 0, stop=j == len(keys) - 1)
                        mm.then_inc(sem("num_ready"), 1)

                scores_ml(0)
                spread_m(0)
                spread_m(1)
                for u, (h, d) in enumerate(L.pairs):
                    if u in (0, 2, 4):
                        na_w = blk(next_slot())
                    if u < 4:
                        feature_major(l, ("nq", "nk")[u // 2] + str(u % 2), na_w, u % 2, (tq, slice(0, T))[u // 2], u % 2 == 1)
                    else:
                        token_major(l, f"nv{u - 4}", na_w, u - 4)
                    pe.wait_ge(sem("p_ready"), before("p_ready", l) + u + 1)
                    if d == 1 and h + 1 < HEADS:
                        scores_ml(h + 1)
                    values_ml(u)
                    if u + 2 < len(L.pairs):
                        spread_m(u + 2)
                pe.wait_ge(sem("e1_ready"), before("e1_ready", l) + 4 * len(L.pairs))
                for half in range(2):
                    w = blk(next_slot())
                    for j in range(2):
                        feature_major(l, f"mo{2 * half + j}", w, j, tq, j == 1)
                pe.wait_ge(sem("hn_ready"), before("hn_ready", l) + 1)
                for h in range(HEADS):
                    if h >= 2:
                        pe.wait_ge(sem("mlstm_out"), before("mlstm_out", l) + h - 1)
                    for t in L.chunks:
                        mm = transpose(ps[:, 4 + h % 2, t * P:(t + 1) * P], hml[:, t, h, :], P)
                    mm.then_inc(sem("hm_tr"), 1)
                pe.wait_ge(sem("mlstm_out"), before("mlstm_out", l) + HEADS)
                w = blk(next_slot())
                for j in range(2):
                    feature_major(l, f"cq{j}", w, j, tq, j == 1)
                w = blk(next_slot(), C_NQ - C_CKV)
                feature_major(l, "ckv", w, 0, slice(0, T), False)
                pe.wait_ge(sem("krw_ready"), before("krw_ready", l) + 1)
                i = pj_index(l, "kr")
                assert i == pj[0]
                pj[0] += 1
                pe.wait_ge(sem("proj_taken"), BANK_USED_BY[i] + 1)
                for k in range(KD):
                    pe.matmul(ps[64:96, PROJECTION_BANK[i], :], w[:, k, P:P + ROPE], hT[:, k, :], start=k == 0, stop=k == KD - 1)
                    mm = pe.matmul(ps[96:128, PROJECTION_BANK[i], 0:SEQ], krw[:, k, :], hT[:, k, CTX:T], start=k == 0, stop=k == KD - 1)
                mm.then_inc(sem("proj_ready"), 1)
                slot_done[0] = True
                pe.wait_ge(sem("sq_ready"), before("sq_ready", l) + 1)
                project(l, "cq_sum", lambda b: b[:, tq], [(ones[:, :], sq[:, k, tq]) for k in range(2)])
                project(l, "ckv_sum", lambda b: b[:, :], [(ones[:, :], sq[:, 2, :])])
                pe.wait_ge(sem("rel_loaded"), before("rel_loaded", l) + 2 * HEADS * 16)
                bt = BT.rearrange("p h d c -> p (h d c)")
                for b in range(3):
                    mm = pe.matmul(ps[:, 4 + b, :], flip[:, :], bt[:, 512 * b:512 * b + 512], start=True, stop=True)
                mm.then_inc(sem("rel_mm"), 1)
                pe.wait_ge(sem("lowrank_ready"), before("lowrank_ready", l) + 1)
                pe.wait_ge(sem("wuqr_ready"), before("wuqr_ready", l) + 1)
                for h in range(HEADS):
                    project(l, f"q{h}", lambda b: b[:, tq], [(wuq[:, k, h, :], cq[:, k, tq]) for k in range(2)])
                for hp in range(HEADS // 2):
                    project(l, f"k{hp}", lambda b: b[:, :], [(wukv[:, 0, hp * P:(hp + 1) * P], ckv[:, :])])
                for t in range(4):
                    project(l, f"v{t}", lambda b: b[:, 0:256], [(ckv[:, t * P:(t + 1) * P], wukv[:, 1, :])])
                pe.wait_ge(sem("proj_taken"), pj[0])
                pe.wait_ge(sem("roped"), before("roped", l) + 1)
                pe.wait_ge(sem("rel_turned"), before("rel_turned", l) + 1)

                def score(i):
                    kind, h, t = L.units[i]
                    nkey = T if t >= 2 else CTX
                    if i >= 2:
                        pe.wait_ge(sem("attn_exp"), before("attn_exp", l) + i - 1)
                    p0 = 64 * (h % 2)
                    if kind == "mla":
                        a, b = qT[0:QK, h, t * P:(t + 1) * P], kT[0:QK, h, 0:nkey]
                    else:
                        a, b = nq[p0:p0 + 64, h // 2, t * P:(t + 1) * P], nk[p0:p0 + 64, h // 2, 0:nkey]
                    pe.matmul(ps[:, i % 2, 0:nkey], a, b, start=True, stop=True).then_inc(sem("attn_score"), 1)

                def turn(i):
                    kind, h, t = L.units[i]
                    nk_ = 4 if t >= 2 else 2
                    pe.wait_ge(sem("attn_p"), before("attn_p", l) + i + 1)
                    if i >= 2:
                        pe.wait_ge(sem("attn_pt"), before("attn_pt", l) + i - 1)
                    for j in range(nk_):
                        mm = transpose(ps[:, 2 + i % 2, j * P:(j + 1) * P], Pa[i % 2][:, j * P:(j + 1) * P], P)
                    mm.then_inc(sem("attn_tr"), 1)

                def values(i):
                    kind, h, t = L.units[i]
                    nk_ = 4 if t >= 2 else 2
                    v = vM if kind == "mla" else nv
                    pe.wait_ge(sem("attn_pt"), before("attn_pt", l) + i + 2)
                    if i >= 4:
                        pe.wait_ge(sem("attn_o"), before("attn_o", l) + i // 2 - 1)
                    for j in range(nk_):
                        for b in range(2):
                            mm = pe.matmul(ps[64 * b:64 * b + 64, 4 + i // 2 % 2, 0:P], v[:, j, (h + b) * 64:(h + b + 1) * 64],
                                           PT[b][:, j * P:(j + 1) * P], start=j == 0, stop=j == nk_ - 1)
                    mm.then_inc(sem("attn_v"), 1)

                def gate_products(n0, n1):
                    for n in range(n0, n1):
                        f, k = divmod(n, KD)
                        g = pj_index(l, f"gate{f}")
                        if n % (2 * KD) == 0:
                            gate_w[0] = blk(next_slot())
                        if k == 0:
                            assert g == pj[0]
                            pj[0] += 1
                            if BANK_USED_BY[g] is not None:
                                pe.wait_ge(sem("proj_taken"), BANK_USED_BY[g] + 1)
                        mm = pe.matmul(ps[:, PROJECTION_BANK[g], tq], gate_w[0][:, k, (f % 2) * P:(f % 2 + 1) * P], hT[:, k, tq],
                                       start=k == 0, stop=k == KD - 1, skip_group_check=True)
                        if k == KD - 1:
                            mm.then_inc(sem("proj_ready"), 1)
                        if n and n % (2 * KD) == 0:
                            mm.then_inc(used, 1)

                gate_w = [None]
                nu = len(L.units)
                pe.wait_ge(sem("rel_turned"), before("rel_turned", l) + 1)
                for i in range(nu + 2):
                    if i < nu:
                        score(i)
                    if i < nu:
                        gate_products(6 * KD * i // nu, 6 * KD * (i + 1) // nu)
                    if 1 <= i <= nu:
                        turn(i - 1)
                    if i >= 3 and i % 2:
                        values(i - 3)
                pe.wait_ge(sem("attn_o"), before("attn_o", l) + nu // 2)
                pe.wait_ge(sem("proj_taken"), pj[0])
                pe.nop().then_inc(used, 1)
                u = 0
                for jp in range(KD // 2):
                    wb = branches[jp % 2]
                    pe.wait_ge(sem(f"branch_landed_{jp % 2}"), 48 * (2 * l + jp // 2 + 1))
                    for m in range(3):
                        if jp:
                            wg = blk(next_slot())
                        for half in range(2):
                            if u >= 3:
                                pe.wait_ge(sem("mg_used"), before("mg_used", l) + u - 2)
                            cols = slice(half * P, (half + 1) * P)
                            if jp:
                                for k in range(KD):
                                    mm = pe.matmul(ps[:, u % 3, tq], wg[:, k, cols], hT[:, k, tq],
                                                   start=k == 0, stop=k == KD - 1)
                                mm.then_inc(sem("mg_gate"), 1)
                            k0, src = ((0, aT["mla"]), (2, aT["na"]), (4, mT))[m]
                            nk_ = 4 if m == 2 else 2
                            for k in range(nk_):
                                mm = pe.matmul(ps[:, 3 + u % 3, tq], wb[:, k0 + k, cols], src[:, k, tq],
                                               start=k == 0, stop=k == nk_ - 1)
                                if k == 0 and jp and half:
                                    mm.then_inc(used, 1)
                            mm.then_inc(sem("mg_branch"), 1)
                            u += 1
                        if l == 0:
                            merge_mods(3 * jp + m)

                def spread_gate(which):
                    row = gate_rows[:, 2 * l + which - 1, :]
                    for si, s in enumerate(L.streams):
                        for half in range(2):
                            g = si * 2 + half
                            if which == 1 and g >= 2:
                                pe.wait_ge(sem("g1_taken"), before("g1_taken", l) + g - 1)
                            r = 32 * ((2 if which == 2 else 0) + half) + s
                            pe.matmul(ps[:, gate_bank(which, g), :], ident[:, r:r + 1].to_broadcast([P, P]), row,
                                      start=True, stop=True).then_inc(sem(f"g{which}_ready"), 1)

                pe.wait_ge(sem("merged"), before("merged", l) + KD)
                wo = [blk(next_slot()) for nb in range(D // BLK)]
                o = 0
                for t in L.chunks:
                    for nb in range(D // BLK):
                        if o >= 6:
                            pe.wait_ge(sem("wo_taken"), before("wo_taken", l) + o - 5)
                        for k in range(KD):
                            mm = pe.matmul(ps[:, o % 6, 0:BLK], merged[:, k, t * P:(t + 1) * P], wo[nb][:, k, :],
                                           start=k == 0, stop=k == KD - 1)
                            if k == 0 and t == L.chunks[-1] and nb:
                                mm.then_inc(used, 1)
                        mm.then_inc(sem("wo_ready"), 1)
                        o += 1
                    if t == L.chunks[0]:
                        if l == 0:
                            mod_turn(3)
                        pe.wait_ge(sem("mod_col"), 6 if l else 4)
                        spread_gate(1)
                pe.wait_ge(sem("wo_ready"), before("wo_ready", l) + o)
                pe.nop().then_inc(used, 1)
                if l == 0:
                    pe.wait_ge(sem("g1_taken"), 4)
                    for k in range(KD):
                        mod_product(4, k)
                pe.wait_ge(sem("wo_taken"), before("wo_taken", l) + o)
                norm_turn(l, 2, xn2, L.chunks)
                pe.wait_ge(sem("router_loaded"), 16 * (l + 1))
                for r in range(2):
                    for j in range(4):
                        mm = pe.matmul(ps[32 * j:32 * j + 32, 0, tq], wrt[:, 4 * r + j, :], h2T[:, 4 * r + j, tq],
                                       start=r == 0, stop=r == 1)
                mm.then_inc(sem("logit_parts"), 1)
                pe.wait_ge(sem("lgT_ready"), before("lgT_ready", l) + 1)
                for c2 in range(2):
                    for si, s in enumerate(L.streams):
                        t = 2 * s + c2
                        at = (c2 * L.ns + si) * N_EXP
                        mm = pe.matmul(ps[:, 1, at:at + N_EXP], lgT[:, t * P:(t + 1) * P], sum4[:, :], start=True, stop=True)
                mm.then_inc(sem("logits"), 1)
                if l == 0:
                    mod_turn(4)
                R = N_EXP * L.ns
                pe.wait_ge(sem("aff_ready"), before("aff_ready", l) + 1)
                for c2 in range(2):
                    mm = transpose(ps[0:R, 2, c2 * P:(c2 + 1) * P],
                                   aff[:, c2 * L.ns:(c2 + 1) * L.ns, :].rearrange("p s e -> p (s e)"), P)
                mm.then_inc(sem("affT_tr"), 1)
                if l == 0:
                    pe.wait_ge(sem("mod_col"), 5)
                spread_gate(2)
                pe.wait_ge(sem("rank_ready"), before("rank_ready", l) + 1)
                for c2 in range(2):
                    mm = transpose(ps[:, 3, 32 * c2:32 * c2 + R], csum[0:R, c2 * P:(c2 + 1) * P], R)
                mm.then_inc(sem("rank_tr"), 1)
                pe.wait_ge(sem("g2_taken"), before("g2_taken", l) + 2 * L.ns)
                M, NT, NW = L.M, L.NT, L.NW
                NB_ = 4 * L.ns
                with pe.Fori(0, LOOPS) as i:
                    pe.wait_ge(sem("ya_added"), before("ya_added", l) + i * NB_ + 1)
                    for si, s in enumerate(L.streams):
                        pe.wait_ge(sem("routed"), before("routed", l) + 2 * (si + 1))
                        for k in range(KD):
                            for c2 in range(2):
                                mm = pe.matmul(ps[:, 2 * si + k // 4, (k % 4) * P:(k % 4 + 1) * P],
                                               xn2[:, 2 * s + c2, k * P:(k + 1) * P],
                                               Ssel[:, si, c2, bass.ds(i * P, P)], start=c2 == 0, stop=c2 == 1)
                            if k % 4 == 3:
                                mm.then_inc(sem("gathered"), 1)

                    for e in range(GROUP):
                        def slot(j):
                            n = LOOP_BASE[l] + e * EXP_LOADS + j
                            pe.wait_ge(landed[n % SLOTS], i * (16 * LOOP_LOADS // SLOTS) + 16 * uses(n))
                            return w_slot(n).rearrange("p (k n) -> p k n", k=2)

                        b0 = 2 * (e % 2)
                        for m in range(2):
                            for q in range(4):
                                if e == 0 and m == 0 and q % 2 == 0:
                                    pe.wait_ge(sem("xs_lat"), before("xs_lat", l) + 2 * i + (q // 2 + 1))
                                    if L.ns == 2:
                                        pe.wait_ge(sem("xs_ctx"), before("xs_ctx", l) + 2 * i + (q // 2 + 1))
                                w = slot(4 * m + q)
                                for k in range(2):
                                    kk = 2 * q + k
                                    for j in range(NT):
                                        mm = pe.matmul(ps[M * j:M * j + M, b0 + m, 0:NW], XST[:, kk, e, 0:M],
                                                       w[:, k, j * NW:(j + 1) * NW], start=kk == 0, stop=kk == KD - 1)
                                mm.then_inc(used, 1)
                        pe.wait_ge(sem("hid_ready"), before("hid_ready", l) + i * GROUP + (e + 1))
                        nb = NW // P
                        for b in range(nb):
                            mm = transpose(ps[:, 4 + e % 2, b * P:(b + 1) * P], hid[:, b * P:(b + 1) * P], P)
                        mm.then_inc(sem("hid_tr"), 1)
                        pe.wait_ge(sem("hidT_ready"), before("hidT_ready", l) + i * GROUP + (e + 1))
                        if e >= 2:
                            pe.wait_ge(sem("y_taken"), before("y_taken", l) + i * GROUP + (e - 1))
                        for q in range(4):
                            w = slot(8 + q)
                            for k in range(2):
                                kk = 2 * q + k
                                lhs = hidT[:, (kk % nb) * P + (kk // nb) * M:(kk % nb) * P + (kk // nb) * M + M]
                                for j in range(NT):
                                    mm = pe.matmul(ps[M * j:M * j + M, 6 + e % 2, 0:NW], lhs,
                                                   w[:, k, j * NW:(j + 1) * NW], start=kk == 0, stop=kk == KD - 1)
                            mm.then_inc(used, 1)
                        if e == 0:
                            pe.wait_ge(sem("staged"), before("staged", l) + i + 1)
                            for si in range(L.ns):
                                for c2 in range(2):
                                    mm = transpose(ps[:, 5, (2 * si + c2) * P:(2 * si + c2 + 1) * P], stg[:, si, c2, :], P)
                            mm.then_inc(sem("gt_tr"), 1)
                            pe.wait_ge(sem("gt_ready"), before("gt_ready", l) + i + 1)
                    pe.wait_ge(sem("y_taken"), before("y_taken", l) + i * GROUP + GROUP)
                    for o in range(NB_):
                        si, c2, half = o // 4, (o // 2) % 2, o % 2
                        if o >= 4:
                            pe.wait_ge(sem("ya_added"), before("ya_added", l) + i * NB_ + (o - 4 + 2))
                        pe.matmul(ps[:, o % 4, :], GT[:, si, c2 * P:(c2 + 1) * P], Yg[:, si, half * 512:(half + 1) * 512],
                                  start=True, stop=True).then_inc(sem("scattered"), 1)
                taken[0] += LOOPS * LOOP_LOADS
                if l == 0:
                    pe.wait_ge(sem("ya_added"), 8 * LOOPS + 1)

        @block.scalar
        def _(act):
            done = [0]

            def own(ins):
                done[0] += 1
                ins.then_inc(sem("act_own"), 1)
                act.wait_ge(sem("act_own"), done[0])

            def copy(o, i):
                return act.activation(o, i, ACT.Copy)

            def rstd(o, i, n):
                own(act.activation(o, i, ACT.Ln, bias=eps_t[:, 0:1], scale=1.0 / n))
                return act.activation(o, o, ACT.Exp, scale=-0.5)

            def exp_ln():
                act.preload_act_table_set("natural_log_exp_and_others")

            def mod_cols(o):
                l, g = MOD_GROUPS[o]
                act.wait_ge(sem("mod_tr"), o + 1)
                src = ps[:, 7, :].rearrange("p (b j r) -> p b j r", b=4, r=32)[:, :, :, 0:2]
                copy(modT[:, l, g, :, :, :], src).then_inc(sem("mod_col"), 1)

            def norm_stat(which, t, junk):
                own(act.activation(junk, X[:, t, :], ACT.Square, accum_out=stat[:, t:t + 1]))
                rstd(stat[:, t:t + 1], stat[:, t:t + 1], D).then_inc(sem(f"n{which}_rstd"), 1)

            def norm_ctx(l, which, dst):
                n = f"n{which}"
                sc, sh = ((SC1, SH1), (SC2, SH2))[which - 1]
                for k in range(KD):
                    act.wait_ge(sem(f"{n}_tr"), before(f"{n}_tr", l) + k + 1)
                    act.activation(dst[:, k, 0:CTX], ps[:, k % 2, 0:CTX], ACT.Identity, bias=mod_col(l, sh, k, 0),
                                   scale=mod_col(l, sc, k, 0)).then_inc(sem(f"{n}_ctx"), 1)

            pj = [0]

            def bank(l, name):
                i = pj_index(l, name)
                assert i == pj[0]
                pj[0] += 1
                act.wait_ge(sem("proj_ready"), i + 1)
                return ps[:, PROJECTION_BANK[i], :]

            def took(ins):
                ins.then_inc(sem("proj_taken"), 1)

            def took_plain(o, i, func=ACT.Copy, scale=1.0):
                took(act.activation(o, i, func, scale=scale))

            act.wait_ge(small, 16 * 6)
            act.activation(vrow[0:16, :], vrow[0:16, :], ACT.Silu).then_inc(sem("vrow_ready"), 1)
            act.wait_ge(sem("vrow_tr"), 1)
            act.wait_ge(sem("consts_ready"), 1)
            own(copy(vcol[:, 0:30], ps[:, 7, 0:30]))
            for s, at in ((1, 0), (0, 8)):
                ins = copy(cT[:, :, s:s + 1], vcol[:, at:at + 8].rearrange("p (k a) -> p k a", a=1))
            ins.then_inc(sem("vcol_ready"), 1)
            exp_ln()

            for l, L in enumerate(layers):
                tq, nt = L.tq, L.nt
                if l == 0:
                    act.wait_ge(sem("x_loaded"), 32)
                for t in range(4):
                    if l:
                        act.wait_ge(sem("x_post2"), t + 1)
                    norm_stat(1, t, junk1)
                if l == 0:
                    mod_cols(0)
                    act.wait_ge(sem("mod_col"), 1)
                norm_ctx(l, 1, hT)
                if l:
                    mod_cols(5)
                act.wait_ge(sem("bml_loaded"), 128)
                b = bank(l, "gate_rows")
                for p0, row in ((0, rI), (64, rF)):
                    act.activation(row[p0:p0 + 32, :], b[p0:p0 + 32, :], ACT.Identity, bias=bml[p0:p0 + 32, l:l + 1])
                    ins = act.activation(row[p0 + 32:p0 + 64, :].rearrange("p (s t) -> p s t", s=2)[:, :, ::-1],
                                         b[p0 + 32:p0 + 64, :].rearrange("p (s t) -> p s t", s=2), ACT.Identity,
                                         bias=bml[p0 + 32:p0 + 64, l:l + 1])
                took(ins)
                act.wait_ge(sem("abs_f"), before("abs_f", l) + 1)
                own(act.activation(rA[64:128, :], rA[64:128, :], ACT.Exp, scale=-1.0))
                act.activation(rA[64:128, :], rA[64:128, :], ACT.Ln, bias=1.0).then_inc(sem("log1p"), 1)
                for c2 in range(2):
                    took_plain(mq[:, c2, tq], bank(l, f"mq{c2}")[:, tq])
                for c2 in range(2):
                    took_plain(mk[:, c2, :], bank(l, f"mk{c2}"), scale=0.125)
                act.wait_ge(sem("rows_tr"), before("rows_tr", l) + 1)
                copy(gcol, ps[:, 4, 0:256].rearrange("p (t r) -> p t r", t=4))
                act.activation(enm, ps[:, 4, 256:512].rearrange("p (t r) -> p t r", t=4), ACT.Exp, scale=-1.0)\
                    .then_inc(sem("cols_ready"), 1)
                for half in range(2):
                    for t in range(4):
                        took_plain(mv1[:, t, 2 * half:2 * half + 2, 0:ML_V],
                                   bank(l, f"mv{half}{t}")[:, 0:256].rearrange("p (h v) -> p h v", h=2))
                for u in range(len(L.pairs)):
                    d = L.pairs[u][1]
                    for s in range(4):
                        act.wait_ge(sem("e1_ready"), before("e1_ready", l) + 4 * u + s + 1)
                        t0, t1, _ = span(L, d, s)
                        e = E[u % 2][:, s, t0 * P:t1 * P]
                        act.activation(e, e, ACT.Exp).then_inc(sem("exp_done"), 1)
                    if u < 2:
                        took_plain(nq[:, u, tq], bank(l, f"nq{u}")[:, tq], scale=0.125)
                    elif u < 4:
                        took_plain(nk[:, u - 2, :], bank(l, f"nk{u - 2}"))
                    else:
                        took_plain(nv[:, u - 4, :], bank(l, f"nv{u - 4}")[:, 0:256])
                act.wait_ge(sem("num_used"), before("num_used", l) + len(L.pairs) * nt // 2)
                act.wait_ge(sem("act_own"), done[0])
                for t in L.chunks:
                    for h in range(HEADS):
                        ins = act.activation(E[0][:, t, 0:ML_V], hml[:, t, h, :], ACT.Square,
                                             accum_out=stat[:, 16 + 4 * t + h:17 + 4 * t + h])
                        own(ins)
                a = stat[:, 16 + 4 * L.chunks[0]:32]
                rstd(a, a, ML_V).then_inc(sem("head_rstd"), 1)
                for h in range(HEADS):
                    took_plain(sgo[:, h, tq], bank(l, f"mo{h}")[:, tq], ACT.Sigmoid)
                exp_ln()
                w = w_slot(BASE[l] + krw_load(l))[:, 0:KD * 160].rearrange("p (k n) -> p k n", k=KD)[:, :, P:160]\
                    .rearrange("p k (a b i) -> p k a b i", a=2, b=2)
                n = BASE[l] + krw_load(l)
                act.wait_ge(sem("mlstm_out"), before("mlstm_out", l) + HEADS)
                for c2 in range(2):
                    b = bank(l, f"cq{c2}")
                    copy(cq[:, c2, tq], b[:, tq])
                    took(act.activation(sq[:, c2, tq], b[:, tq], ACT.Square))
                act.wait_ge(landed[n % SLOTS], 16 * uses(n))
                kr = krw[:, :, :].rearrange("p k (a b i) -> p k a b i", a=2, b=2)
                for b2 in range(2):
                    ins = copy(kr[:, :, :, b2, :], w[:, :, :, 1 - b2, :])
                ins.then_inc(sem("krw_ready"), 1)
                b = bank(l, "ckv")
                copy(ckv, b)
                took(act.activation(sq[:, 2, :], b, ACT.Square))
                act.wait_ge(sem("proj_taken"), pj[0])
                act.nop().then_inc(sem("sq_ready"), 1)
                b = bank(l, "kr")
                copy(kT[64:96, :, 0:CTX], b[64:96, 0:CTX].rearrange("p (a t) -> p a t", a=1).to_broadcast([32, HEADS, CTX]))
                copy(kr_a, b[64:96, CTX:T])
                took(copy(kr_b, b[96:128, 0:SEQ]))
                for j, (name, n_) in enumerate((("cq_sum", Q_RANK), ("ckv_sum", P))):
                    b = bank(l, name)
                    cols = tq if j == 0 else slice(0, T)
                    own(act.activation(rs2[:, j, cols], b[:, cols], ACT.Ln, bias=eps_t[:, 0:1], scale=1.0 / n_))
                    took(act.activation(rs2[:, j, cols], rs2[:, j, cols], ACT.Exp, scale=-0.5))
                scale = float(np.float32(QK) ** np.float32(-0.5))
                act.wait_ge(sem("lowrank_ready"), before("lowrank_ready", l) + 1)
                for h in range(HEADS):
                    b = bank(l, f"q{h}")
                    act.activation(qT[0:QK, h, tq], b[0:QK, tq], ACT.Copy, scale=scale)
                    took_plain(qrt[64:96, h, :], b[QK:P, CTX:T], scale=scale)
                for hp in range(HEADS // 2):
                    b = bank(l, f"k{hp}")
                    copy(kT[0:64, 2 * hp, :], b[0:64, :])
                    took_plain(kT[0:64, 2 * hp + 1, :], b[64:128, :])
                for t in range(4):
                    took_plain(vM[:, t, :], bank(l, f"v{t}")[:, 0:256])

                def pt_copy(i):
                    n_ = T if L.units[i][2] >= 2 else CTX
                    act.wait_ge(sem("attn_tr"), before("attn_tr", l) + i + 1)
                    if i >= 2:
                        act.wait_ge(sem("attn_v"), before("attn_v", l) + i // 2)
                    copy(PT[i % 2][:, 0:n_], ps[:, 2 + i % 2, 0:n_]).then_inc(sem("attn_pt"), 1)

                nu = len(L.units)
                for i in range(nu + 1):
                    if i < nu:
                        n_ = T if L.units[i][2] >= 2 else CTX
                        act.wait_ge(sem("attn_max"), before("attn_max", l) + i + 1)
                        if i >= 2:
                            act.wait_ge(sem("attn_tr"), before("attn_tr", l) + i - 1)
                        act.activation(Pa[i % 2][:, 0:n_], ps[:, i % 2, 0:n_], ACT.Exp, bias=stat[:, 32 + i % 2:33 + i % 2],
                                       accum_out=stat[:, 34 + i % 2:35 + i % 2]).then_inc(sem("attn_exp"), 1)
                    if i >= 1:
                        pt_copy(i - 1)
                    for f in range(6):
                        if i < nu and gate_step(f, nu) == i:
                            took_plain(early[f][:, tq], bank(l, f"gate{f}")[:, tq])
                act.wait_ge(sem("attn_o"), before("attn_o", l) + nu // 2)
                act.wait_ge(sem("proj_taken"), pj[0])
                for u in range(24):
                    if u >= 3:
                        act.wait_ge(sem("mg_used"), before("mg_used", l) + u - 2)
                    if u >= 6:
                        act.wait_ge(sem("mg_gate"), before("mg_gate", l) + u - 5)
                    src = early[u] if u < 6 else ps[:, u % 3, :]
                    act.activation(sg_m[u % 3][:, tq], src[:, tq], ACT.Sigmoid).then_inc(sem("mg_sig"), 1)
                    for o in range(1, 4):
                        if l == 0 and u % 2 and mod_step(o) == u // 2 - 1:
                            mod_cols(o)
                exp_ln()

                def gate_rows_taken(which, G):
                    for si, s in enumerate(L.streams):
                        for half in range(2):
                            act.wait_ge(sem(f"g{which}_ready"), before(f"g{which}_ready", l) + 2 * si + half + 1)
                            copy(G[:, s, 512 * half:512 * half + 512], ps[:, gate_bank(which, 2 * si + half), :]).then_inc(sem(f"g{which}_taken"), 1)

                def post_stat(which, t, Y, junk):
                    own(act.activation(junk, Y[:, t, :], ACT.Square, accum_out=stat[:, 40 + t:41 + t]))
                    rstd(stat[:, 40 + t:41 + t], stat[:, 40 + t:41 + t], D).then_inc(sem(f"post{which}_rstd"), 1)

                o = 0
                for j, t in enumerate(L.chunks):
                    for nb in range(4):
                        act.wait_ge(sem("wo_ready"), before("wo_ready", l) + o + 1)
                        copy(Ym[:, t, nb * BLK:(nb + 1) * BLK], ps[:, o % 6, 0:BLK]).then_inc(sem("wo_taken"), 1)
                        o += 1
                    if j == 0:
                        if l == 0:
                            mod_cols(3)
                        gate_rows_taken(1, G1)
                    act.wait_ge(sem("wo_taken"), before("wo_taken", l) + o)
                    post_stat(1, t, Ym, junk_y)
                    if j:
                        act.wait_ge(sem("x_post1"), before("x_post1", l) + j)
                        norm_stat(2, L.chunks[j - 1], junk_y)
                act.wait_ge(sem("x_post1"), before("x_post1", l) + nt)
                norm_stat(2, L.chunks[-1], junk_y)
                if l == 0:
                    norm_ctx(l, 2, h2T)
                act.wait_ge(sem("logit_parts"), before("logit_parts", l) + 1)
                copy(lgT[:, tq], ps[:, 0, tq]).then_inc(sem("lgT_ready"), 1)
                act.wait_ge(sem("lg_shift"), before("lg_shift", l) + 1)
                act.activation(lg[:, 0:2 * L.ns, :], lg[:, 0:2 * L.ns, :], ACT.Exp).then_inc(sem("lg_exp"), 1)
                if l == 0:
                    mod_cols(4)
                gate_rows_taken(2, G2)
                act.preload_act_table(ACT.Silu)
                M, NT, NW = L.M, L.NT, L.NW
                with act.Fori(0, LOOPS) as i:
                    if L.ns == 2:
                        for k in range(KD):
                            if k % 4 == 0:
                                act.wait_ge(sem("gathered"), before("gathered", l) + i * 4 + (k // 4 + 1))
                            ins = act.activation(XST[:, k, :, 0:CAP],
                                                 ps[:, k // 4, (k % 4) * P:(k % 4 + 1) * P].rearrange("p (e j) -> p e j", e=GROUP),
                                                 ACT.Identity, bias=mod_col(l, SH2, k, 0), scale=mod_col(l, SC2, k, 0))
                            if k % 4 == 3:
                                ins.then_inc(sem("xs_ctx"), 1)
                    for e in range(GROUP):
                        act.wait_ge(used, i * LOOP_LOADS + (LOOP_BASE[l] + e * EXP_LOADS + 4))
                        act.activation(sgh[:, 0:NW], ps[:, 2 * (e % 2), 0:NW], ACT.Silu).then_inc(sem("silu"), 1)
                        act.wait_ge(sem("hid_tr"), before("hid_tr", l) + i * GROUP + (e + 1))
                        copy(hidT[:, 0:NW], ps[:, 4 + e % 2, 0:NW]).then_inc(sem("hidT_ready"), 1)
                        if e == 0:
                            act.wait_ge(sem("gt_tr"), before("gt_tr", l) + i + 1)
                            copy(GT[:, 0:L.ns, :], ps[:, 5, 0:256 * L.ns].rearrange("p (s t) -> p s t", s=L.ns))\
                                .then_inc(sem("gt_ready"), 1)
                exp_ln()
                for j, t in enumerate(L.chunks):
                    act.wait_ge(sem("ya_added"), before("ya_added", l) + 4 * L.ns * (LOOPS - 1) + 2 * (j + 1) + 1)
                    post_stat(2, t, Ya, junk2)

        @block.vector
        def _(dve):
            done = [0]

            def own(ins):
                done[0] += 1
                ins.then_inc(sem("dve_own"), 1)
                dve.wait_ge(sem("dve_own"), done[0])

            def mod_row(o):
                l, g = MOD_GROUPS[o]
                dst = mod_tmp[:, :] if g == 0 else gate_rows[:, 2 * l + g - 1, :]
                dve.wait_ge(used, mod_loaded(o))
                dve.wait_ge(sem("mod_rows_ready"), o + 1)
                own(dve.tensor_tensor(dst, ps[:, 6, :], b_row[:, :], ALU.add))
                dve.scalar_tensor_tensor(out=dst, in0=dst, scalar=one_add[:, g:g + 1], in1=g_row[:, :],
                                         op0=ALU.add, op1=ALU.mult).then_inc(sem("mod_row"), 1)

            def norm_rows(l, which, j, t, dst):
                n = f"n{which}"
                dve.wait_ge(sem(f"{n}_rstd"), before(f"{n}_rstd", l) + j + 1)
                dve.tensor_scalar(dst[:, t, :], X[:, t, :], stat[:, t:t + 1], None, ALU.mult).then_inc(sem(f"{n}_xn"), 1)

            def norm_lat(l, which, hdst):
                n = f"n{which}"
                sc, sh = ((SC1, SH1), (SC2, SH2))[which - 1]
                for k in range(KD):
                    dve.wait_ge(sem(f"{n}_tr"), before(f"{n}_tr", l) + k + 1)
                    dve.tensor_scalar(hdst[:, k, CTX:T], ps[:, 2 + k % 2, 0:SEQ], mod_col(l, sc, k, 1), mod_col(l, sh, k, 1),
                                      ALU.mult, ALU.add).then_inc(sem(f"{n}_lat"), 1)

            dve.wait_ge(sem("consts_ready"), 1)
            for l, L in enumerate(layers):
                tq, nt = L.tq, L.nt
                for t in range(4):
                    norm_rows(l, 1, t, t, xn1)
                if l == 0:
                    mod_row(0)
                    dve.wait_ge(sem("mod_col"), 1)
                else:
                    mod_row(5)
                norm_lat(l, 1, hT)
                dve.wait_ge(sem("proj_taken"), pj_index(l, "gate_rows") + 1)
                fg = slice(64, 128)
                dve.scalar_tensor_tensor(out=rA[fg, :], in0=rF[fg, :], scalar=-1.0, in1=rF[fg, :],
                                         op0=ALU.mult, op1=ALU.max).then_inc(sem("abs_f"), 1)
                dve.wait_ge(sem("log1p"), before("log1p", l) + 1)
                own(dve.scalar_tensor_tensor(out=rS[fg, :], in0=rF[fg, :], scalar=0.0, in1=rA[fg, :],
                                             op0=ALU.min, op1=ALU.subtract))
                own(dve.tensor_tensor_scan(out=rF[fg, :], data0=ones[fg, 0:1].to_broadcast([64, T]), data1=rS[fg, :],
                                           initial=0.0, op0=ALU.mult, op1=ALU.add))
                own(dve.tensor_copy(rF[0:64, :], rF[fg, :]))
                own(dve.tensor_tensor(rG[0:64, :], rI[0:64, :], rF[0:64, :], ALU.subtract))
                own(dve.tensor_tensor_scan(out=rM[0:64, :], data0=rG[0:64, :], data1=rG[0:64, :], initial=0.0,
                                           op0=ALU.max, op1=ALU.max))
                for d in range(2):
                    rows = slice(32 * d, 32 * d + 32)

                    def natural(a):
                        v = a[rows, :].rearrange("p (s t) -> p s t", s=2)
                        return v[:, :, ::-1] if d else v

                    def plain(a):
                        return a[rows, :].rearrange("p (s t) -> p s t", s=2)

                    dve.tensor_copy(natural(R3[:, 0, :]), plain(rG))
                    dve.tensor_tensor(natural(R3[:, 1, :]), plain(rF), plain(rM), ALU.add)
                    ins = dve.tensor_scalar(natural(R3[:, 2, :]), plain(rM), -1.0, None, ALU.mult)
                ins.then_inc(sem("rows_ready"), 1)
                dve.wait_ge(sem("cols_ready"), before("cols_ready", l) + 1)

                def exponents(u):
                    h, d = L.pairs[u]
                    dve.wait_ge(sem("nm_ready"), before("nm_ready", l) + u + 1)
                    if u >= 2:
                        dve.wait_ge(sem("num_ready"), before("num_ready", l) + (u - 1) * (nt // 2))
                    for s in range(4):
                        t0, t1, m = span(L, d, s)
                        mask = (mask_f, mask_b)[d]
                        r = 32 * d + h
                        dve.scalar_tensor_tensor(out=E[u % 2][:, s, t0 * P:t1 * P], in0=ps[:, 3 + d, t0 * P:t1 * P],
                                                 scalar=gcol[:, s, r:r + 1], in1=mask[:, m:m + (t1 - t0) * P],
                                                 op0=ALU.add, op1=ALU.min).then_inc(sem("e1_ready"), 1)

                def weigh(u):
                    h, d = L.pairs[u]
                    dve.wait_ge(sem("sc_ready"), before("sc_ready", l) + h + 1)
                    for s in range(4):
                        t0, t1, m = span(L, d, s)
                        sc = ps[:, s, t0 * P:t1 * P] if s < 2 else \
                            ps[:, 2, 256 * (s - 2) + (t0 - 2) * P:256 * (s - 2) + (t1 - 2) * P]
                        e = E[u % 2][:, s, t0 * P:t1 * P]
                        dve.wait_ge(sem("exp_done"), before("exp_done", l) + 4 * u + s + 1)
                        ins = dve.tensor_tensor(e, sc, e, ALU.mult)
                    ins.then_inc(sem("p_ready"), 1)

                def head_out(u):
                    h, d = L.pairs[u]
                    r = 32 * d + h
                    for pi in range(nt // 2):
                        o = u * (nt // 2) + pi
                        ta = L.chunks[2 * pi]
                        b = ps[:, 5 + o % 2, 0:258].rearrange("p (t v) -> p t v", t=2)
                        den = b[:, :, ML_V:ML_V + 1]
                        z = stat[:, 48:50].rearrange("p (t v) -> p t v", v=1)
                        dve.wait_ge(sem("num_ready"), before("num_ready", l) + o + 1)
                        own(dve.scalar_tensor_tensor(out=z, in0=den, scalar=-1.0, in1=enm[:, ta:ta + 2, r:r + 1],
                                                     op0=ALU.mult, op1=ALU.max))
                        own(dve.scalar_tensor_tensor(out=z, in0=den, scalar=1.0, in1=z, op0=ALU.mult, op1=ALU.max))
                        own(dve.reciprocal(z, z))
                        for ti in range(2):
                            hh = hml[:, ta + ti, h, :]
                            if d == 0:
                                ins = dve.tensor_scalar(hh, b[:, ti, 0:ML_V], stat[:, 48 + ti:49 + ti], None, ALU.mult)
                            else:
                                ins = dve.scalar_tensor_tensor(out=hh, in0=b[:, ti, 0:ML_V], scalar=stat[:, 48 + ti:49 + ti],
                                                               in1=hh, op0=ALU.mult, op1=ALU.add)
                        ins.then_inc(sem("num_used"), 1)
                        dve.wait_ge(sem("num_used"), before("num_used", l) + o + 1)

                np_ = len(L.pairs)
                exponents(0)
                for u in range(np_):
                    if u + 1 < np_:
                        exponents(u + 1)
                    weigh(u)
                    if u:
                        head_out(u - 1)
                head_out(np_ - 1)
                c0 = L.chunks[0]
                hv = hml[:, c0:4, :, :].rearrange("p t h v -> p (t h) v")
                rb = stat[:, 16 + 4 * c0:32].rearrange("p (a v) -> p a v", v=1).to_broadcast([P, 4 * nt, ML_V])
                dve.wait_ge(sem("head_rstd"), before("head_rstd", l) + 1)
                dve.tensor_tensor(hv, hv, rb, ALU.mult).then_inc(sem("hn_ready"), 1)
                dve.wait_ge(sem("proj_taken"), pj_index(l, "mo3") + 1)
                for h in range(HEADS):
                    dve.wait_ge(sem("hm_tr"), before("hm_tr", l) + h + 1)
                    at = COL_GML + 4 * l + h
                    dve.scalar_tensor_tensor(out=mT[:, h, tq], in0=ps[:, 4 + h % 2, tq], scalar=vcol[:, at:at + 1],
                                             in1=sgo[:, h, tq], op0=ALU.mult, op1=ALU.mult)\
                        .then_inc(sem("mlstm_out"), 1)
                dve.wait_ge(small, 16 * 6)
                cos, sin = rope_t[64:96, 0, :], rope_t[64:96, 1, :]
                dve.wait_ge(sem("proj_taken"), pj_index(l, "kr") + 1)
                own(dve.tensor_tensor(kr_a, kr_a, cos, ALU.mult))
                own(dve.tensor_tensor(kr_b, kr_b, sin, ALU.mult))

                def heads(a):
                    return a.rearrange("p (a t) -> p a t", a=1).to_broadcast([32, HEADS, SEQ])

                dve.tensor_tensor(kT[64:96, :, CTX:T], heads(kr_a), heads(kr_b), ALU.add)
                dve.wait_ge(sem("proj_taken"), pj_index(l, "ckv_sum") + 1)
                for c2 in range(2):
                    at = COL_GQ + 2 * l + c2
                    dve.scalar_tensor_tensor(out=cq[:, c2, tq], in0=cq[:, c2, tq], scalar=vcol[:, at:at + 1],
                                             in1=rs2[:, 0, tq], op0=ALU.mult, op1=ALU.mult)
                dve.scalar_tensor_tensor(out=ckv, in0=ckv, scalar=vcol[:, COL_GKV + l:COL_GKV + l + 1],
                                         in1=rs2[:, 1, :], op0=ALU.mult, op1=ALU.mult).then_inc(sem("lowrank_ready"), 1)
                dve.wait_ge(sem("rel_mm"), before("rel_mm", l) + 1)
                dve.tensor_copy(BT.rearrange("p h d c -> p (h d c)").rearrange("p (b n) -> p b n", b=3), ps[:, 4:7, :])\
                    .then_inc(sem("rel_turned"), 1)
                dve.wait_ge(sem("proj_taken"), pj_index(l, "q3") + 1)
                ql = qT[64:96, :, CTX:T]
                own(dve.tensor_tensor(ql, ql, heads(cos), ALU.mult))
                own(dve.tensor_tensor(qrt[64:96, :, :], qrt[64:96, :, :], heads(sin), ALU.mult))
                dve.tensor_tensor(ql, ql, qrt[64:96, :, :], ALU.add).then_inc(sem("roped"), 1)
                dve.wait_ge(sem("proj_taken"), pj_index(l, "v3") + 1)

                def row_max(i):
                    kind, h, t = L.units[i]
                    n_ = T if t >= 2 else CTX
                    dve.wait_ge(sem("attn_score"), before("attn_score", l) + i + 1)
                    if kind == "na" and t >= 2:
                        d0 = 2 - 2 * (t - 2)
                        loc = ps[:, i % 2, CTX:T]
                        dve.wait_ge(sem("rel_ready"), before("rel_ready", l) + 1)
                        own(dve.tensor_tensor(loc, loc, BT[:, h, d0:d0 + 4, :].rearrange("p d c -> p (d c)"), ALU.add))
                    dve.tensor_reduce(stat[:, 32 + i % 2:33 + i % 2], ps[:, i % 2, 0:n_], AX.X, ALU.max, negate=True)\
                        .then_inc(sem("attn_max"), 1)

                def normalise(i):
                    n_ = T if L.units[i][2] >= 2 else CTX
                    dve.wait_ge(sem("attn_exp"), before("attn_exp", l) + i + 1)
                    own(dve.reciprocal(stat[:, 36 + i % 2:37 + i % 2], stat[:, 34 + i % 2:35 + i % 2]))
                    dve.tensor_scalar(Pa[i % 2][:, 0:n_], Pa[i % 2][:, 0:n_], stat[:, 36 + i % 2:37 + i % 2], None, ALU.mult)\
                        .then_inc(sem("attn_p"), 1)

                def head(i):
                    kind, h, t = L.units[i]
                    dve.wait_ge(sem("attn_v"), before("attn_v", l) + i // 2 + 1)
                    dve.tensor_copy(aT[kind][:, h // 2, t * P:(t + 1) * P], ps[:, 4 + i // 2 % 2, 0:P])\
                        .then_inc(sem("attn_o"), 1)

                nu = len(L.units)
                for i in range(nu + 3):
                    if 1 <= i <= nu:
                        normalise(i - 1)
                    if i < nu:
                        row_max(i)
                    if i >= 4 and i % 2 == 0:
                        head(i - 4)
                for u in range(24):
                    jp, m, half = u // 6, (u // 2) % 3, u % 2
                    dst = merged[:, 2 * jp + half, tq]
                    dve.wait_ge(sem("mg_sig"), before("mg_sig", l) + u + 1)
                    dve.wait_ge(sem("mg_branch"), before("mg_branch", l) + u + 1)
                    if m == 0:
                        dve.tensor_tensor(dst, sg_m[u % 3][:, tq], ps[:, 3 + u % 3, tq], ALU.mult).then_inc(sem("mg_used"), 1)
                    else:
                        dve.tensor_tensor(tmp_m[:, tq], sg_m[u % 3][:, tq], ps[:, 3 + u % 3, tq], ALU.mult)\
                            .then_inc(sem("mg_used"), 1)
                        dve.wait_ge(sem("mg_used"), before("mg_used", l) + u + 1)
                        ins = dve.tensor_tensor(dst, dst, tmp_m[:, tq], ALU.add)
                        if m == 2:
                            ins.then_inc(sem("merged"), 1)
                            dve.wait_ge(sem("merged"), before("merged", l) + 2 * jp + half + 1)
                        else:
                            own(ins)
                    for o in range(1, 4):
                        if l == 0 and u % 2 and mod_step(o) == u // 2:
                            mod_row(o)

                def post(which, j, t, Y, G, tmp):
                    s = t // 2
                    if t % 2 == 0:
                        dve.wait_ge(sem(f"g{which}_taken"), before(f"g{which}_taken", l) + 2 * L.streams.index(s) + 2)
                    dve.wait_ge(sem(f"post{which}_rstd"), before(f"post{which}_rstd", l) + j + 1)
                    own(dve.scalar_tensor_tensor(out=tmp, in0=Y[:, t, :], scalar=stat[:, 40 + t:41 + t], in1=G[:, s, :],
                                                 op0=ALU.mult, op1=ALU.mult))
                    dve.tensor_tensor(X[:, t, :], X[:, t, :], tmp, ALU.add).then_inc(sem(f"x_post{which}"), 1)
                    dve.wait_ge(sem(f"x_post{which}"), before(f"x_post{which}", l) + j + 1)

                for j, t in enumerate(L.chunks):
                    post(1, j, t, Ym, G1, tmp1)
                    if j:
                        norm_rows(l, 2, j - 1, L.chunks[j - 1], xn2)
                norm_rows(l, 2, nt - 1, L.chunks[-1], xn2)
                norm_lat(l, 2, h2T)
                if l == 0:
                    mod_row(4)
                ns = L.ns
                R = N_EXP * ns
                lgp = ps[:, 1, 0:2 * R].rearrange("p (a e) -> p a e", e=N_EXP)
                lgs, af = lg[:, 0:2 * ns, :], aff[:, 0:2 * ns, :]

                def per_token(at):
                    return stat[:, at:at + 2 * ns].rearrange("p (a e) -> p a e", e=1).to_broadcast([P, 2 * ns, N_EXP])

                dve.wait_ge(sem("logits"), before("logits", l) + 1)
                own(dve.tensor_reduce(stat[:, 52:52 + 2 * ns], lgp, AX.X, ALU.max, negate=True))
                dve.tensor_tensor(lgs, lgp, per_token(52), ALU.add).then_inc(sem("lg_shift"), 1)
                dve.wait_ge(sem("lg_exp"), before("lg_exp", l) + 1)
                own(dve.tensor_reduce(stat[:, 56:56 + 2 * ns], lgs, AX.X, ALU.add))
                own(dve.reciprocal(stat[:, 60:60 + 2 * ns], stat[:, 56:56 + 2 * ns]))
                dve.tensor_tensor(af, lgs, per_token(60), ALU.mult).then_inc(sem("aff_ready"), 1)
                dve.wait_ge(sem("affT_tr"), before("affT_tr", l) + 1)
                own(dve.tensor_copy(wk[0][0:R, :], ps[0:R, 2, 0:SEQ]))
                for r in range(CAP // 8):
                    own(dve.max(top8[0:R, :], wk[r % 2][0:R, :]))
                    own(dve.match_replace(wk[(r + 1) % 2][0:R, :], top8[0:R, :], wk[r % 2][0:R, :], -1.0))
                own(dve.tensor_scalar(msk[0:R, :], wk[0][0:R, :], 0.0, None, ALU.is_lt))
                own(dve.tensor_tensor_scan(out=affT[0:R, :], data0=ones[0:R, 0:1].to_broadcast([R, SEQ]), data1=msk[0:R, :],
                                           initial=0.0, op0=ALU.mult, op1=ALU.add))
                own(dve.tensor_tensor(csum[0:R, :], affT[0:R, :], msk[0:R, :], ALU.mult))
                dve.tensor_scalar(csum[0:R, :], csum[0:R, :], -1.0, None, ALU.add).then_inc(sem("rank_ready"), 1)
                dve.wait_ge(sem("rank_tr"), before("rank_tr", l) + 1)
                own(dve.tensor_copy(pmT[:, :, 0:R], ps[:, 3, 0:64].rearrange("p (c r) -> p c r", c=2)[:, :, 0:R]))
                io = iota[:, :].rearrange("p (a j) -> p a j", a=1).to_broadcast([P, N_EXP, CAP])
                for si in range(ns):
                    for c2 in range(2):
                        s_ = Ssel[:, si, c2, :].rearrange("p (e j) -> p e j", e=N_EXP)
                        pm = pmT[:, c2, si * N_EXP:(si + 1) * N_EXP].rearrange("p (e j) -> p e j", j=1)
                        dve.tensor_tensor(s_, io, pm.to_broadcast([P, N_EXP, CAP]), ALU.is_equal).then_inc(sem("routed"), 1)
                M, NT, NW = L.M, L.NT, L.NW
                NB_ = 4 * ns
                dve.wait_ge(sem("ya_added"), before("ya_added", l) + 1)
                with dve.Fori(0, LOOPS) as i:
                    so = ns - 1
                    for k in range(KD):
                        if k % 4 == 0:
                            dve.wait_ge(sem("gathered"), before("gathered", l) + i * (2 * ns) + (2 * so + k // 4 + 1))
                        ins = dve.tensor_scalar(XST[:, k, :, so * CAP:(so + 1) * CAP],
                                                ps[:, 2 * so + k // 4, (k % 4) * P:(k % 4 + 1) * P].rearrange("p (e j) -> p e j", e=GROUP),
                                                mod_col(l, SC2, k, 1), mod_col(l, SH2, k, 1), ALU.mult, ALU.add)
                        if k % 4 == 3:
                            ins.then_inc(sem("xs_lat"), 1)
                    for e in range(GROUP):
                        dve.wait_ge(sem("silu"), before("silu", l) + i * GROUP + (e + 1))
                        dve.wait_ge(used, i * LOOP_LOADS + (LOOP_BASE[l] + e * EXP_LOADS + 8))
                        dve.tensor_tensor(hid[:, 0:NW], sgh[:, 0:NW], ps[:, 2 * (e % 2) + 1, 0:NW], ALU.mult)\
                            .then_inc(sem("hid_ready"), 1)
                        dve.wait_ge(used, i * LOOP_LOADS + (LOOP_BASE[l] + (e + 1) * EXP_LOADS))
                        for j in range(4):
                            si, at = y_piece(L, j)
                            ins = dve.tensor_copy(Yg[e * CAP:(e + 1) * CAP, si, at:at + NW],
                                                  ps[j * CAP:(j + 1) * CAP, 6 + e % 2, 0:NW])
                        ins.then_inc(sem("y_taken"), 1)
                    for o in range(NB_):
                        si, c2, half = o // 4, (o // 2) % 2, o % 2
                        y = Ya[:, 2 * L.streams[si] + c2, half * 512:(half + 1) * 512]
                        dve.wait_ge(sem("scattered"), before("scattered", l) + i * NB_ + (o + 1))
                        dve.tensor_tensor(y, y, ps[:, o % 4, :], ALU.add).then_inc(sem("ya_added"), 1)
                dve.wait_ge(sem("ya_added"), before("ya_added", l) + NB_ * LOOPS + 1)
                for j, t in enumerate(L.chunks):
                    post(2, j, t, Ya, G2, tmp2)
                if l == 0:
                    dve.wait_ge(sem("x_post2"), 4)


def uses(n):
    return n // SLOTS + 1


def mod_loaded(o):
    l = 1 if o == 5 else 0
    return BASE[l] + ring_loads(l).index(("mod", *MOD_GROUPS[o], KD - 1)) + 1


def gate_step(f, nu):
    return next(i for i in range(nu) if (f + 1) * KD <= 6 * KD * (i + 1) // nu)


def krw_load(l):
    return ring_loads(l).index(("in", l, C_CKV, C_NQ - C_CKV))


def gate_bank(which, g):
    return 6 + g % 2 if which == 1 else 4 + g


def keys_of(t, d):
    if t < 2:
        return [s for s in range(2) if (s <= t if d == 0 else s >= t)]
    return [0, 1] + [s for s in (2, 3) if (s <= t if d == 0 else s >= t)]


def span(L, d, s):
    if L.n and s < 2:
        return 2, 4, 2 * P if d else P
    if d == 0:
        return s, 4, 0
    if s < 2:
        return 0, 4, P - s * P
    return 2, s + 1, P if s == 2 else 0


def y_piece(L, j):
    return (j % 2, (j // 2) * L.NW) if L.ns == 2 else (0, j * L.NW)


_INS = ['x', 'c', 'ctx', 'c_ctx', 'w_mod', 'b_mod', 'g_pre1', 'g_post1', 'g_pre2', 'g_post2', 'w_in', 'g_q', 'g_kv',
        'w_uq', 'w_ukv', 'rpb', 'b_ml_gates', 'g_ml', 'w_br_mla', 'w_br_na', 'w_br_ml', 'w_out',
        'w_router', 'w_e1', 'w_e3', 'w_e2']


def kernel(**inputs):
    import numpy as _np
    import concourse.bacc as _bacc
    from concourse import mybir as _mybir
    from concourse.bass_utils import run_bass_kernel_spmd as _run

    nc = _bacc.Bacc("TRN2", target_bir_lowering=False, num_devices=1)
    arrays, args = {}, []
    for name in _INS:
        a = _np.ascontiguousarray(inputs[name])
        arrays[f"in_{name}_dram"] = a
        args.append(nc.dram_tensor(f"in_{name}_dram", a.shape, _mybir.dt.from_np(a.dtype), kind="ExternalInput").ap())
    a = rope_table()
    arrays["rope_dram"] = a
    args.append(nc.dram_tensor("rope_dram", a.shape, _mybir.dt.from_np(a.dtype), kind="ExternalInput").ap())
    args.append(nc.dram_tensor("out_0_dram", (1, SEQ, D), _mybir.dt.from_np(_np.dtype("float32")), kind="ExternalOutput").ap())
    backbone(nc, *args)
    r = _run(nc, [arrays], core_ids=[0])
    return r.results[0]["out_0_dram"]
```
